# Optimizing a Trainium2 kernel written in Bass

```python
import math
import jax
import jax.numpy as jnp
from jax import lax
import numpy as np
import jax, jax.numpy as jnp

D_MODEL = 1024
BATCH = 1
SEQ = 256
DEPTH = 2

D_MIX = D_MODEL
GROUP_W = D_MIX // 4
HEAD_DIM = 64
GLA_HEADS = GROUP_W // HEAD_DIM
GLA_GATE_RANK = 16
GLA_GATE_NORMALIZER = 16.0
GLA_CHUNK = 64
FOX_HEADS = GROUP_W // HEAD_DIM
FOX_BLOCK = 128
SSM_HEADS = GROUP_W // HEAD_DIM
SSM_HEAD_DIM = HEAD_DIM
SSM_GROUPS = 2
SSM_STATE = 128
SSM_CONV = 4
SSM_CHUNK = 128
SSM_XBC = GROUP_W + 2 * SSM_GROUPS * SSM_STATE
SC_GROUPS = 4
SC_CONV = 3
D_FF = 2816
EPS = 1e-6

GLA_COLS = 4 * GROUP_W + GLA_GATE_RANK
FOX_COLS = 3 * GROUP_W + FOX_HEADS
SSM_COLS = GROUP_W + SSM_XBC + SSM_HEADS
SC_COLS = 3 * GROUP_W
IN_COLS = GLA_COLS + FOX_COLS + SSM_COLS + SC_COLS


def rms_norm(x, g):
    xf = x.astype(jnp.float32)
    y = xf * lax.rsqrt(jnp.mean(xf * xf, axis=-1, keepdims=True) + EPS)
    return (y * g.astype(jnp.float32)).astype(x.dtype)

def headwise_rms(x, g, n):
    shp = x.shape
    y = rms_norm(x.reshape(shp[:-1] + (shp[-1] // n, n)), g.reshape(-1, n))
    return y.reshape(shp)

def swiglu(h, w_gate, w_up, w_down):
    return (jax.nn.silu(h @ w_gate) * (h @ w_up)) @ w_down

def causal_depthwise_conv(u, w):
    K, C = w.shape
    return lax.conv_general_dilated(
        u, w[:, None, :].astype(u.dtype), window_strides=(1,),
        padding=[(K - 1, 0)], dimension_numbers=('NWC', 'WIO', 'NWC'),
        feature_group_count=C)

def gla_mixer(q, k, v, g_out, g_lr, w_gate_up, b_gate, norm_g):
    dtype = q.dtype
    f32 = jnp.float32
    Bsz, L, _ = q.shape
    H, D, C = GLA_HEADS, HEAD_DIM, GLA_CHUNK
    NC = L // C
    log_a = jax.nn.log_sigmoid((g_lr @ w_gate_up + b_gate).astype(f32)) / GLA_GATE_NORMALIZER

    def chunked(t):
        return t.astype(f32).reshape(Bsz, NC, C, H, D)

    qc = chunked(q) * (D ** -0.5)
    kc, vc, gc = chunked(k), chunked(v), chunked(log_a)
    b = jnp.cumsum(gc, axis=2)
    b_last = b[:, :, -1]
    q_dec = qc * jnp.exp(b)
    k_dec = kc * jnp.exp(-b)
    causal = jnp.tril(jnp.ones((C, C), bool))
    att = jnp.einsum('bnihd,bnjhd->bnhij', q_dec, k_dec)
    att = jnp.where(causal, att, 0.0)
    o_intra = jnp.einsum('bnhij,bnjhv->bnihv', att, vc)
    k_to_end = kc * jnp.exp(b_last[:, :, None] - b)
    chunk_kv = jnp.einsum('bnjhd,bnjhv->nbhdv', k_to_end, vc)
    chunk_decay = jnp.exp(b_last).transpose(1, 0, 2, 3)

    def step(S, inp):
        kv, dec = inp
        return S * dec[..., None] + kv, S

    S0 = jnp.zeros((Bsz, H, D, D), f32)
    _, S_prev = lax.scan(step, S0, (chunk_kv, chunk_decay))
    o_inter = jnp.einsum('bnihd,nbhdv->bnihv', q_dec, S_prev)
    o = (o_intra + o_inter).reshape(Bsz, L, H * D)
    o = headwise_rms(o, norm_g, D) * jax.nn.silu(g_out.astype(f32))
    return o.astype(dtype)

def fox_mixer(q, k, v, f_logit, b_forget, q_norm, k_norm, out_norm):
    dtype = q.dtype
    f32 = jnp.float32
    Bsz, L, _ = q.shape
    H, D, T = FOX_HEADS, HEAD_DIM, FOX_BLOCK
    NB = L // T
    qh = rms_norm(q.astype(f32).reshape(Bsz, L, H, D), q_norm) * (D ** -0.5)
    kh = rms_norm(k.astype(f32).reshape(Bsz, L, H, D), k_norm)
    vh = v.astype(f32).reshape(Bsz, L, H, D)
    log_f = jax.nn.log_sigmoid(f_logit.astype(f32) + b_forget.astype(f32))
    F = jnp.cumsum(log_f, axis=1)
    q_blocks = qh.reshape(Bsz, NB, T, H, D).transpose(1, 0, 2, 3, 4)
    F_blocks = F.reshape(Bsz, NB, T, H).transpose(1, 0, 2, 3)
    F_keys = F.transpose(0, 2, 1)[:, :, None, :]
    k_pos = jnp.arange(L)

    def block(args):
        qb, Fb, i = args
        s = jnp.einsum('bqhd,bkhd->bhqk', qb, kh)
        s = s + (Fb.transpose(0, 2, 1)[..., None] - F_keys)
        q_pos = i * T + jnp.arange(T)
        s = jnp.where(k_pos[None, :] <= q_pos[:, None], s, -jnp.inf)
        p = jax.nn.softmax(s, axis=-1)
        return jnp.einsum('bhqk,bkhd->bqhd', p, vh)

    o = lax.map(block, (q_blocks, F_blocks, jnp.arange(NB)))
    o = o.transpose(1, 0, 2, 3, 4).reshape(Bsz, L, H * D)
    return headwise_rms(o, out_norm, D).astype(dtype)

def ssd_mixer(z, xbc, dt_raw, conv_w, conv_b, dt_bias, A_log, D_skip, norm_g):
    dtype = z.dtype
    f32 = jnp.float32
    Bsz, L, _ = z.shape
    H, P, G, N, Q = SSM_HEADS, SSM_HEAD_DIM, SSM_GROUPS, SSM_STATE, SSM_CHUNK
    NC = L // Q
    xbc = jax.nn.silu(causal_depthwise_conv(xbc, conv_w) + conv_b).astype(f32)
    xs = xbc[..., :GROUP_W].reshape(Bsz, L, H, P)
    Bm = jnp.repeat(xbc[..., GROUP_W:GROUP_W + G * N].reshape(Bsz, L, G, N), H // G, axis=2)
    Cm = jnp.repeat(xbc[..., GROUP_W + G * N:].reshape(Bsz, L, G, N), H // G, axis=2)
    dt = jax.nn.softplus(dt_raw.astype(f32) + dt_bias.astype(f32))
    A = -jnp.exp(A_log.astype(f32))
    a = (dt * A).reshape(Bsz, NC, Q, H).transpose(0, 3, 1, 2)
    Xd = (xs * dt[..., None]).reshape(Bsz, NC, Q, H, P)
    Bc = Bm.reshape(Bsz, NC, Q, H, N)
    Cc = Cm.reshape(Bsz, NC, Q, H, N)
    a_cs = jnp.cumsum(a, axis=-1)
    causal = jnp.tril(jnp.ones((Q, Q), bool))
    seg = a_cs[..., :, None] - a_cs[..., None, :]
    Lmat = jnp.exp(jnp.where(causal, seg, -jnp.inf))
    scores = jnp.einsum('bcihn,bcjhn->bhcij', Cc, Bc) * Lmat
    y_diag = jnp.einsum('bhcij,bcjhp->bcihp', scores, Xd)
    decay_to_end = jnp.exp(a_cs[..., -1:] - a_cs)
    chunk_states = jnp.einsum('bcjhn,bhcj,bcjhp->cbhpn', Bc, decay_to_end, Xd)
    chunk_decay = jnp.exp(a_cs[..., -1]).transpose(2, 0, 1)

    def step(S, inp):
        st, dec = inp
        return S * dec[..., None, None] + st, S

    S0 = jnp.zeros((Bsz, H, P, N), f32)
    _, S_prev = lax.scan(step, S0, (chunk_states, chunk_decay))
    y_off = jnp.einsum('bcihn,cbhpn,bhci->bcihp', Cc, S_prev, jnp.exp(a_cs))
    y = (y_diag + y_off).reshape(Bsz, L, H, P) + xs * D_skip.astype(f32)[:, None]
    y = y.reshape(Bsz, L, H * P) * jax.nn.silu(z.astype(f32))
    return headwise_rms(y, norm_g, GROUP_W // G).astype(dtype)

def short_conv_mixer(b_gate, c_gate, val, conv_w, out_norm):
    y = b_gate * causal_depthwise_conv(c_gate * val, conv_w)
    return headwise_rms(y, out_norm, GROUP_W // SC_GROUPS)

def hybrid_mixing(h, w_in, gla_w_gate_up, gla_b_gate, gla_norm,
                  fox_b_forget, fox_q_norm, fox_k_norm, fox_out_norm,
                  ssm_conv_w, ssm_conv_b, ssm_dt_bias, ssm_A_log, ssm_D, ssm_norm,
                  sc_conv_w, sc_out_norm, w_out):
    proj = h @ w_in
    sizes = ([GROUP_W] * 4 + [GLA_GATE_RANK] + [GROUP_W] * 3 + [FOX_HEADS]
             + [GROUP_W, SSM_XBC, SSM_HEADS] + [GROUP_W] * 3)
    cuts = [int(c) for c in np.cumsum(sizes)[:-1]]
    (a_q, a_k, a_v, a_g, a_lr, b_q, b_k, b_v, b_f,
     c_z, c_xbc, c_dt, d_b, d_c, d_v) = jnp.split(proj, cuts, axis=-1)
    y_a = gla_mixer(a_q, a_k, a_v, a_g, a_lr, gla_w_gate_up, gla_b_gate, gla_norm)
    y_b = fox_mixer(b_q, b_k, b_v, b_f, fox_b_forget, fox_q_norm, fox_k_norm, fox_out_norm)
    y_c = ssd_mixer(c_z, c_xbc, c_dt, ssm_conv_w, ssm_conv_b, ssm_dt_bias, ssm_A_log, ssm_D, ssm_norm)
    y_d = short_conv_mixer(d_b, d_c, d_v, sc_conv_w, sc_out_norm)
    y = jnp.concatenate([y_a, y_b, y_c, y_d], axis=-1).astype(h.dtype)
    return y @ w_out

def first_inputs(seed: int = 0) -> dict:
    key = jax.random.key(seed)
    k = jax.random.split(key, 27)
    f32 = jnp.float32
    Ld = DEPTH

    def nrm(kk, shape, scale):
        return jax.random.normal(kk, shape, f32) * scale

    def gain(kk, shape):
        return 1.0 + 0.02 * jax.random.normal(kk, shape, f32)

    dt0 = jnp.exp(jax.random.uniform(k[16], (Ld, SSM_HEADS), f32, math.log(1e-3), math.log(1e-1)))
    return {
        'x': nrm(k[0], (BATCH, SEQ, D_MODEL), 1.0),
        'ffn1_norm': gain(k[1], (Ld, D_MODEL)),
        'ffn1_w_gate': nrm(k[2], (Ld, D_MODEL, D_FF), D_MODEL ** -0.5),
        'ffn1_w_up': nrm(k[3], (Ld, D_MODEL, D_FF), D_MODEL ** -0.5),
        'ffn1_w_down': nrm(k[4], (Ld, D_FF, D_MODEL), D_FF ** -0.5),
        'mix_norm': gain(k[5], (Ld, D_MODEL)),
        'w_in': nrm(k[6], (Ld, D_MODEL, IN_COLS), D_MODEL ** -0.5),
        'gla_w_gate_up': nrm(k[7], (Ld, GLA_GATE_RANK, GROUP_W), GLA_GATE_RANK ** -0.5),
        'gla_b_gate': nrm(k[8], (Ld, GROUP_W), 0.1),
        'gla_norm': gain(k[9], (Ld, GROUP_W)),
        'fox_b_forget': 2.0 + nrm(k[10], (Ld, FOX_HEADS), 0.1),
        'fox_q_norm': gain(k[11], (Ld, HEAD_DIM)),
        'fox_k_norm': gain(k[12], (Ld, HEAD_DIM)),
        'fox_out_norm': gain(k[13], (Ld, GROUP_W)),
        'ssm_conv_w': nrm(k[14], (Ld, SSM_CONV, SSM_XBC), SSM_CONV ** -0.5),
        'ssm_conv_b': nrm(k[15], (Ld, SSM_XBC), 0.02),
        'ssm_dt_bias': dt0 + jnp.log(-jnp.expm1(-dt0)),
        'ssm_A_log': jnp.log(jax.random.uniform(k[17], (Ld, SSM_HEADS), f32, 1.0, 16.0)),
        'ssm_D': 1.0 + nrm(k[18], (Ld, SSM_HEADS), 0.1),
        'ssm_norm': gain(k[19], (Ld, GROUP_W)),
        'sc_conv_w': nrm(k[20], (Ld, SC_CONV, GROUP_W), SC_CONV ** -0.5),
        'sc_out_norm': gain(k[21], (Ld, GROUP_W)),
        'w_out': nrm(k[22], (Ld, D_MIX, D_MODEL), D_MIX ** -0.5),
        'ffn2_norm': gain(k[23], (Ld, D_MODEL)),
        'ffn2_w_gate': nrm(k[24], (Ld, D_MODEL, D_FF), D_MODEL ** -0.5),
        'ffn2_w_up': nrm(k[25], (Ld, D_MODEL, D_FF), D_MODEL ** -0.5),
        'ffn2_w_down': nrm(k[26], (Ld, D_FF, D_MODEL), D_FF ** -0.5),
    }

def first_block(x, ffn1_norm, ffn1_w_gate, ffn1_w_up, ffn1_w_down,
              mix_norm, w_in, gla_w_gate_up, gla_b_gate, gla_norm,
              fox_b_forget, fox_q_norm, fox_k_norm, fox_out_norm,
              ssm_conv_w, ssm_conv_b, ssm_dt_bias, ssm_A_log, ssm_D, ssm_norm,
              sc_conv_w, sc_out_norm, w_out,
              ffn2_norm, ffn2_w_gate, ffn2_w_up, ffn2_w_down):
    for l in range(DEPTH):
        x = x + 0.5 * swiglu(rms_norm(x, ffn1_norm[l]), ffn1_w_gate[l], ffn1_w_up[l], ffn1_w_down[l])
        h = rms_norm(x, mix_norm[l])
        x = x + hybrid_mixing(h, w_in[l], gla_w_gate_up[l], gla_b_gate[l], gla_norm[l],
                              fox_b_forget[l], fox_q_norm[l], fox_k_norm[l], fox_out_norm[l],
                              ssm_conv_w[l], ssm_conv_b[l], ssm_dt_bias[l], ssm_A_log[l],
                              ssm_D[l], ssm_norm[l], sc_conv_w[l], sc_out_norm[l], w_out[l])
        x = x + 0.5 * swiglu(rms_norm(x, ffn2_norm[l]), ffn2_w_gate[l], ffn2_w_up[l], ffn2_w_down[l])
    return x


NSA_HEADS = 8
NSA_KV_HEADS = 2
NSA_GROUP = NSA_HEADS // NSA_KV_HEADS
MOBA_HEADS = 8
MIX_WIDTH = (NSA_HEADS + MOBA_HEADS) * HEAD_DIM
ROT_DIM = HEAD_DIM // 4
ROPE_THETA = 500000.0
CMP_LEN = 32
CMP_STRIDE = 16
CMP_HIDDEN = 256
SLC_BLOCK = 64
SLC_TOPN = 16
WINDOW = 512
MOBA_BLOCK = 256
MOBA_TOPK = 3
Q_BLOCK = 128
SLC_CHUNK = 128
MOBA_CHUNK = 32
NEG = -1e30
FORCE_BONUS = 1e4

NSA_Q_COLS = NSA_HEADS * HEAD_DIM
NSA_KV_COLS = 3 * 2 * NSA_KV_HEADS * HEAD_DIM
NSA_GATE_COLS = NSA_HEADS * 3
MOBA_COLS = 3 * MOBA_HEADS * HEAD_DIM
IN_COLS_2 = NSA_Q_COLS + NSA_KV_COLS + NSA_GATE_COLS + MOBA_COLS


def rms_norm_2(x, g):
    xf = x.astype(jnp.float32)
    y = xf * lax.rsqrt(jnp.mean(xf * xf, axis=-1, keepdims=True) + EPS)
    return (y * g.astype(jnp.float32)).astype(x.dtype)

def swiglu_2(x, w_gate, w_up, w_down):
    return (jax.nn.silu(x @ w_gate) * (x @ w_up)) @ w_down

def rope_tables(S):
    inv_freq = jnp.power(ROPE_THETA, -(jnp.arange(0, ROT_DIM, 2, dtype=jnp.float32) / ROT_DIM))
    ang = jnp.arange(S, dtype=jnp.float32)[:, None] * inv_freq[None, :]
    return jnp.cos(ang), jnp.sin(ang)

def apply_partial_rope(x, cos, sin):
    half = ROT_DIM // 2
    cos = cos.astype(x.dtype)
    sin = sin.astype(x.dtype)
    x1 = x[..., :half]
    x2 = x[..., half:ROT_DIM]
    return jnp.concatenate([x1 * cos - x2 * sin, x2 * cos + x1 * sin, x[..., ROT_DIM:]], axis=-1)

def masked_softmax(s, valid):
    s = jnp.where(valid, s.astype(jnp.float32), NEG)
    m = jnp.max(s, axis=-1, keepdims=True)
    p = jnp.where(valid, jnp.exp(s - m), 0.0)
    return p / jnp.maximum(jnp.sum(p, axis=-1, keepdims=True), 1.0)

def nsa_mixer(q, k_cmp, v_cmp, k_slc, v_slc, k_win, v_win, gates,
              pos_ck, w_ck1, w_ck2, pos_cv, w_cv1, w_cv2, cos, sin):
    B, G, R, S, Dh = q.shape
    scale = Dh ** -0.5
    t = jnp.arange(S)
    q_rot = apply_partial_rope(q, cos, sin)
    k_slc = apply_partial_rope(k_slc, cos, sin)
    k_win = apply_partial_rope(k_win, cos, sin)

    n_cmp = (S - CMP_LEN) // CMP_STRIDE + 1
    starts = jnp.arange(n_cmp) * CMP_STRIDE
    cidx = starts[:, None] + jnp.arange(CMP_LEN)[None, :]

    def compress(k, pos, w1, w2):
        blocks = k[:, :, cidx, :] + pos
        flat = blocks.reshape(B, G, n_cmp, CMP_LEN * Dh)
        return jax.nn.gelu(flat @ w1) @ w2

    kc = compress(k_cmp, pos_ck, w_ck1, w_ck2)
    vc = compress(v_cmp, pos_cv, w_cv1, w_cv2)
    s_c = jnp.einsum('bgrqd,bgnd->bgrqn', q, kc) * scale
    valid_c = (starts + CMP_LEN - 1)[None, :] <= t[:, None]
    p_c = masked_softmax(s_c, valid_c)
    o_cmp = jnp.einsum('bgrqn,bgnd->bgrqd', p_c.astype(vc.dtype), vc)

    n_slc = S // SLC_BLOCK
    top_n = min(SLC_TOPN, n_slc)
    sb = jnp.arange(n_slc) * SLC_BLOCK
    overlap = ((starts[:, None] < (sb + SLC_BLOCK)[None, :]) &
               ((starts + CMP_LEN)[:, None] > sb[None, :])).astype(jnp.float32)
    imp = jnp.einsum('bgrqn,nj->bgqj', p_c, overlap)
    qblk = t // SLC_BLOCK
    j = jnp.arange(n_slc)
    forced = (j[None, :] == 0) | (j[None, :] == qblk[:, None]) | (j[None, :] == qblk[:, None] - 1)
    visible = sb[None, :] <= t[:, None]
    score = jnp.where(visible, jnp.where(forced, FORCE_BONUS, imp), NEG)
    sel_idx = lax.top_k(score, top_n)[1]

    ks_blocks = k_slc.reshape(B, G, n_slc, SLC_BLOCK, Dh)
    vs_blocks = v_slc.reshape(B, G, n_slc, SLC_BLOCK, Dh)
    bi = jnp.arange(B)[:, None, None, None]
    gi = jnp.arange(G)[None, :, None, None]

    def slc_chunk(c):
        q0 = c * SLC_CHUNK
        qc = lax.dynamic_slice_in_dim(q_rot, q0, SLC_CHUNK, axis=3)
        ic = lax.dynamic_slice_in_dim(sel_idx, q0, SLC_CHUNK, axis=2)
        kg = ks_blocks[bi, gi, ic]
        vg = vs_blocks[bi, gi, ic]
        s = jnp.einsum('bgrqd,bgqnld->bgrqnl', qc, kg) * scale
        kpos = ic[..., None] * SLC_BLOCK + jnp.arange(SLC_BLOCK)
        tq = q0 + jnp.arange(SLC_CHUNK)
        valid = (kpos <= tq[None, None, :, None, None]).reshape(B, G, 1, SLC_CHUNK, top_n * SLC_BLOCK)
        p = masked_softmax(s.reshape(B, G, R, SLC_CHUNK, top_n * SLC_BLOCK), valid)
        p = p.reshape(B, G, R, SLC_CHUNK, top_n, SLC_BLOCK).astype(vg.dtype)
        return jnp.einsum('bgrqnl,bgqnld->bgrqd', p, vg)

    o_slc = lax.map(slc_chunk, jnp.arange(S // SLC_CHUNK))
    o_slc = jnp.moveaxis(o_slc, 0, 3).reshape(B, G, R, S, Dh)

    n_qb = S // Q_BLOCK
    kw_pad = jnp.pad(k_win, ((0, 0), (0, 0), (WINDOW, 0), (0, 0)))
    vw_pad = jnp.pad(v_win, ((0, 0), (0, 0), (WINDOW, 0), (0, 0)))
    widx = jnp.arange(n_qb)[:, None] * Q_BLOCK + jnp.arange(WINDOW + Q_BLOCK)[None, :]
    kw = kw_pad[:, :, widx]
    vw = vw_pad[:, :, widx]
    qw = q_rot.reshape(B, G, R, n_qb, Q_BLOCK, Dh)
    s_w = jnp.einsum('bgrcqd,bgckd->bgrcqk', qw, kw) * scale
    kpos = widx - WINDOW
    tq = jnp.arange(n_qb)[:, None] * Q_BLOCK + jnp.arange(Q_BLOCK)[None, :]
    diff = tq[:, :, None] - kpos[:, None, :]
    valid_w = (diff >= 0) & (diff < WINDOW) & (kpos[:, None, :] >= 0)
    p_w = masked_softmax(s_w, valid_w).astype(vw.dtype)
    o_win = jnp.einsum('bgrcqk,bgckd->bgrcqd', p_w, vw).reshape(B, G, R, S, Dh)

    g = jax.nn.sigmoid(gates)
    return g[..., 0:1] * o_cmp + g[..., 1:2] * o_slc + g[..., 2:3] * o_win

def moba_mixer(q, k, v, cos, sin):
    B, H, S, Dh = q.shape
    scale = Dh ** -0.5
    q = apply_partial_rope(q, cos, sin)
    k = apply_partial_rope(k, cos, sin)
    n_blk = -(-S // MOBA_BLOCK)
    pad = n_blk * MOBA_BLOCK - S
    kb = jnp.pad(k, ((0, 0), (0, 0), (0, pad), (0, 0))).reshape(B, H, n_blk, MOBA_BLOCK, Dh)
    vb = jnp.pad(v, ((0, 0), (0, 0), (0, pad), (0, 0))).reshape(B, H, n_blk, MOBA_BLOCK, Dh)
    k_mean = jnp.mean(kb.astype(jnp.float32), axis=3)
    t = jnp.arange(S)
    qblk = t // MOBA_BLOCK
    past = jnp.arange(n_blk)[None, :] < qblk[:, None]
    gate = jnp.einsum('bhqd,bhnd->bhqn', q.astype(jnp.float32), k_mean)
    gate = jnp.where(past, gate, NEG)
    kk = max(min(MOBA_TOPK, n_blk - 1), 1)
    idx = lax.top_k(gate, kk)[1]
    sel_valid = idx < qblk[None, None, :, None]
    bi = jnp.arange(B)[:, None, None, None]
    hi = jnp.arange(H)[None, :, None, None]

    def chunk(c):
        q0 = c * MOBA_CHUNK
        qc = lax.dynamic_slice_in_dim(q, q0, MOBA_CHUNK, axis=2)
        ic = lax.dynamic_slice_in_dim(idx, q0, MOBA_CHUNK, axis=2)
        vc_ = lax.dynamic_slice_in_dim(sel_valid, q0, MOBA_CHUNK, axis=2)
        kg = kb[bi, hi, ic]
        vg = vb[bi, hi, ic]
        s_past = jnp.einsum('bhqd,bhqnld->bhqnl', qc, kg).reshape(B, H, MOBA_CHUNK, kk * MOBA_BLOCK)
        own = q0 // MOBA_BLOCK
        ko = lax.dynamic_index_in_dim(kb, own, axis=2, keepdims=False)
        vo = lax.dynamic_index_in_dim(vb, own, axis=2, keepdims=False)
        s_own = jnp.einsum('bhqd,bhld->bhql', qc, ko)
        tq = q0 + jnp.arange(MOBA_CHUNK)
        own_valid = (own * MOBA_BLOCK + jnp.arange(MOBA_BLOCK))[None, :] <= tq[:, None]
        valid = jnp.concatenate([
            jnp.broadcast_to(vc_[..., None], (B, H, MOBA_CHUNK, kk, MOBA_BLOCK)).reshape(B, H, MOBA_CHUNK, kk * MOBA_BLOCK),
            jnp.broadcast_to(own_valid, (B, H, MOBA_CHUNK, MOBA_BLOCK))], axis=-1)
        s = jnp.concatenate([s_past, s_own], axis=-1) * scale
        p = masked_softmax(s, valid).astype(vg.dtype)
        p_past = p[..., :kk * MOBA_BLOCK].reshape(B, H, MOBA_CHUNK, kk, MOBA_BLOCK)
        p_own = p[..., kk * MOBA_BLOCK:]
        return (jnp.einsum('bhqnl,bhqnld->bhqd', p_past, vg) +
                jnp.einsum('bhql,bhld->bhqd', p_own, vo))

    o = lax.map(chunk, jnp.arange(S // MOBA_CHUNK))
    return jnp.moveaxis(o, 0, 2).reshape(B, H, S, Dh)

def hybrid_mixer(h, w_in, pos_ck, w_ck1, w_ck2, pos_cv, w_cv1, w_cv2, w_out, cos, sin):
    B, S, _ = h.shape
    G, R, Dh = NSA_KV_HEADS, NSA_GROUP, HEAD_DIM
    proj = h @ w_in
    q_n, kv_n, gate_n, moba = jnp.split(
        proj, [NSA_Q_COLS, NSA_Q_COLS + NSA_KV_COLS, NSA_Q_COLS + NSA_KV_COLS + NSA_GATE_COLS], axis=-1)
    q_n = q_n.reshape(B, S, G, R, Dh).transpose(0, 2, 3, 1, 4)
    kv_n = kv_n.reshape(B, S, 6, G, Dh).transpose(2, 0, 3, 1, 4)
    gate_n = gate_n.reshape(B, S, G, R, 3).transpose(0, 2, 3, 1, 4)
    o_nsa = nsa_mixer(q_n, kv_n[0], kv_n[1], kv_n[2], kv_n[3], kv_n[4], kv_n[5], gate_n,
                      pos_ck, w_ck1, w_ck2, pos_cv, w_cv1, w_cv2, cos, sin)
    o_nsa = o_nsa.transpose(0, 3, 1, 2, 4).reshape(B, S, NSA_HEADS * Dh)
    qkv_m = moba.reshape(B, S, 3, MOBA_HEADS, Dh).transpose(2, 0, 3, 1, 4)
    o_moba = moba_mixer(qkv_m[0], qkv_m[1], qkv_m[2], cos, sin)
    o_moba = o_moba.transpose(0, 2, 1, 3).reshape(B, S, MOBA_HEADS * Dh)
    return jnp.concatenate([o_nsa, o_moba], axis=-1) @ w_out

def second_inputs(seed: int = 0) -> dict:
    key = jax.random.key(seed)
    ks = jax.random.split(key, 19)

    def w(k, shape, fan_in):
        return jax.random.normal(k, shape, jnp.float32) * fan_in ** -0.5

    def gain(k, shape):
        return 1.0 + 0.02 * jax.random.normal(k, shape, jnp.float32)

    return {
        "x": jax.random.normal(ks[0], (BATCH, SEQ, D_MODEL), jnp.float32),
        "norm_ffn1": gain(ks[1], (DEPTH, D_MODEL)),
        "w_ffn1_gate": w(ks[2], (DEPTH, D_MODEL, D_FF), D_MODEL),
        "w_ffn1_up": w(ks[3], (DEPTH, D_MODEL, D_FF), D_MODEL),
        "w_ffn1_down": w(ks[4], (DEPTH, D_FF, D_MODEL), D_FF),
        "norm_mix": gain(ks[5], (DEPTH, D_MODEL)),
        "w_in": w(ks[6], (DEPTH, D_MODEL, IN_COLS_2), D_MODEL),
        "pos_ck": 0.1 * jax.random.normal(ks[7], (DEPTH, CMP_LEN, HEAD_DIM), jnp.float32),
        "w_ck1": w(ks[8], (DEPTH, CMP_LEN * HEAD_DIM, CMP_HIDDEN), CMP_LEN * HEAD_DIM),
        "w_ck2": w(ks[9], (DEPTH, CMP_HIDDEN, HEAD_DIM), CMP_HIDDEN),
        "pos_cv": 0.1 * jax.random.normal(ks[10], (DEPTH, CMP_LEN, HEAD_DIM), jnp.float32),
        "w_cv1": w(ks[11], (DEPTH, CMP_LEN * HEAD_DIM, CMP_HIDDEN), CMP_LEN * HEAD_DIM),
        "w_cv2": w(ks[12], (DEPTH, CMP_HIDDEN, HEAD_DIM), CMP_HIDDEN),
        "w_out": w(ks[13], (DEPTH, MIX_WIDTH, D_MODEL), MIX_WIDTH),
        "norm_ffn2": gain(ks[14], (DEPTH, D_MODEL)),
        "w_ffn2_gate": w(ks[15], (DEPTH, D_MODEL, D_FF), D_MODEL),
        "w_ffn2_up": w(ks[16], (DEPTH, D_MODEL, D_FF), D_MODEL),
        "w_ffn2_down": w(ks[17], (DEPTH, D_FF, D_MODEL), D_FF),
        "norm_final": gain(ks[18], (D_MODEL,)),
    }

def second_block(x, norm_ffn1, w_ffn1_gate, w_ffn1_up, w_ffn1_down, norm_mix, w_in,
              pos_ck, w_ck1, w_ck2, pos_cv, w_cv1, w_cv2, w_out,
              norm_ffn2, w_ffn2_gate, w_ffn2_up, w_ffn2_down, norm_final):
    cos, sin = rope_tables(x.shape[1])
    for l in range(DEPTH):
        x = x + 0.5 * swiglu_2(rms_norm_2(x, norm_ffn1[l]), w_ffn1_gate[l], w_ffn1_up[l], w_ffn1_down[l])
        x = x + hybrid_mixer(rms_norm_2(x, norm_mix[l]), w_in[l], pos_ck[l], w_ck1[l], w_ck2[l],
                             pos_cv[l], w_cv1[l], w_cv2[l], w_out[l], cos, sin)
        x = x + 0.5 * swiglu_2(rms_norm_2(x, norm_ffn2[l]), w_ffn2_gate[l], w_ffn2_up[l], w_ffn2_down[l])
    return rms_norm_2(x, norm_final)


def setup_inputs(seed=0):
    out = dict(first_inputs(seed))
    for name, value in second_inputs(seed + 1).items():
        if name != "x":
            out[name + "_2"] = value
    return out


def reference(
    x, ffn1_norm, ffn1_w_gate, ffn1_w_up, ffn1_w_down, mix_norm, w_in, gla_w_gate_up,
    gla_b_gate, gla_norm, fox_b_forget, fox_q_norm, fox_k_norm, fox_out_norm, ssm_conv_w,
    ssm_conv_b, ssm_dt_bias, ssm_A_log, ssm_D, ssm_norm, sc_conv_w, sc_out_norm, w_out,
    ffn2_norm, ffn2_w_gate, ffn2_w_up, ffn2_w_down, norm_ffn1_2, w_ffn1_gate_2, w_ffn1_up_2,
    w_ffn1_down_2, norm_mix_2, w_in_2, pos_ck_2, w_ck1_2, w_ck2_2, pos_cv_2, w_cv1_2, w_cv2_2,
    w_out_2, norm_ffn2_2, w_ffn2_gate_2, w_ffn2_up_2, w_ffn2_down_2, norm_final_2,
):
    x = first_block(
        x, ffn1_norm, ffn1_w_gate, ffn1_w_up, ffn1_w_down, mix_norm, w_in, gla_w_gate_up,
        gla_b_gate, gla_norm, fox_b_forget, fox_q_norm, fox_k_norm, fox_out_norm, ssm_conv_w,
        ssm_conv_b, ssm_dt_bias, ssm_A_log, ssm_D, ssm_norm, sc_conv_w, sc_out_norm, w_out,
        ffn2_norm, ffn2_w_gate, ffn2_w_up, ffn2_w_down,
    )
    return second_block(
        x, norm_ffn1_2, w_ffn1_gate_2, w_ffn1_up_2, w_ffn1_down_2, norm_mix_2, w_in_2, pos_ck_2,
        w_ck1_2, w_ck2_2, pos_cv_2, w_cv1_2, w_cv2_2, w_out_2, norm_ffn2_2, w_ffn2_gate_2,
        w_ffn2_up_2, w_ffn2_down_2, norm_final_2,
    )


_drawn_inputs = setup_inputs


def setup_inputs(seed=0):
    import zlib

    import numpy as np

    out = dict(_drawn_inputs(seed))
    spreads = {}
    factors = {'ffn1_norm': 3.231,
     'gla_b_gate': 3.86,
     'gla_norm': 8.0,
     'fox_b_forget': 2.673,
     'fox_q_norm': 6.02,
     'fox_k_norm': 7.46,
     'fox_out_norm': 4.628,
     'ssm_conv_b': 3.214,
     'ssm_norm': 4.972,
     'sc_out_norm': 5.037,
     'ffn2_norm': 5.89,
     'norm_ffn1_2': 8.0,
     'norm_mix_2': 8.0,
     'pos_ck_2': 8.0,
     'pos_cv_2': 18.985,
     'norm_ffn2_2': 8.0,
     'norm_final_2': 7.847}
    for name, (base, spread) in spreads.items():
        noise = np.random.default_rng([zlib.crc32(name.encode()), seed]).standard_normal(out[name].shape)
        drawn = base * np.exp(spread * noise) if base else spread * noise
        out[name] = jnp.asarray(drawn.astype(out[name].dtype))
    for name, factor in factors.items():
        out[name] = (out[name] * factor).astype(out[name].dtype)
    return out
```

```python
from contextlib import ExitStack

import numpy as np

import concourse.bass as bass
from concourse import mybir

F32 = mybir.dt.float32
F32R = mybir.dt.float32r
I32 = mybir.dt.int32
ALU = mybir.AluOpType
ACT = mybir.ActivationFunctionType
AX = mybir.AxisListType.X

P = 128
SEQ, D, FF, DEPTH = 256, 1024, 2816, 2
NT = SEQ // P
KD = D // P
GW, HD, H = 256, 64, 4
EPS = 1e-6
NEG = -1e30
SCALE = HD ** -0.5
SLOT = 1024
RING = 6
AHEAD = 4
STEPS = FF // P
FFN_SLOTS = 3 * STEPS
IP1 = 15
IP2 = 11
WO_SLOTS = KD
MIX1 = 2 * IP1 + WO_SLOTS
CMP_SLOTS = 4
MIX2 = 2 * IP2 + 1 + 2 * CMP_SLOTS + WO_SLOTS
LAYER1 = 2 * FFN_SLOTS + MIX1
LAYER2 = 2 * FFN_SLOTS + MIX2
TAIL = AHEAD
N_SLOTS = DEPTH * (LAYER1 + LAYER2) + TAIL
NCMP = 15
NCT = 16
MIX_W = 18400
CHAIN = 256

XBC0, XBC1, XBC2, ZG, GG, ROWS, GQ, GK, FQ, FK, GV, FV, DC, DV, DB = range(IP1)
KVC, KSW, Q0, Q1, VSW, MQ0, MQ1, MK0, MK1, MV0, MV1, GATES = range(IP2 + 1)


ROPED = [KSW, Q0, Q1, MQ0, MQ1, MK0, MK1]
UNITS = 24


def positions(mix):
    total = 2 * FFN_SLOTS + mix
    gap = -total % RING
    return [n if n < FFN_SLOTS else n + gap for n in range(total)]


def columns(fields):
    at, out = 0, {}
    for name, width in fields:
        out[name] = (at, at + width)
        at += width
    return out, at


CON, CON_W = columns([("ident", P), ("negq", P), ("negT", P), ("glam", P), ("rreset", SEQ), ("greset", 2 * SEQ),
                      ("sel", 15), ("half", 2), ("own", 8), ("cmpmask", 256), ("ropeC", SEQ), ("ropeS", SEQ), ("ropeR", P)])
PAR1, PAR1_W = columns([("convw", 24), ("convb", 6), ("scw", 6), ("skip", 4), ("rbias", 1), ("ralog", 1), ("gbg", 2),
                        ("fqg", HD), ("fkg", HD), ("gup", GW), ("ygain", D)])
PAR2, PAR2_W = columns([("posk", NCT), ("posv", NCT), ("ck2", 4 * HD), ("cv2", 2 * HD)])


class Turns:

    def __init__(self):
        self.of, self.count, self.fulls = {}, [0] * 8, [0] * 8

    def add(self, name, bank, by_slot=None, times=1):
        self.of[name] = (bank, self.count[bank], self.fulls[bank], by_slot)
        self.count[bank] += times
        self.fulls[bank] += by_slot is None


def norm_turns(t, w):
    for T in range(NT):
        for j in range(2):
            t.add(("norm", w, T, j), 2 * T + j)


def ffn_turns(t, f, mixer):
    for s in range(2):
        t.add(("gu", f, s), s, by_slot=-1, times=STEPS // 2)
    end = FFN_SLOTS - 1 + f * (FFN_SLOTS + mixer)
    for T in range(NT):
        for half in range(2):
            t.add(("acc", f, T, half), 4 + 2 * T + half, by_slot=end if (T, half) == (NT - 1, 1) else None)


def out_turns(t, mixer):
    for T in range(NT):
        for j in range(2):
            t.add(("yT", T, j), 2 * T + j)
    end = FFN_SLOTS + mixer - 1
    for T in range(NT):
        for half in range(2):
            t.add(("wo", T, half), 4 + 2 * T + half, by_slot=end if (T, half) == (NT - 1, 1) else None)


def attention_turns(t, units, s_banks, pt_banks, o_bank):
    for u in range(units + 2):
        if u < units:
            t.add(("s", u), s_banks[u % 2])
        if 1 <= u <= units:
            t.add(("pt", u - 1), pt_banks[(u - 1) % 2])
        if u >= 2 and (u - 2) % 4 == 0:
            t.add(("o", (u - 2) // 4), o_bank((u - 2) // 4))


def first_turns():
    t = Turns()
    norm_turns(t, 0)
    ffn_turns(t, 0, MIX1)
    norm_turns(t, 1)
    for m in range(IP1):
        t.add(("ip", m), m % 4, by_slot=FFN_SLOTS + 2 * m + 1)
        if m == GK:
            t.add("gla_z", 4)
    for name, bank in (("ssd_xs", 5), ("ssd_b", 6), ("rowsT", 7), ("gla_kend", 4), ("ssd_sc", 3), ("ssd_seg0", 0),
                       ("ssd_seg1", 1), ("ssd_seg2", 2), ("ssd_seg3", 7), ("gla_att0", 5), ("gla_att1", 6), ("gla_kv", 2), ("fox_q", 7), ("fox_k", 4),
                       ("ssd_st", 3), ("ssd_y", 0), ("ssd_yoff", 1), ("gla_o", 5), ("sc_t", 6)):
        t.add(name, bank)
    attention_turns(t, H, (2, 3), (4, 7), lambda g: 0)
    out_turns(t, MIX1)
    norm_turns(t, 2)
    ffn_turns(t, 1, MIX1)
    return t


def second_turns():
    t = Turns()
    norm_turns(t, 0)
    ffn_turns(t, 0, MIX2)
    norm_turns(t, 1)
    for m in range(IP2 + 1):
        t.add(("ip", m), m % 4, by_slot=FFN_SLOTS + min(2 * m + 1, 2 * IP2))
        if m in ROPED:
            t.add(("rot", m), 4 + ROPED.index(m) % 2)
    for c in range(2):
        t.add(("hid", c), 6 + c, by_slot=FFN_SLOTS + 2 * IP2 + CMP_SLOTS * (c + 1))
    for name, bank in (("kc", 4), ("vc", 5), ("cmp_s", 6), ("cmp_pt", 7), ("cmp_o0", 4), ("cmp_o1", 5)):
        t.add(name, bank)
    attention_turns(t, UNITS, (0, 1), (2, 3), lambda g: 6 + g % 2)
    out_turns(t, MIX2)
    norm_turns(t, 2)
    ffn_turns(t, 1, MIX2)
    return t


TURNS1, TURNS2 = first_turns(), second_turns()


class Layer:

    def __init__(self, l, blk):
        self.l, self.blk = l, blk
        self.turns = TURNS2 if blk else TURNS1
        pos = positions(MIX2 if blk else MIX1)
        self.pos = pos + [pos[-1] + 1 + n for n in range(AHEAD)]
        self.one = l + 1
        self.deep = l + blk * DEPTH
        self.slot0 = l * (LAYER2 if blk else LAYER1) + blk * DEPTH * LAYER1
        self.chain0 = self.deep * CHAIN

    def bank(self, name):
        b, k, _, _ = self.turns.of[name]
        return b, self.l * self.turns.count[b] + (self.blk * DEPTH * TURNS1.count[b] + k)

    def fulls(self, name):
        b, _, k, _ = self.turns.of[name]
        return self.l * self.turns.fulls[b] + (self.blk * DEPTH * TURNS1.fulls[b] + k)

    def raw_use(self, n):
        place = self.pos[n] % RING
        per = [sum(p % RING == place for p in positions(m)) for m in (MIX1, MIX2)]
        return place, self.l * per[self.blk] + (self.blk * DEPTH * per[0] + sum(p % RING == place for p in self.pos[:n]))

    def before(self, n):
        p = self.pos[n] - RING
        while p >= 0 and p not in self.pos:
            p -= RING
        return self.pos.index(p) if p >= 0 else p


def build(nc, x_d, w_d, gain_d, par1_d, par2_d, con_d, out_d):
    with ExitStack() as ctx:
        def sb(name, shape, dt=F32):
            return ctx.enter_context(nc.sbuf_tensor(name, shape, dt))

        def sem(name):
            return ctx.enter_context(nc.semaphore(name))

        raw = sb("raw", [P, RING, SLOT])
        whi = sb("whi", [P, RING, SLOT], F32R)
        wlo = sb("wlo", [P, RING, SLOT], F32R)
        x = sb("x", [P, NT, D])
        xs = sb("xs", [P, NT, D])
        thi = sb("thi", [P, KD, SEQ], F32R)
        tlo = sb("tlo", [P, KD, SEQ], F32R)
        gain = sb("gain", [P, D])
        par = sb("par", [P, max(PAR1_W, PAR2_W)])
        con = sb("con", [P, CON_W])
        sg = sb("sg", [P, 2, SEQ])
        hf = sb("hf", [P, 2, SEQ])
        hhi = sb("hhi", [P, 2 * NCT * 2 * NCMP], F32R)
        hlo = sb("hlo", [P, 2 * NCT * 2 * NCMP], F32R)
        stat = sb("stat", [P, 256])
        mix = sb("mix", [P, MIX_W])
        bank = [ctx.enter_context(nc.psum_tensor(f"bank{b}", [P, 512], F32)) for b in range(8)]

        def c_(name):
            return con[:, CON[name][0]:CON[name][1]]

        def p1(name):
            return par[:, PAR1[name][0]:PAR1[name][1]]

        def p2(name):
            return par[:, PAR2[name][0]:PAR2[name][1]]

        ident = c_("ident")

        class Parts:
            pass

        def carve(fields):
            part, at = {}, 0
            for name, width in fields:
                if isinstance(width, str):
                    part[name] = part[width]
                else:
                    part[name] = at
                    at += width
            assert at <= MIX_W, at
            return part

        M1 = carve([
            ("xbcu", 4 * 260), ("dcu", 2 * 260), ("xbcs", 6 * SEQ), ("siluz", 512), ("silug", 512),
            ("ru", SEQ), ("re", SEQ), ("rs", SEQ), ("rs2", SEQ), ("rp", SEQ),
            ("rsp", SEQ), ("rcs", SEQ), ("rE", SEQ), ("FR", SEQ), ("DL", SEQ), ("DR", SEQ), ("lrT", SEQ),
            ("gq", 512), ("gk", 512), ("zb", 512), ("ge", 512), ("gb", 512), ("eb", 512), ("enb", 512), ("gd", 512),
            ("kend", 512), ("fqk", "xbcu"), ("fsq", 1024), ("fT", "gd"), ("av", 512), ("bv", 512), ("dc", 512),
            ("avs", 256), ("db", 512), ("Bt", 256), ("Mt", 1024), ("St", "lrT"), ("kendT", 768), ("Sg", 384), ("Sbd", 768), ("FL", "Mt"),
            ("P", "gb"), ("Lm", "zb"), ("xd", "ru"), ("xsD", "rs"), ("xdd", "rp"), ("attT", "fsq"), ("ysq", "gb"),
            ("dy", "dc"), ("pt", "xbcs"), ("tmr", 16), ("ralogx", 1), ("mx", 4), ("nm", 4), ("rowsum", 8), ("frec", 8)])
        M2 = carve([
            ("kx", 1024), ("blk", 960), ("kr", 512), ("qraw", 1024), ("qr", 1024), ("mqr", 1024), ("mkr", 1024),
            ("rtmp", 1024), ("rc", 512), ("vsw", 512), ("mv", 1024), ("gate", 64), ("gex", 64), ("hid", 64), ("hx2", 64),
            ("hu", 64), ("he", 64), ("hk", 64), ("hv", 64), ("hvr", 256), ("kc", 32), ("vcd", 512), ("cs", 256), ("cpT", 256),
            ("P", 768), ("pt", 768), ("mx", 4), ("nm", 4), ("rowsum", 2 * UNITS), ("fac", 8), ("otmp", 512),
            ("cmx", 16), ("csum", 16), ("cfac", 16)])

        def m1(name, width):
            return mix[:, M1[name]:M1[name] + width]

        def m2(name, width):
            return mix[:, M2[name]:M2[name] + width]

        s_x, s_con, s_par, s_gain, s_out = sem("x_loaded"), sem("con_loaded"), sem("par_loaded"), sem("gain_loaded"), sem("out_stored")
        s_raw = [sem(f"raw_loaded{i}") for i in range(RING)]
        hi_done = sem("hi_done")
        split_done = sem("split_done")
        slot_used = sem("slot_used")
        bank_full = [sem(f"bank_full{b}") for b in range(8)]
        bank_read = [sem(f"bank_read{b}") for b in range(8)]
        sq_done = sem("sq_done")
        xs_ready = sem("xs_ready")
        thi_done = sem("thi_done")
        sg_done = sem("sg_done")
        hhi_done = sem("hhi_done")
        h_ready = sem("h_ready")
        act_own, dve_own = sem("act_own"), sem("dve_own")
        sm_max = sem("sm_max")
        events = {}

        def ev(name):
            if name not in events:
                events[name] = sem(name)
            return events[name]

        def wait_full(eng, L, name):
            b, _, _, by_slot = L.turns.of[name]
            if by_slot is None:
                eng.wait_ge(bank_full[b], L.fulls(name) + 1)
            else:
                eng.wait_ge(slot_used, L.slot0 + (by_slot + 1 + RING))

        def wait_drained(eng, L, name):
            b, k = L.bank(name)
            eng.wait_ge(bank_read[b], k + 2)

        def claim(pe, L, name):
            b, k = L.bank(name)
            pe.wait_ge(bank_read[b], k + 1)
            return bank[b]

        def psum(L, name):
            return bank[L.bank(name)[0]]

        def full(L, name, ins):
            ins.then_inc(bank_full[L.bank(name)[0]], 1)

        def drained(L, name, ins):
            ins.then_inc(bank_read[L.bank(name)[0]], 1)

        class Own:

            def __init__(self, eng, done, L):
                self.eng, self.done, self.L, self.n = eng, done, L, 0

            def step(self, ins):
                self.n += 1
                ins.then_inc(self.done, 1)

            def wait(self):
                self.eng.wait_ge(self.done, self.L.chain0 + self.n)

            def link(self, ins):
                self.step(ins)
                self.wait()

            def close(self):
                assert self.n <= CHAIN, self.n
                self.eng.sem_inc(self.done, CHAIN - self.n)

        def raw_of(m):
            if m in (Q0, Q1):
                return m2("qraw", 1024)[:, (m - Q0) * 512:(m - Q0 + 1) * 512]
            s = [KSW, MQ0, MQ1, MK0, MK1].index(m) % 2
            return m2("rtmp", 1024)[:, s * 512:(s + 1) * 512]

        def quarter(j, T):
            return slice(4 * j, 4 * j + 4), slice(T * P, (T + 1) * P)

        block = ctx.enter_context(nc.Block())

        @block.sync
        def _(sp):
            def snap(value):
                return value if isinstance(value, int) else sp.snap(value)

            def load(L, n, i=0):
                place, uses = L.raw_use(n)
                slot = snap(L.slot0 + n + RING * i)
                free = snap(L.slot0 + (L.before(n) + 1 + RING) + RING * i)
                sp.wait_ge(split_done, free)
                sp.dma_start(raw[:, place, :], w_d[bass.ds(slot, 1)].rearrange("a p n -> (a p) n")).then_inc(s_raw[place], 16)

            def load_gain(L, w):
                row = snap(L.deep * 3 + w)
                used = snap((L.deep * 3 + w) * NT + NT)
                sp.wait_ge(xs_ready, used)
                sp.dma_start(gain[:], gain_d[bass.ds(row, 1)].rearrange("a p n -> (a p) n")).then_inc(s_gain, 16)

            def layer(l, blk):
                L = Layer(l, blk)
                mixer = MIX2 if blk else MIX1
                load_gain(L, 0)
                row = snap(l + 0)
                done = snap(L.deep * 3 * NT + NT)
                sp.wait_ge(xs_ready, done)
                src, width = (par2_d, PAR2_W) if blk else (par1_d, PAR1_W)
                sp.dma_start(par[:, 0:width], src[bass.ds(row, 1)].rearrange("a p n -> (a p) n")).then_inc(s_par, 16)
                with sp.Fori(0, FFN_SLOTS // RING) as i:
                    for n in range(RING):
                        load(L, n, i)
                load_gain(L, 1)
                for n in range(FFN_SLOTS, FFN_SLOTS + mixer):
                    load(L, n)
                load_gain(L, 2)
                with sp.Fori(0, FFN_SLOTS // RING) as i:
                    for n in range(RING):
                        load(L, FFN_SLOTS + mixer + n, i)

            def last_uses(last, place):
                return (sum(p % RING == place for p in positions(MIX1)) + sum(p % RING == place for p in positions(MIX2))) * DEPTH \
                    + sum(p % RING == place for p in last.pos[:TAIL])

            sp.dma_start(x[:], x_d).then_inc(s_x, 16)
            sp.dma_start(con[:], con_d).then_inc(s_con, 16)
            with sp.Fori(0, DEPTH) as l:
                layer(l, 0)
            with sp.Fori(0, DEPTH) as l:
                layer(l, 1)
            last = Layer(DEPTH, 1)
            for n in range(TAIL):
                load(last, n)
            load_gain(last, 0)
            sp.wait_ge(xs_ready, 2 * DEPTH * 3 * NT + NT + NT)
            sp.dma_start(out_d, xs[:]).then_inc(s_out, 16)
            sp.wait_ge(s_out, 16)
            for place in range(RING):
                sp.wait_ge(s_raw[place], 16 * last_uses(last, place))


        @block.tensor
        def _(pe):
            def wait_slot(L, n, i=0):
                pe.wait_ge(split_done, L.slot0 + (n + 1 + RING) + RING * i)

            def fm_tile(L, n, out, i=0):
                wait_slot(L, n, i)
                r = L.pos[n] % RING
                for k in range(KD):
                    hi, lo = whi[:, r, k * P:(k + 1) * P], wlo[:, r, k * P:(k + 1) * P]
                    pe.matmul(out, hi, thi[:, k, :], start=(k == 0), stop=False)
                    pe.matmul(out, hi, tlo[:, k, :], start=False, stop=False)
                    mm = pe.matmul(out, lo, thi[:, k, :], start=False, stop=(k == KD - 1))
                mm.then_inc(slot_used, 1)

            def tm_pair(L, n, out):
                wait_slot(L, n + 1)
                for T in range(NT):
                    for k in range(KD):
                        r, c = L.pos[n + k // 4] % RING, (k % 4) * GW
                        hi, lo = whi[:, r, c:c + GW], wlo[:, r, c:c + GW]
                        ahi, alo = thi[:, k, T * P:(T + 1) * P], tlo[:, k, T * P:(T + 1) * P]
                        o = out[:, T * GW:(T + 1) * GW]
                        pe.matmul(o, ahi, hi, start=(k == 0), stop=False)
                        pe.matmul(o, alo, hi, start=False, stop=False)
                        mm = pe.matmul(o, ahi, lo, start=False, stop=(k == KD - 1))
                        if T == NT - 1 and k % 4 == 3:
                            mm.then_inc(slot_used, 1)

            def acc_slot(L, n, ahi, alo, acc, first, last, i=0):
                wait_slot(L, n, i)
                r = L.pos[n] % RING
                if first:
                    for T in range(NT):
                        for half in range(2):
                            claim(pe, L, acc(T, half))
                for T in range(NT):
                    for half in range(2):
                        o = psum(L, acc(T, half))[:]
                        hi, lo = whi[:, r, half * 512:(half + 1) * 512], wlo[:, r, half * 512:(half + 1) * 512]
                        pe.matmul(o, ahi[:, T * P:(T + 1) * P], hi, start=first, stop=False)
                        pe.matmul(o, alo[:, T * P:(T + 1) * P], hi, start=False, stop=False)
                        mm = pe.matmul(o, ahi[:, T * P:(T + 1) * P], lo, start=False, stop=last)
                        if last and (T, half) != (NT - 1, 1):
                            full(L, acc(T, half), mm)
                mm.then_inc(slot_used, 1)

            def turn_tiles(L, names, source):
                for j, name in enumerate(names):
                    out = claim(pe, L, name)
                    for c in range(4):
                        mm = pe.transpose(out[:, c * P:(c + 1) * P], source[:, (4 * j + c) * P:(4 * j + c + 1) * P], ident)
                    full(L, name, mm)

            def norm(L, w):
                for T in range(NT):
                    pe.wait_ge(xs_ready, L.deep * (3 * NT) + (w * NT + T + 1 + NT))
                    turn_tiles(L, [("norm", w, T, j) for j in range(2)], xs[:, T, :])
                for T in range(NT):
                    for j in range(2):
                        wait_drained(pe, L, ("norm", w, T, j))

            def ffn(L, f):
                base = f * (FFN_SLOTS + (MIX2 if L.blk else MIX1))
                steps0 = (2 * L.deep + f) * STEPS
                accs = lambda T, half: ("acc", f, T, half)

                def gate_up(n, s, turn, i=0):
                    b, k = L.bank(("gu", f, s))
                    pe.wait_ge(bank_read[b], k + turn + 1)
                    fm_tile(L, base + n, bank[b][:, 0:SEQ], i)
                    fm_tile(L, base + n + 1, bank[b][:, SEQ:2 * SEQ], i)

                def down(n, step, i=0, first=False, last=False):
                    pe.wait_ge(h_ready, steps0 + step + 1 + 2 * i)
                    c = (step % 2) * SEQ
                    acc_slot(L, base + n, hhi[:, c:c + SEQ], hlo[:, c:c + SEQ], accs, first, last, i)

                gate_up(0, 0, 0)
                gate_up(2, 1, 0)
                down(4, 0, first=True)
                with pe.Fori(0, STEPS // 2 - 1) as i:
                    gate_up(5, 0, i + 1, i)
                    down(7, 1, i)
                    gate_up(8, 1, i + 1, i)
                    down(10, 2, i)
                down(FFN_SLOTS - 1, STEPS - 1, last=True)

            def project_out(L, first_slot):
                if L.blk:
                    wait_drained(pe, L, ("o", UNITS // 4 - 1))
                else:
                    pe.wait_ge(ev("y_ready"), L.one)
                for T in range(NT):
                    turn_tiles(L, [("yT", T, j) for j in range(2)], xs[:, T, :])
                for T in range(NT):
                    for j in range(2):
                        wait_drained(pe, L, ("yT", T, j))
                for k in range(KD):
                    acc_slot(L, first_slot + k, thi[:, k, :], tlo[:, k, :], lambda T, half: ("wo", T, half), k == 0, k == KD - 1)

            def attention(L, units, scores, values, probs, turned):
                for u in range(units + 2):
                    if u < units:
                        out = claim(pe, L, ("s", u))
                        scores(u, out)
                        full(L, ("s", u), pe.matmul(out[:, 2 * P:3 * P], ident, c_("negq"), start=False, stop=True))
                    if 1 <= u <= units:
                        out = claim(pe, L, ("pt", u - 1))
                        wait_drained(pe, L, ("s", u - 1))
                        pr = probs((u - 1) % 2)
                        for c in range(3):
                            mm = pe.transpose(out[:, c * P:(c + 1) * P], pr[:, c * P:(c + 1) * P], ident)
                        full(L, ("pt", u - 1), mm)
                    if u >= 2:
                        v = u - 2
                        out = claim(pe, L, ("o", v // 4)) if v % 4 == 0 else psum(L, ("o", v // 4))
                        wait_drained(pe, L, ("pt", v))
                        pt, c = turned(v % 2), (v % 4) * HD
                        pe.matmul(out[:, c:c + HD], pt[:, 0:P], values(v, 0), start=True, stop=True)
                        pe.matmul(out[:, GW + c:GW + c + HD], pt[:, P:2 * P], values(v, 0), start=True, stop=False)
                        mm = pe.matmul(out[:, GW + c:GW + c + HD], pt[:, 2 * P:3 * P], values(v, 1), start=False, stop=True)
                        if v % 4 == 3:
                            full(L, ("o", v // 4), mm)

            def first_mixer(L):
                lrT = m1("lrT", SEQ)
                for m in range(IP1):
                    out = claim(pe, L, ("ip", m))
                    n = FFN_SLOTS + 2 * m
                    if m in (ZG, GG, FQ, FK, GV, FV):
                        tm_pair(L, n, out)
                    else:
                        fm_tile(L, n, out[:, 0:SEQ])
                        fm_tile(L, n + 1, out[:, SEQ:2 * SEQ])
                    if m == GK:
                        out = claim(pe, L, "gla_z")
                        wait_drained(pe, L, ("ip", ROWS))
                        pe.wait_ge(s_par, 16 * L.deep + 16)
                        for t in range(2):
                            mm = pe.matmul(out[:, t * SEQ:(t + 1) * SEQ], p1("gup")[0:16, t * P:(t + 1) * P], lrT[0:16, :],
                                           start=True, stop=True)
                        full(L, "gla_z", mm)
                xbcs = m1("xbcs", 6 * SEQ).rearrange("p (t n) -> p t n", t=6)
                out = claim(pe, L, "ssd_xs")
                for m in range(3):
                    pe.wait_ge(ev(f"xbc_act{m}"), L.one)
                for T in range(NT):
                    for t in range(2):
                        mm = pe.transpose(out[:, T * GW + t * P:T * GW + (t + 1) * P], xbcs[:, t, T * P:(T + 1) * P], ident)
                full(L, "ssd_xs", mm)
                out = claim(pe, L, "ssd_b")
                for g in range(2):
                    mm = pe.transpose(out[:, g * P:(g + 1) * P], xbcs[:, 2 + g, 0:P], ident)
                full(L, "ssd_b", mm)
                out = claim(pe, L, "rowsT")
                pe.wait_ge(ev("rowsE"), L.one)
                for c, part in enumerate(("rsp", "rE")):
                    for T in range(NT):
                        q = 2 * c + T
                        mm = pe.transpose(out[:, q * P:(q + 1) * P], m1(part, SEQ)[:, T * P:(T + 1) * P], ident)
                full(L, "rowsT", mm)
                out = claim(pe, L, "gla_kend")
                pe.wait_ge(ev("gla_dec"), L.one)
                kend = m1("kend", 512)
                for T in range(NT):
                    for t in range(2):
                        mm = pe.transpose(out[:, T * GW + t * P:T * GW + (t + 1) * P], kend[:, t * SEQ + T * P:t * SEQ + (T + 1) * P], ident)
                full(L, "gla_kend", mm)
                out = claim(pe, L, "ssd_sc")
                for T in range(NT):
                    for g in range(2):
                        c = (2 * T + g) * P
                        mm = pe.matmul(out[:, c:c + P], xbcs[:, 2 + g, T * P:(T + 1) * P], xbcs[:, 4 + g, T * P:(T + 1) * P],
                                       start=True, stop=True)
                full(L, "ssd_sc", mm)
                DL, DR = m1("DL", SEQ), m1("DR", SEQ)
                for h in range(H):
                    out = claim(pe, L, f"ssd_seg{h}")
                    for T in range(NT):
                        o, rows, tok = out[:, T * P:(T + 1) * P], slice(32 * h, 32 * h + 4), slice(T * P, (T + 1) * P)
                        pe.matmul(o, ident, c_("negT"), start=True, stop=False)
                        mm = pe.matmul(o, DL[rows, tok], DR[rows, tok], start=False, stop=True)
                    full(L, f"ssd_seg{h}", mm)
                gq, gk = m1("gq", 512), m1("gk", 512)
                claim(pe, L, "gla_kv")
                wait_drained(pe, L, "gla_kend")
                wait_drained(pe, L, ("ip", GV))
                for hh in range(2):
                    out = claim(pe, L, f"gla_att{hh}")
                    rows = slice(HD * hh, HD * hh + HD)
                    for T in range(NT):
                        for t in range(2):
                            c, tok = (2 * T + t) * P, slice(t * SEQ + T * P, t * SEQ + (T + 1) * P)
                            mm = pe.matmul(out[:, c:c + P], gk[rows, tok], gq[rows, tok], start=True, stop=True)
                    full(L, f"gla_att{hh}", mm)
                out = psum(L, "gla_kv")
                kendT = m1("kendT", 768).rearrange("p (c n) -> p c n", c=3)
                av, avs = m1("av", 512), m1("avs", 256)
                chunk_v = [av[0:HD, 0:GW], avs[0:HD, :], av[0:HD, GW:2 * GW]]
                for c in range(3):
                    for h in range(H):
                        o = out[HD * (h % 2):HD * (h % 2) + HD, c * P + (h // 2) * HD:c * P + (h // 2) * HD + HD]
                        mm = pe.matmul(o, kendT[0:HD, c, h * HD:(h + 1) * HD], chunk_v[c][:, h * HD:(h + 1) * HD], start=True, stop=True)
                full(L, "gla_kv", mm)
                fqk = m1("fqk", 1024).rearrange("p (c t n) -> p c t n", c=2, t=NT)
                pe.wait_ge(ev("fqk_ready"), L.one)
                for c, name in enumerate(("fox_q", "fox_k")):
                    out = claim(pe, L, name)
                    for T in range(NT):
                        for t in range(2):
                            mm = pe.transpose(out[:, t * SEQ + T * P:t * SEQ + (T + 1) * P], fqk[:, c, T, t * P:(t + 1) * P], ident)
                    full(L, name, mm)
                out = claim(pe, L, "ssd_st")
                wait_drained(pe, L, "ssd_b")
                pe.wait_ge(ev("xd_ready"), L.one)
                for g in range(2):
                    mm = pe.matmul(out[:, g * P:(g + 1) * P], m1("Bt", 256)[:, g * P:(g + 1) * P], m1("xdd", 256)[:, g * P:(g + 1) * P],
                                   start=True, stop=True)
                full(L, "ssd_st", mm)
                out = claim(pe, L, "ssd_y")
                wait_drained(pe, L, "ssd_sc")
                Mt, xd = m1("Mt", 1024), m1("xd", 512)
                for T in range(NT):
                    for h in range(H):
                        c = T * GW + h * HD
                        mm = pe.matmul(out[:, c:c + HD], Mt[:, T * 512 + h * P:T * 512 + (h + 1) * P], xd[:, c:c + HD], start=True, stop=True)
                full(L, "ssd_y", mm)
                out = claim(pe, L, "ssd_yoff")
                wait_drained(pe, L, "ssd_st")
                for g in range(2):
                    mm = pe.matmul(out[:, g * P:(g + 1) * P], xbcs[:, 4 + g, P:2 * P], m1("St", 256)[:, g * P:(g + 1) * P], start=True, stop=True)
                full(L, "ssd_yoff", mm)
                out = claim(pe, L, "gla_o")
                for hh in range(2):
                    wait_drained(pe, L, f"gla_att{hh}")
                pe.wait_ge(ev("gla_states"), L.one)
                attT, Sbd = m1("attT", 1024), m1("Sbd", 768)
                for T in range(NT):
                    for h in range(H):
                        hh, t = h % 2, h // 2
                        c, a = T * GW + h * HD, hh * 512 + (2 * T + t) * P
                        pe.matmul(out[:, c:c + HD], attT[:, a:a + P], av[:, c:c + HD], start=(T == 0 and h == 0), stop=False,
                                  skip_group_check=True)
                    for t in range(2):
                        for half in range(2):
                            chunk = 2 * T + half
                            if chunk:
                                c, tok, s = T * GW + t * P, t * SEQ + chunk * HD, ((chunk - 1) * 2 + t) * P
                                mm = pe.matmul(out[HD * half:HD * half + HD, c:c + P], gq[:, tok:tok + HD], Sbd[:, s:s + P],
                                               start=False, stop=(half == 1), skip_group_check=True)
                full(L, "gla_o", mm)
                out = claim(pe, L, "sc_t")
                pe.wait_ge(ev("dy_ready"), L.one)
                dy = m1("dy", 512)
                for T in range(NT):
                    for t in range(2):
                        mm = pe.transpose(out[:, T * GW + t * P:T * GW + (t + 1) * P], dy[:, t * SEQ + T * P:t * SEQ + (T + 1) * P], ident)
                full(L, "sc_t", mm)

                fT = m1("fT", 1024).rearrange("p (c t n) -> p c t n", c=2, t=2)
                FL, FR, bv = m1("FL", 4 * SEQ), m1("FR", SEQ), m1("bv", 512)

                def scores(u, out):
                    rows, t, f = slice(HD * (u % 2), HD * (u % 2) + HD), u // 2, u * SEQ
                    pe.matmul(out[:, 0:P], fT[rows, 0, t, 0:P], fT[rows, 1, t, 0:P], start=True, stop=False)
                    pe.matmul(out[:, 0:P], ident, c_("negq"), start=False, stop=False)
                    pe.matmul(out[:, 0:P], FL[:, f:f + P], FR[:, 0:P], start=False, stop=True)
                    pe.matmul(out[:, P:3 * P], fT[rows, 0, t, P:2 * P], fT[rows, 1, t, :], start=True, stop=False)
                    pe.matmul(out[:, P:3 * P], FL[:, f + P:f + 2 * P], FR[:], start=False, stop=False)

                wait_drained(pe, L, "fox_q")
                wait_drained(pe, L, "fox_k")
                pe.wait_ge(ev("FL_ready"), L.one)
                wait_drained(pe, L, ("ip", FV))
                attention(L, H, scores, lambda u, T: bv[:, T * GW + u * HD:T * GW + (u + 1) * HD],
                          lambda s: m1("P", 768)[:, s * 384:(s + 1) * 384], lambda s: m1("pt", 768)[:, s * 384:(s + 1) * 384])
                project_out(L, FFN_SLOTS + 2 * IP1)

            def second_mixer(L):
                def rotate(m):
                    out = claim(pe, L, ("rot", m))
                    wait_drained(pe, L, ("ip", m))
                    full(L, ("rot", m), pe.matmul(out[:], c_("ropeR"), raw_of(m), start=True, stop=True))

                for m in range(IP2 + 1):
                    out = claim(pe, L, ("ip", m))
                    n = FFN_SLOTS + 2 * m
                    if m in (VSW, MV0, MV1):
                        tm_pair(L, n, out)
                    elif m == GATES:
                        wait_slot(L, n)
                        r = L.pos[n] % RING
                        for T in range(NT):
                            for k in range(KD):
                                hi, lo = whi[:, r, k * P:k * P + 32], wlo[:, r, k * P:k * P + 32]
                                ahi, alo = thi[:, k, T * P:(T + 1) * P], tlo[:, k, T * P:(T + 1) * P]
                                o = out[:, T * 32:(T + 1) * 32]
                                pe.matmul(o, ahi, hi, start=(k == 0), stop=False)
                                pe.matmul(o, alo, hi, start=False, stop=False)
                                mm = pe.matmul(o, ahi, lo, start=False, stop=(k == KD - 1))
                        mm.then_inc(slot_used, 1)
                    else:
                        fm_tile(L, n, out[:, 0:SEQ])
                        fm_tile(L, n + 1, out[:, SEQ:2 * SEQ])
                    if m - 1 in ROPED:
                        rotate(m - 1)
                for c in range(2):
                    out = claim(pe, L, ("hid", c))
                    pe.wait_ge(ev(f"blk_ready{c}"), L.one)
                    for s in range(CMP_SLOTS):
                        n = FFN_SLOTS + 2 * IP2 + 1 + c * CMP_SLOTS + s
                        wait_slot(L, n)
                        r, o = L.pos[n] % RING, out[:, (s // 2) * 32:(s // 2) * 32 + 2 * NCMP]
                        for k in range(8):
                            step = (s % 2) * 8 + k
                            hi, lo = whi[:, r, k * P:(k + 1) * P], wlo[:, r, k * P:(k + 1) * P]
                            b0 = (c * NCT + step) * 2 * NCMP
                            pe.matmul(o, hi, hhi[:, b0:b0 + 2 * NCMP], start=(step == 0), stop=False)
                            pe.matmul(o, hi, hlo[:, b0:b0 + 2 * NCMP], start=False, stop=False)
                            mm = pe.matmul(o, lo, hhi[:, b0:b0 + 2 * NCMP], start=False, stop=(step == NCT - 1))
                        mm.then_inc(slot_used, 1)
                pe.wait_ge(s_par, 16 * L.deep + 16)
                out = claim(pe, L, "kc")
                pe.wait_ge(ev("gelu0"), L.one)
                for t in range(2):
                    mm = pe.matmul(out[:, 0:2 * NCMP], p2("ck2")[:, t * P:(t + 1) * P], m2("hk", 64)[:, t * 32:t * 32 + 2 * NCMP],
                                   start=(t == 0), stop=(t == 1))
                full(L, "kc", mm)
                out = claim(pe, L, "vc")
                pe.wait_ge(ev("gelu1"), L.one)
                for t in range(2):
                    mm = pe.matmul(out[:, 0:HD], m2("hvr", 256)[:, t * P:(t + 1) * P], p2("cv2")[:, t * HD:(t + 1) * HD],
                                   start=(t == 0), stop=(t == 1))
                full(L, "vc", mm)
                out = claim(pe, L, "cmp_s")
                wait_drained(pe, L, "kc")
                qraw = m2("qraw", 1024)
                pe.matmul(out[:, 0:256], ident, c_("cmpmask"), start=True, stop=False, skip_group_check=True)
                for T in range(NT):
                    for r in range(4):
                        c = (T * 4 + r) * 32
                        mm = pe.matmul(out[:, c:c + 32], qraw[:, r * SEQ + T * P:r * SEQ + (T + 1) * P], m2("kc", 32),
                                       start=False, stop=(T == 1 and r == 3), skip_group_check=True)
                full(L, "cmp_s", mm)
                out = claim(pe, L, "cmp_pt")
                pe.wait_ge(ev("cmp_exp"), L.one)
                for T in range(NT):
                    mm = pe.transpose(out[:, T * P:(T + 1) * P], m2("cs", 256)[:, T * P:(T + 1) * P], ident)
                full(L, "cmp_pt", mm)
                wait_drained(pe, L, "vc")
                wait_drained(pe, L, "cmp_pt")
                for T in range(NT):
                    out = claim(pe, L, f"cmp_o{T}")
                    full(L, f"cmp_o{T}", pe.matmul(out[:], m2("cpT", 256)[:, T * P:(T + 1) * P], m2("vcd", 512), start=True, stop=True))

                kr, qr, mqr, mkr = m2("kr", 512), m2("qr", 1024), m2("mqr", 1024), m2("mkr", 1024)
                vsw, mv = m2("vsw", 512), m2("mv", 1024)

                def scores(u, out):
                    kind, h = u // 8, u % 8
                    if kind < 2:
                        rows, q, k = slice(HD * (h // 4), HD * (h // 4) + HD), qr[:, (h % 4) * SEQ:(h % 4 + 1) * SEQ], kr[:, kind * SEQ:(kind + 1) * SEQ]
                    else:
                        rows, t = slice(HD * (h % 2), HD * (h % 2) + HD), h // 2
                        q, k = mqr[:, t * SEQ:(t + 1) * SEQ], mkr[:, t * SEQ:(t + 1) * SEQ]
                    pe.matmul(out[:, 0:P], q[rows, 0:P], k[rows, 0:P], start=True, stop=False)
                    pe.matmul(out[:, 0:P], ident, c_("negq"), start=False, stop=True)
                    pe.matmul(out[:, P:3 * P], q[rows, P:2 * P], k[rows, :], start=True, stop=False)

                def values(u, T):
                    kind, h = u // 8, u % 8
                    if kind < 2:
                        c = T * GW + kind * P + (h // 4) * HD
                        return vsw[:, c:c + HD]
                    return mv[:, (h // 4) * 512 + T * GW + (h % 4) * HD:(h // 4) * 512 + T * GW + (h % 4 + 1) * HD]

                pe.wait_ge(ev("roped"), L.one)
                wait_drained(pe, L, ("ip", MV1))
                attention(L, UNITS, scores, values, lambda s: m2("P", 768)[:, s * 384:(s + 1) * 384],
                          lambda s: m2("pt", 768)[:, s * 384:(s + 1) * 384])
                project_out(L, FFN_SLOTS + 2 * IP2 + 1 + 2 * CMP_SLOTS)

            pe.sem_inc(slot_used, RING)
            pe.wait_ge(s_con, 16)
            for blk, mixer in enumerate((first_mixer, second_mixer)):
                with pe.Fori(0, DEPTH) as l:
                    L = Layer(l, blk)
                    norm(L, 0)
                    ffn(L, 0)
                    norm(L, 1)
                    mixer(L)
                    norm(L, 2)
                    ffn(L, 1)

        @block.scalar
        def _(act):
            def split_hi(L, n, i=0):
                place, uses = L.raw_use(n)
                act.wait_ge(s_raw[place], 16 * uses + 16 * i + 16)
                act.wait_ge(slot_used, L.slot0 + (L.before(n) + 1 + RING) + RING * i)
                nc.scalar.copy(whi[:, place, :], raw[:, place, :]).then_inc(hi_done, 1)

            def quarters(L, q, name):
                for T in range(NT):
                    for j in range(2):
                        wait_full(act, L, name(T, j))
                        k, t = quarter(j, T)
                        nc.scalar.copy(thi[:, k, t], psum(L, name(T, j))[:].rearrange("p (k n) -> p k n", k=4)).then_inc(thi_done, 1)

            def squares(L, w):
                for T in range(NT):
                    for half in range(2):
                        if w == 0:
                            b, k = L.bank(("acc", 0, T, half))
                            act.wait_ge(bank_read[b], k + 1)
                        else:
                            wait_drained(act, L, ("acc", 0, T, half) if w == 1 else ("wo", T, half))
                    nc.scalar.activation(xs[:, T, :], x[:, T, :], ACT.Square, accum_out=stat[:, P + T:P + T + 1]).then_inc(sq_done, 1)

            def norm(L, w):
                squares(L, w)
                quarters(L, (0, 1, 3)[w], lambda T, j: ("norm", w, T, j))

            def ffn(L, f):
                base = f * (FFN_SLOTS + (MIX2 if L.blk else MIX1))
                nc.scalar.preload_act_table_set("silu_and_others")

                def step(s, turn, n, up, i=0, last=False):
                    c = s * SEQ
                    b, k = L.bank(("gu", f, s))
                    act.wait_ge(slot_used, L.slot0 + (base + up + 1 + RING) + RING * i)
                    nc.scalar.activation(sg[:, s, :], bank[b][:, 0:SEQ], ACT.Silu).then_inc(sg_done, 1)
                    if not last:
                        split_hi(L, base + n, i)
                    act.wait_ge(bank_read[b], k + turn + 2)
                    nc.scalar.copy(hhi[:, c:c + SEQ], hf[:, s, :]).then_inc(hhi_done, 1)
                    for m in range(0 if last else 1, 3):
                        split_hi(L, base + n + m, i)

                step(0, 0, 4, 1)
                step(1, 0, 7, 3)
                with act.Fori(0, STEPS // 2 - 2) as i:
                    step(0, i + 1, 10, 6, i)
                    step(1, i + 1, 13, 9, i)
                for s in range(2):
                    step(s, STEPS // 2 - 1, 3 * (STEPS - 2 + s) + 4, 3 * (STEPS - 2 + s), last=(s == 1))

            def exps(L, u, scale, rows, units, probs, per_layer, nm):
                s = u % 2
                act.wait_ge(sm_max, L.blk * DEPTH * H + L.l * per_layer + (u + 1))
                S, pr = psum(L, ("s", u)), probs[:, s * 384:(s + 1) * 384]
                nc.scalar.activation(pr[:, 0:P], S[:, 0:P], ACT.Exp, scale=scale, bias=nm[:, 2 * s:2 * s + 1], accum_out=rows[:, u:u + 1])
                drained(L, ("s", u), nc.scalar.activation(pr[:, P:3 * P], S[:, P:3 * P], ACT.Exp, scale=scale,
                                                          bias=nm[:, 2 * s + 1:2 * s + 2], accum_out=rows[:, units + u:units + u + 1]))

            def first_mixer(L, own):
                xbcu = m1("xbcu", 6 * 260).rearrange("p (t n) -> p t n", t=6)
                xbcs = m1("xbcs", 6 * SEQ).rearrange("p (t n) -> p t n", t=6)
                keep = {GQ: m1("gq", 512), GK: m1("gk", 512), FQ: m1("fqk", 1024)[:, 0:512], FK: m1("fqk", 1024)[:, 512:1024],
                        GV: m1("av", 512), FV: m1("bv", 512), DC: m1("dc", 512), DB: m1("db", 512)}
                act.wait_ge(s_par, 16 * L.deep + 16)
                for m in range(IP1):
                    out = psum(L, ("ip", m))
                    if m not in (ROWS, DV):
                        wait_full(act, L, ("ip", m))
                    if m <= XBC2:
                        drained(L, ("ip", m), nc.scalar.copy(xbcu[:, 2 * m:2 * m + 2, 3:3 + SEQ], out[:].rearrange("p (t n) -> p t n", t=2)))
                    elif m in (ZG, GG):
                        drained(L, ("ip", m), nc.scalar.activation(m1("siluz" if m == ZG else "silug", 512), out[:], ACT.Silu))
                    elif m in keep:
                        if m == GV:
                            nc.scalar.copy(m1("avs", 256)[0:HD, :], out[HD:2 * HD, 0:GW])
                        drained(L, ("ip", m), nc.scalar.copy(keep[m], out[:]))
                    for n in (2 * m + 4, 2 * m + 5):
                        split_hi(L, FFN_SLOTS + n)
                    if 1 <= m <= 3:
                        act.wait_ge(ev(f"conv{m - 1}"), L.one)
                        for t in (2 * m - 2, 2 * m - 1):
                            ins = nc.scalar.activation(xbcs[:, t, :], xbcs[:, t, :], ACT.Silu, bias=p1("convb")[:, t:t + 1])
                        ins.then_inc(ev(f"xbc_act{m - 1}"), 1)
                    if m == GG:
                        nc.scalar.preload_act_table_set("natural_log_exp_and_others")
                    if m == ROWS:
                        act.wait_ge(ev("rows_na"), L.one)
                        nc.scalar.activation(m1("ralogx", 1), p1("ralog"), ACT.Exp)
                        nc.scalar.activation(m1("re", SEQ), m1("re", SEQ), ACT.Exp).then_inc(ev("rows_e"), 1)
                    if m == GK:
                        act.wait_ge(ev("rows_cs"), L.one)
                        rcs, rE = m1("rcs", SEQ), m1("rE", SEQ)
                        nc.scalar.activation(rE[:, 0:P], rcs[:, 0:P], ACT.Exp, scale=-1.0, bias=rcs[:, P - 1:P])
                        nc.scalar.activation(rE[:, P:2 * P], rcs[:, P:2 * P], ACT.Exp).then_inc(ev("rowsE"), 1)
                    if m == FQ:
                        act.wait_ge(ev("z_na"), L.one)
                        ge = m1("ge", 512)
                        own.link(nc.scalar.activation(ge, ge, ACT.Exp))
                        nc.scalar.activation(ge, ge, ACT.Ln, bias=1.0).then_inc(ev("z_l"), 1)
                    if m == FK:
                        act.wait_ge(ev("gla_b"), L.one)
                        gb, gd = m1("gb", 512), m1("gd", 512)
                        nc.scalar.activation(m1("eb", 512), gb, ACT.Exp, scale=1.0 / 16)
                        nc.scalar.activation(m1("enb", 512), gb, ACT.Exp, scale=-1.0 / 16)
                        nc.scalar.activation(gd, gd, ACT.Exp, scale=1.0 / 16).then_inc(ev("gla_exp"), 1)

                def take(name, dst, src, func=None):
                    wait_full(act, L, name)
                    drained(L, name, nc.scalar.activation(dst, src, func) if func else nc.scalar.copy(dst, src))

                take("ssd_b", m1("Bt", 256), psum(L, "ssd_b")[:, 0:256])
                kend, kendT = psum(L, "gla_kend"), m1("kendT", 768).rearrange("p (c n) -> p c n", c=3)
                wait_full(act, L, "gla_kend")
                for c in range(2):
                    nc.scalar.copy(kendT[0:HD, c, :], kend[HD * c:HD * c + HD, 0:GW])
                drained(L, "gla_kend", nc.scalar.copy(kendT[0:HD, 2, :], kend[0:HD, GW:2 * GW]))
                for h in range(H):
                    take(f"ssd_seg{h}", m1("Lm", 1024).rearrange("p (t h n) -> p t h n", t=NT, h=H)[:, :, h, :],
                         psum(L, f"ssd_seg{h}")[:, 0:2 * P].rearrange("p (t n) -> p t n", t=NT), ACT.Exp)
                take("fox_q", m1("fT", 1024)[:, 0:512], psum(L, "fox_q")[:])
                take("fox_k", m1("fT", 1024)[:, 512:1024], psum(L, "fox_k")[:])
                take("ssd_st", m1("St", 256), psum(L, "ssd_st")[:, 0:256])
                for name, c in (("gla_o", 0), ("sc_t", 3 * GW)):
                    take(name, xs[:, :, c:c + GW], psum(L, name)[:].rearrange("p (t n) -> p t n", t=NT))
                for u in range(H):
                    exps(L, u, 1.0, m1("rowsum", 8), H, m1("P", 768), H, m1("nm", 4))
                finish(L, FFN_SLOTS + MIX1)

            def finish(L, end):
                quarters(L, 2, lambda T, j: ("yT", T, j))
                for n in range(end - 4, end + AHEAD):
                    split_hi(L, n)

            def second_mixer(L, own):
                nc.scalar.preload_act_table_set("exp_and_others")
                kx = m2("kx", 1024).rearrange("p (c g n) -> p c g n", c=2, g=2)
                keep = {VSW: m2("vsw", 512), MV0: m2("mv", 1024)[:, 0:512], MV1: m2("mv", 1024)[:, 512:1024]}
                for m in range(IP2 + 1):
                    out = psum(L, ("ip", m))
                    wait_full(act, L, ("ip", m))
                    if m == KVC:
                        src = out[:].rearrange("p (c n) -> p c n", c=2)
                        for g in range(2):
                            nc.scalar.copy(kx[0:HD, :, g, :], src[HD * g:HD * g + HD, :, :])
                            ins = nc.scalar.copy(kx[HD:P, :, g, 0:SEQ - 1], src[HD * g:HD * g + HD, :, 1:SEQ])
                        drained(L, ("ip", m), ins)
                    elif m in ROPED:
                        if m in (MQ1, MK0, MK1):
                            wait_drained(act, L, ("rot", {MQ1: KSW, MK0: MQ0, MK1: MQ1}[m]))
                        drained(L, ("ip", m), nc.scalar.copy(raw_of(m), out[:]))
                    elif m == GATES:
                        drained(L, ("ip", m), nc.scalar.activation(m2("gex", 64), out[:, 0:64], ACT.Exp, scale=-1.0))
                    else:
                        drained(L, ("ip", m), nc.scalar.copy(keep[m], out[:]))
                    for n in (2 * m + 4, 2 * m + 5) if m != GATES else (2 * m + 4,):
                        split_hi(L, FFN_SLOTS + n)
                for c in range(2):
                    act.wait_ge(ev(f"blk{c}"), L.one)
                    nc.scalar.copy(hhi[:, c * 480:(c + 1) * 480], m2("blk", 960)[:, c * 480:(c + 1) * 480]).then_inc(ev(f"blk_hi{c}"), 1)
                first = FFN_SLOTS + 2 * IP2 + 1
                for n in range(first + AHEAD, first + 2 * CMP_SLOTS):
                    split_hi(L, n)
                for c in range(2):
                    act.wait_ge(ev(f"gelu_in{c}"), L.one)
                    nc.scalar.activation(m2("he", 64), m2("hu", 64), ACT.Exp, scale=-2.0 * (2.0 / np.pi) ** 0.5).then_inc(ev(f"gelu_e{c}"), 1)
                for n in range(first + 2 * CMP_SLOTS, first + 2 * CMP_SLOTS + AHEAD):
                    split_hi(L, n)
                wait_drained(act, L, "cmp_s")
                nc.scalar.activation(m2("cs", 256), m2("cs", 256), ACT.Exp, scale=SCALE).then_inc(ev("cmp_exp"), 1)
                wait_full(act, L, "cmp_pt")
                drained(L, "cmp_pt", nc.scalar.copy(m2("cpT", 256), psum(L, "cmp_pt")[:, 0:256]))
                for u in range(UNITS):
                    exps(L, u, SCALE, m2("rowsum", 2 * UNITS), UNITS, m2("P", 768), UNITS, m2("nm", 4))
                finish(L, FFN_SLOTS + MIX2)

            act.wait_ge(s_x, 16)
            for n in range(AHEAD):
                split_hi(Layer(0, 0), n)
            for blk, mixer in enumerate((first_mixer, second_mixer)):
                with act.Fori(0, DEPTH) as l:
                    L = Layer(l, blk)
                    own = Own(act, act_own, L)
                    norm(L, 0)
                    ffn(L, 0)
                    norm(L, 1)
                    mixer(L, own)
                    norm(L, 2)
                    ffn(L, 1)
                    own.close()
            squares(Layer(DEPTH, 1), 0)

        @block.vector
        def _(dve):
            def split_lo(L, n, i=0):
                place, _ = L.raw_use(n)
                dve.wait_ge(hi_done, L.slot0 + (n + 1) + RING * i)
                dve.tensor_tensor(wlo[:, place, :], raw[:, place, :], whi[:, place, :].bitcast(F32), ALU.subtract).then_inc(split_done, 1)

            def quarters(L, q, name):
                for T in range(NT):
                    for j in range(2):
                        k, t = quarter(j, T)
                        dve.wait_ge(thi_done, 16 * L.deep + (4 * q + 2 * T + j + 1))
                        drained(L, name(T, j), dve.tensor_tensor(tlo[:, k, t], psum(L, name(T, j))[:].rearrange("p (k n) -> p k n", k=4),
                                                                 thi[:, k, t].bitcast(F32), ALU.subtract))

            def inverse_root(own, sums, n, count):
                v, y, t, vh = (stat[:, 32 * i:32 * i + n] for i in range(4))
                own.link(dve.tensor_scalar(v, sums, 1.0 / count, EPS, ALU.mult, ALU.add))
                own.step(dve.tensor_scalar(vh, v, -0.5, None, ALU.mult))
                own.link(dve.tensor_scalar(t.bitcast(I32), v.bitcast(I32), 1, None, ALU.logical_shift_right))
                own.link(dve.tensor_scalar(y.bitcast(I32), t.bitcast(I32), -1.0, float(0x5f3759df), ALU.mult, ALU.add))
                for _ in range(3):
                    own.link(dve.tensor_tensor(t, y, y, ALU.mult))
                    own.link(dve.tensor_tensor(t, t, vh, ALU.mult))
                    own.link(dve.scalar_tensor_tensor(y, t, 1.5, y, ALU.add, ALU.mult))
                return y

            def scale_x(L, own, w):
                dve.wait_ge(sq_done, L.deep * (3 * NT) + (w * NT + NT))
                rstd = inverse_root(own, stat[:, P:P + NT], NT, D)
                dve.wait_ge(s_gain, L.deep * 48 + (16 * w + 16))
                for T in range(NT):
                    dve.scalar_tensor_tensor(xs[:, T, :], x[:, T, :], rstd[:, T:T + 1], gain[:], ALU.mult, ALU.mult).then_inc(xs_ready, 1)

            def norm(L, own, w):
                scale_x(L, own, w)
                quarters(L, (0, 1, 3)[w], lambda T, j: ("norm", w, T, j))

            def add_to_x(L, name, factor):
                for T in range(NT):
                    for half in range(2):
                        wait_full(dve, L, name(T, half))
                        part = x[:, T, half * 512:(half + 1) * 512]
                        drained(L, name(T, half), dve.scalar_tensor_tensor(part, psum(L, name(T, half))[:], factor, part, ALU.mult, ALU.add))

            def ffn(L, f):
                base = f * (FFN_SLOTS + (MIX2 if L.blk else MIX1))
                steps0 = (2 * L.deep + f) * STEPS

                def step(s, j, n, i=0, last=False):
                    c = s * SEQ
                    b = L.bank(("gu", f, s))[0]
                    dve.wait_ge(sg_done, steps0 + (j + 1) + 2 * i)
                    dve.tensor_tensor(hf[:, s, :], sg[:, s, :], bank[b][:, SEQ:2 * SEQ], ALU.mult).then_inc(bank_read[b], 1)
                    if not last:
                        split_lo(L, base + n, i)
                    dve.wait_ge(hhi_done, steps0 + (j + 1) + 2 * i)
                    dve.tensor_tensor(hlo[:, c:c + SEQ], hf[:, s, :], hhi[:, c:c + SEQ].bitcast(F32), ALU.subtract).then_inc(h_ready, 1)
                    for m in range(0 if last else 1, 3):
                        split_lo(L, base + n + m, i)

                step(0, 0, 4)
                step(1, 1, 7)
                with dve.Fori(0, STEPS // 2 - 2) as i:
                    step(0, 2, 10, i)
                    step(1, 3, 13, i)
                for s in range(2):
                    step(s, STEPS - 2 + s, 3 * (STEPS - 2 + s) + 4, last=(s == 1))
                add_to_x(L, lambda T, half: ("acc", f, T, half), 0.5)

            def maxima(L, own, u, scale, mx, nm):
                s = u % 2
                wait_full(dve, L, ("s", u))
                S = psum(L, ("s", u))
                own.step(dve.tensor_reduce(mx[:, 2 * s:2 * s + 1], S[:, 0:P], AX, ALU.max))
                own.link(dve.tensor_reduce(mx[:, 2 * s + 1:2 * s + 2], S[:, P:3 * P], AX, ALU.max))
                dve.tensor_scalar(nm[:, 2 * s:2 * s + 2], mx[:, 2 * s:2 * s + 2], -scale, None, ALU.mult).then_inc(sm_max, 1)

            def keep_turned(L, u, pt):
                wait_full(dve, L, ("pt", u))
                s = u % 2
                drained(L, ("pt", u), dve.tensor_copy(pt[:, s * 384:(s + 1) * 384], psum(L, ("pt", u))[:, 0:384]))

            def finish(L, end):
                quarters(L, 2, lambda T, j: ("yT", T, j))
                for n in range(end - 4, end + AHEAD):
                    split_lo(L, n)
                add_to_x(L, lambda T, half: ("wo", T, half), 1.0)

            def bc(ap, shape):
                return ap.to_broadcast(shape)

            def convolve(own, dst, src, weights, taps):
                for k in range(taps):
                    for t, d in enumerate(dst):
                        s, w = src[t][:, k:k + SEQ], weights[:, t * taps + k:t * taps + k + 1]
                        if k == 0:
                            ins = dve.tensor_scalar(d, s, w, None, ALU.mult)
                        else:
                            ins = dve.scalar_tensor_tensor(d, s, w, d, ALU.mult, ALU.add)
                        if k < taps - 1:
                            own.step(ins)
                    if k < taps - 1:
                        own.wait()
                return ins

            def first_mixer(L, own):
                xbcu = m1("xbcu", 6 * 260).rearrange("p (t n) -> p t n", t=6)
                xbcs = m1("xbcs", 6 * SEQ).rearrange("p (t n) -> p t n", t=6)
                dcu = m1("dcu", 520).rearrange("p (t n) -> p t n", t=2)
                sel = c_("sel")
                zb, ge, gb, gd = m1("zb", 512), m1("ge", 512), m1("gb", 512), m1("gd", 512)
                gq, gk = m1("gq", 512), m1("gk", 512)
                ru, re, rs, rs2, rp, rsp, rcs = (m1(n, SEQ) for n in ("ru", "re", "rs", "rs2", "rp", "rsp", "rcs"))
                rows_bank = psum(L, ("ip", ROWS))
                own.link(dve.memset(xbcu[:, :, 0:3], 0.0))
                dve.wait_ge(s_par, 16 * L.deep + 16)
                for m in range(IP1):
                    if m == ROWS:
                        wait_full(dve, L, ("ip", ROWS))
                        dve.tensor_copy(m1("lrT", SEQ)[0:16, :], rows_bank[0:16, 0:SEQ])
                        drained(L, ("ip", ROWS), dve.tensor_scalar(ru, rows_bank[:, SEQ:2 * SEQ], p1("rbias"), sel[:, 0:1], ALU.add, ALU.mult))
                    if m == DV:
                        own.link(dve.memset(dcu[:, :, 0:2], 0.0))
                        wait_full(dve, L, ("ip", DV))
                        wait_drained(dve, L, ("ip", DC))
                        drained(L, ("ip", DV), dve.tensor_tensor(dcu[:, :, 2:2 + SEQ], m1("dc", 512).rearrange("p (t n) -> p t n", t=2),
                                                                 psum(L, ("ip", DV))[:].rearrange("p (t n) -> p t n", t=2), ALU.mult))
                    for n in (2 * m + 4, 2 * m + 5):
                        split_lo(L, FFN_SLOTS + n)
                    if m <= XBC2:
                        wait_drained(dve, L, ("ip", m))
                        tiles = (2 * m, 2 * m + 1)
                        convolve(own, [xbcs[:, t, :] for t in tiles], [xbcu[:, t, :] for t in tiles],
                                 p1("convw")[:, 8 * m:8 * m + 8], 4).then_inc(ev(f"conv{m}"), 1)
                    if m == ROWS:
                        wait_drained(dve, L, ("ip", ROWS))
                        dve.scalar_tensor_tensor(re, ru, -1.0, ru, ALU.mult, ALU.min).then_inc(ev("rows_na"), 1)
                    if m == GQ:
                        dve.wait_ge(ev("rows_e"), L.one)
                        own.link(dve.tensor_scalar(rs, re, 2.0, None, ALU.add))
                        own.link(dve.reciprocal(rs, rs))
                        own.link(dve.tensor_tensor(rs, rs, re, ALU.mult))
                        own.link(dve.tensor_tensor(rs2, rs, rs, ALU.mult))
                        own.link(dve.tensor_scalar(rp, rs2, 1.0 / 17, None, ALU.mult))
                        for odd in (15, 13, 11, 9, 7, 5, 3):
                            own.link(dve.scalar_tensor_tensor(rp, rp, 1.0 / odd, rs2, ALU.add, ALU.mult))
                        own.link(dve.scalar_tensor_tensor(rp, rp, 1.0, rs, ALU.add, ALU.mult))
                        own.step(dve.tensor_scalar(ru, ru, 0.0, None, ALU.max))
                        own.link(dve.tensor_scalar(rp, rp, 2.0, None, ALU.mult))
                        own.link(dve.tensor_tensor(rsp, rp, ru, ALU.add))
                        own.link(dve.tensor_scalar(rp, rsp, m1("ralogx", 1), -1.0, ALU.mult, ALU.mult))
                        own.link(dve.tensor_tensor_scan(rcs, c_("rreset"), rp, 0.0, ALU.mult, ALU.add))
                        for i, name in enumerate(("FR", "DL", "DR")):
                            ins = dve.tensor_scalar(m1(name, SEQ), rcs, sel[:, 1 + 2 * i:2 + 2 * i], sel[:, 2 + 2 * i:3 + 2 * i], ALU.mult, ALU.add)
                        ins.then_inc(ev("rows_cs"), 1)
                    if m == FQ:
                        wait_full(dve, L, "gla_z")
                        z = psum(L, "gla_z")
                        own.step(dve.tensor_scalar(zb[:, 0:SEQ], z[:, 0:SEQ], p1("gbg")[:, 0:1], None, ALU.add))
                        drained(L, "gla_z", dve.tensor_scalar(zb[:, SEQ:512], z[:, SEQ:512], p1("gbg")[:, 1:2], None, ALU.add))
                        wait_drained(dve, L, "gla_z")
                        dve.scalar_tensor_tensor(ge, zb, -1.0, zb, ALU.mult, ALU.min).then_inc(ev("z_na"), 1)
                    if m == FK:
                        dve.wait_ge(ev("z_l"), L.one)
                        own.link(dve.scalar_tensor_tensor(zb, zb, 0.0, ge, ALU.min, ALU.subtract))
                        own.link(dve.tensor_tensor_scan(gb, c_("greset"), zb, 0.0, ALU.mult, ALU.add))
                        b3 = gb.rearrange("p (c n) -> p c n", n=HD)
                        dve.tensor_tensor(gd.rearrange("p (c n) -> p c n", n=HD), bc(b3[:, :, HD - 1:HD], [P, 8, HD]), b3,
                                          ALU.subtract).then_inc(ev("gla_b"), 1)
                    if m == GV:
                        dve.wait_ge(ev("gla_exp"), L.one)
                        wait_drained(dve, L, ("ip", GQ))
                        wait_drained(dve, L, ("ip", GK))
                        dve.scalar_tensor_tensor(gq, gq, SCALE, m1("eb", 512), ALU.mult, ALU.mult)
                        dve.tensor_tensor(m1("kend", 512), gk, gd, ALU.mult)
                        dve.tensor_tensor(gk, gk, m1("enb", 512), ALU.mult).then_inc(ev("gla_dec"), 1)
                    if m == FV:
                        wait_drained(dve, L, ("ip", FQ))
                        wait_drained(dve, L, ("ip", FK))
                        fqk, fsq = m1("fqk", 1024), m1("fsq", 1024)
                        own.link(dve.tensor_tensor(fsq, fqk, fqk, ALU.mult))
                        own.link(dve.tensor_reduce(stat[:, 160:176], fsq.rearrange("p (g n) -> p g n", n=HD), AX, ALU.add))
                        rstd = inverse_root(own, stat[:, 160:176], 16, HD)
                        own.link(dve.tensor_scalar(rstd[:, 0:8], rstd[:, 0:8], SCALE, None, ALU.mult))
                        f3 = fqk.rearrange("p (g n) -> p g n", n=HD)
                        own.link(dve.tensor_tensor(f3, f3, bc(rstd.unsqueeze(2), [P, 16, HD]), ALU.mult))
                        for c, name in enumerate(("fqg", "fkg")):
                            part = f3[:, 8 * c:8 * c + 8, :]
                            ins = dve.tensor_tensor(part, part, bc(p1(name).unsqueeze(1), [P, 8, HD]), ALU.mult)
                        ins.then_inc(ev("fqk_ready"), 1)
                    if m == DB:
                        wait_drained(dve, L, ("ip", DV))
                        wait_drained(dve, L, ("ip", DB))
                        dy, db = m1("dy", 512), m1("db", 512)
                        own.link(convolve(own, [dy[:, 0:SEQ], dy[:, SEQ:512]], [dcu[:, 0, :], dcu[:, 1, :]], p1("scw"), 3))
                        dve.tensor_tensor(dy, dy, db, ALU.mult).then_inc(ev("dy_ready"), 1)

                tmr = m1("tmr", 16)
                wait_full(dve, L, "rowsT")
                drained(L, "rowsT", dve.tensor_copy(tmr.rearrange("p (q h) -> p q h", q=4),
                                                    psum(L, "rowsT")[:].rearrange("p (q h e) -> p q h e", q=4, h=H)[:, :, :, 2]))
                wait_full(dve, L, "ssd_xs")
                wait_drained(dve, L, "rowsT")
                x3 = psum(L, "ssd_xs")[:].rearrange("p (g n) -> p g n", n=HD)
                xd, xsD, xdd = m1("xd", 512), m1("xsD", 512), m1("xdd", 256)
                own.step(dve.tensor_tensor(xd.rearrange("p (g n) -> p g n", n=HD), x3, bc(tmr[:, 0:8].unsqueeze(2), [P, 8, HD]), ALU.mult))
                for T in range(NT):
                    ins = dve.tensor_tensor(xsD.rearrange("p (g n) -> p g n", n=HD)[:, 4 * T:4 * T + 4, :], x3[:, 4 * T:4 * T + 4, :],
                                            bc(p1("skip").unsqueeze(2), [P, H, HD]), ALU.mult)
                drained(L, "ssd_xs", ins)
                own.wait()
                dve.tensor_tensor(xdd.rearrange("p (g n) -> p g n", n=HD), xd[:, 0:256].rearrange("p (g n) -> p g n", n=HD),
                                  bc(tmr[:, 8:12].unsqueeze(2), [P, H, HD]), ALU.mult).then_inc(ev("xd_ready"), 1)
                wait_full(dve, L, "ssd_sc")
                sc = psum(L, "ssd_sc")[:].rearrange("p (g n) -> p g n", n=P)
                Mt, Lm = (m1(n, 1024).rearrange("p (g e n) -> p g e n", g=4, e=2) for n in ("Mt", "Lm"))
                for h in range(H):
                    wait_drained(dve, L, f"ssd_seg{h}")
                for g in range(4):
                    ins = dve.tensor_tensor(Mt[:, g], sc[:, g, :].unsqueeze(1).to_broadcast([P, 2, P]), Lm[:, g], ALU.mult)
                drained(L, "ssd_sc", ins)
                for hh in range(2):
                    wait_full(dve, L, f"gla_att{hh}")
                    drained(L, f"gla_att{hh}", dve.tensor_tensor(
                        m1("attT", 1024)[:, hh * 512:(hh + 1) * 512].rearrange("p (g n) -> p g n", g=4),
                        psum(L, f"gla_att{hh}")[:].rearrange("p (g n) -> p g n", g=4), bc(c_("glam").unsqueeze(1), [P, 4, P]), ALU.mult))
                wait_full(dve, L, "gla_kv")
                kv = psum(L, "gla_kv")[:, 0:384].rearrange("p (c t n) -> p c t n", c=3, t=2)
                Sg = m1("Sg", 384).rearrange("p (c t n) -> p c t n", c=3, t=2)
                eb = m1("eb", 512).rearrange("p (t c n) -> p t c n", t=2, c=4)
                own.link(dve.tensor_copy(Sg[:, 0], kv[:, 0]))
                for t in range(2):
                    own.step(dve.scalar_tensor_tensor(Sg[:, 1, t, :], Sg[:, 0, t, :], eb[:, t, 1, HD - 1:HD], kv[:, 1, t, :], ALU.mult, ALU.add))
                own.wait()
                for t in range(2):
                    ins = dve.scalar_tensor_tensor(Sg[:, 2, t, :], Sg[:, 1, t, :], eb[:, t, 2, HD - 1:HD], kv[:, 2, t, :], ALU.mult, ALU.add)
                drained(L, "gla_kv", ins)
                wait_drained(dve, L, "gla_kv")
                dve.tensor_tensor(m1("Sbd", 768).rearrange("p (g e n) -> p g e n", g=6, e=2),
                                  bc(m1("Sg", 384).rearrange("p (g n) -> p g n", g=6).unsqueeze(2), [P, 6, 2, HD]),
                                  bc(c_("half").unsqueeze(1).unsqueeze(3), [P, 6, 2, HD]), ALU.mult).then_inc(ev("gla_states"), 1)
                wait_full(dve, L, "ssd_y")
                drained(L, "ssd_y", dve.tensor_tensor(xsD, psum(L, "ssd_y")[:], xsD, ALU.add))
                for h in range(H):
                    ins = dve.tensor_scalar(m1("FL", 4 * SEQ)[:, h * SEQ:(h + 1) * SEQ], rcs, sel[:, 7 + 2 * h:8 + 2 * h],
                                            sel[:, 8 + 2 * h:9 + 2 * h], ALU.mult, ALU.add)
                ins.then_inc(ev("FL_ready"), 1)
                wait_full(dve, L, "ssd_yoff")
                drained(L, "ssd_yoff", dve.tensor_tensor(xdd.rearrange("p (g n) -> p g n", n=HD), psum(L, "ssd_yoff")[:, 0:256].rearrange("p (g n) -> p g n", n=HD),
                                                         bc(tmr[:, 12:16].unsqueeze(2), [P, H, HD]), ALU.mult))
                wait_drained(dve, L, "ssd_y")
                wait_drained(dve, L, "ssd_yoff")
                own.link(dve.tensor_tensor(xsD[:, 256:512], xsD[:, 256:512], xdd, ALU.add))
                own.step(dve.tensor_tensor(xs[:, :, 2 * GW:3 * GW], xsD.rearrange("p (t n) -> p t n", t=NT),
                                           m1("siluz", 512).rearrange("p (t n) -> p t n", t=NT), ALU.mult))
                for u in range(H + 1):
                    if u < H:
                        maxima(L, own, u, 1.0, m1("mx", 4), m1("nm", 4))
                    if u >= 1:
                        keep_turned(L, u - 1, m1("pt", 768))
                wait_full(dve, L, ("o", 0))
                rec = m1("frec", 8)
                own.link(dve.reciprocal(rec, m1("rowsum", 8)))
                o4 = psum(L, ("o", 0))[:].rearrange("p (t h n) -> p t h n", t=NT, h=H)
                y5 = xs[:].rearrange("p t (g n) -> p t g n", n=HD)
                for T in range(NT):
                    ins = dve.tensor_tensor(y5[:, T, 4:8, :], o4[:, T], bc(rec[:, 4 * T:4 * T + 4].unsqueeze(2), [P, H, HD]), ALU.mult)
                drained(L, ("o", 0), ins)
                for name in ("gla_o", "sc_t", ("o", 0)):
                    wait_drained(dve, L, name)
                own.wait()
                ysq = m1("ysq", 2048).rearrange("p (t n) -> p t n", t=NT)
                own.link(dve.tensor_tensor(ysq, xs[:], xs[:], ALU.mult))
                ss = stat[:, 160:192]
                own.link(dve.tensor_reduce(ss, ysq.rearrange("p t (g n) -> p (t g) n", n=HD), AX, ALU.add))
                s3 = ss.rearrange("p (t g) -> p t g", t=NT)[:, :, 8:12].rearrange("p t (a b) -> p t a b", b=2)
                pair = stat[:, 196:200].rearrange("p (t a) -> p t a", t=NT)
                own.link(dve.tensor_tensor(pair, s3[:, :, :, 0], s3[:, :, :, 1], ALU.add))
                own.link(dve.tensor_scalar(s3, bc(pair.unsqueeze(3), [P, NT, 2, 2]), 0.5, None, ALU.mult))
                rstd = inverse_root(own, ss, 32, HD)
                y3 = xs[:].rearrange("p t (g n) -> p (t g) n", n=HD)
                own.link(dve.tensor_tensor(y3, y3, bc(rstd.unsqueeze(2), [P, 32, HD]), ALU.mult))
                own.link(dve.tensor_tensor(xs[:], xs[:], bc(p1("ygain").unsqueeze(1), [P, NT, D]), ALU.mult))
                dve.tensor_tensor(xs[:, :, 0:GW], xs[:, :, 0:GW], m1("silug", 512).rearrange("p (t n) -> p t n", t=NT),
                                  ALU.mult).then_inc(ev("y_ready"), 1)
                finish(L, FFN_SLOTS + MIX1)

            def second_mixer(L, own):
                rotated = {KSW: m2("kr", 512), Q0: m2("qr", 1024)[:, 0:512], Q1: m2("qr", 1024)[:, 512:1024],
                           MQ0: m2("mqr", 1024)[:, 0:512], MQ1: m2("mqr", 1024)[:, 512:1024],
                           MK0: m2("mkr", 1024)[:, 0:512], MK1: m2("mkr", 1024)[:, 512:1024]}
                two = lambda ap: ap.rearrange("p (t n) -> p t n", t=2)
                dve.wait_ge(s_par, 16 * L.deep + 16)
                dve.memset(m2("hvr", 256), 0.0)
                dve.memset(m2("hu", 64), 0.0)
                own.link(dve.memset(m2("kc", 32), 0.0))

                def rotate(m):
                    own.wait()
                    wait_full(dve, L, ("rot", m))
                    own.step(dve.tensor_tensor(two(m2("rc", 512)), two(raw_of(m)), bc(c_("ropeC").unsqueeze(1), [P, 2, SEQ]), ALU.mult))
                    drained(L, ("rot", m), dve.tensor_tensor(two(rotated[m]), two(psum(L, ("rot", m))[:]), bc(c_("ropeS").unsqueeze(1), [P, 2, SEQ]), ALU.mult))
                    own.wait()
                    wait_drained(dve, L, ("rot", m))
                    ins = dve.tensor_tensor(rotated[m], rotated[m], m2("rc", 512), ALU.add)
                    if m == MK1:
                        ins.then_inc(ev("roped"), 1)
                    else:
                        own.step(ins)

                for m in range(IP2 + 1):
                    for n in (2 * m + 4, 2 * m + 5) if m != GATES else (2 * m + 4,):
                        split_lo(L, FFN_SLOTS + n)
                    if m - 1 in ROPED:
                        rotate(m - 1)
                    if m == KSW:
                        wait_drained(dve, L, ("ip", KVC))
                        for c, pos in enumerate(("posk", "posv")):
                            for g in range(2):
                                src = m2("kx", 1024)[:, (2 * c + g) * SEQ:(2 * c + g + 1) * SEQ]
                                src = bass.AP(src.tensor, src.offset, [src.ap[0], (2, NCT), (NCT, NCMP)])
                                dst = m2("blk", 960)[:, c * 480:(c + 1) * 480].rearrange("p (k g n) -> p k g n", k=NCT, g=2)[:, :, g, :]
                                ins = dve.tensor_tensor(dst, src, bc(p2(pos).unsqueeze(2), [P, NCT, NCMP]), ALU.add)
                            ins.then_inc(ev(f"blk{c}"), 1)
                gate = m2("gate", 64)
                wait_drained(dve, L, ("ip", GATES))
                own.link(dve.tensor_scalar(gate, m2("gex", 64), 1.0, None, ALU.add))
                own.link(dve.reciprocal(gate, gate))
                for c in range(2):
                    dve.wait_ge(ev(f"blk_hi{c}"), L.one)
                    dve.tensor_tensor(hlo[:, c * 480:(c + 1) * 480], m2("blk", 960)[:, c * 480:(c + 1) * 480],
                                      hhi[:, c * 480:(c + 1) * 480].bitcast(F32), ALU.subtract).then_inc(ev(f"blk_ready{c}"), 1)
                first = FFN_SLOTS + 2 * IP2 + 1
                for n in range(first + AHEAD, first + 2 * CMP_SLOTS):
                    split_lo(L, n)
                hid, hx2, hu, he, hv = (m2(n, 64) for n in ("hid", "hx2", "hu", "he", "hv"))
                part = lambda ap: ap.rearrange("p (t n) -> p t n", t=2)[:, :, 0:2 * NCMP]
                for c in range(2):
                    if c:
                        dve.wait_ge(ev("gelu0"), L.one)
                    wait_full(dve, L, ("hid", c))
                    drained(L, ("hid", c), dve.tensor_copy(part(hid), part(psum(L, ("hid", c))[:, 0:64])))
                    wait_drained(dve, L, ("hid", c))
                    own.link(dve.tensor_tensor(part(hx2), part(hid), part(hid), ALU.mult))
                    own.link(dve.tensor_scalar(part(hx2), part(hx2), 0.044715, 1.0, ALU.mult, ALU.add))
                    own.link(dve.tensor_tensor(part(hu), part(hx2), part(hid), ALU.mult))
                    dve.tensor_scalar(part(hu), part(hu), -50.0, None, ALU.max).then_inc(ev(f"gelu_in{c}"), 1)
                    dve.wait_ge(ev(f"gelu_e{c}"), L.one)
                    own.link(dve.tensor_scalar(part(hv), part(he), 1.0, None, ALU.add))
                    own.link(dve.reciprocal(part(hv), part(hv)))
                    if c == 0:
                        dve.tensor_tensor(part(m2("hk", 64)), part(hv), part(hid), ALU.mult).then_inc(ev("gelu0"), 1)
                    else:
                        for t in range(2):
                            a, b = (ap[:, t * 32:t * 32 + 2 * NCMP].rearrange("p (g n) -> p g n", g=2).unsqueeze(1).to_broadcast([P, 4, 2, NCMP])
                                    for ap in (hv, hid))
                            dst = m2("hvr", 256)[:, t * P:(t + 1) * P].rearrange("p (r g n) -> p r g n", r=4, g=2)[:, :, :, 0:NCMP]
                            ins = dve.tensor_tensor(dst, a, b, ALU.mult)
                        ins.then_inc(ev("gelu1"), 1)
                for n in range(first + 2 * CMP_SLOTS, first + 2 * CMP_SLOTS + AHEAD):
                    split_lo(L, n)
                wait_full(dve, L, "kc")
                drained(L, "kc", dve.tensor_tensor(m2("kc", 32).rearrange("p (g n) -> p g n", g=2)[:, :, 0:NCMP],
                                                   psum(L, "kc")[:, 0:2 * NCMP].rearrange("p (g n) -> p g n", g=2),
                                                   bc(c_("half").unsqueeze(2), [P, 2, NCMP]), ALU.mult))
                wait_full(dve, L, "vc")
                drained(L, "vc", dve.tensor_tensor(m2("vcd", 512).rearrange("p (g n) -> p g n", g=8), bc(psum(L, "vc")[:, 0:HD].unsqueeze(1), [P, 8, HD]),
                                                   bc(c_("own").unsqueeze(2), [P, 8, HD]), ALU.mult))
                wait_full(dve, L, "cmp_s")
                cs, cmx, csum, cfac = m2("cs", 256), m2("cmx", 16), m2("csum", 16), m2("cfac", 16)
                s3 = psum(L, "cmp_s")[:, 0:256].rearrange("p (g n) -> p g n", n=16)
                own.link(dve.tensor_reduce(cmx, s3, AX, ALU.max))
                own.link(dve.tensor_scalar(cmx, cmx, NEG / 10, None, ALU.max))
                drained(L, "cmp_s", dve.tensor_tensor(cs.rearrange("p (g n) -> p g n", n=16), s3, bc(cmx.unsqueeze(2), [P, 16, 16]), ALU.subtract))
                dve.wait_ge(ev("cmp_exp"), L.one)
                own.link(dve.tensor_reduce(csum, cs.rearrange("p (g n) -> p g n", n=16), AX, ALU.add))
                own.link(dve.tensor_scalar(csum, csum, 1.0, None, ALU.max))
                own.link(dve.reciprocal(csum, csum))
                g4 = gate.rearrange("p (t n) -> p t n", t=NT)
                for T in range(NT):
                    heads = lambda ap: ap.rearrange("p (g r) -> p g r", g=2)
                    own.step(dve.tensor_tensor(heads(cfac[:, 8 * T:8 * T + 8]), csum[:, 8 * T:8 * T + 8].rearrange("p (r g) -> p g r", g=2),
                                               heads(g4[:, T, 0:8]), ALU.mult))
                own.wait()
                y4 = xs[:].rearrange("p t (g n) -> p t g n", n=HD)
                for T in range(NT):
                    wait_full(dve, L, f"cmp_o{T}")
                    drained(L, f"cmp_o{T}", dve.tensor_tensor(
                        y4[:, T, 0:8, :], psum(L, f"cmp_o{T}")[:].rearrange("p (g n) -> p g n", g=8),
                        bc(cfac[:, 8 * T:8 * T + 8].unsqueeze(2), [P, 8, HD]), ALU.mult))
                rowsum = m2("rowsum", 2 * UNITS).rearrange("p (t u) -> p t u", t=NT)
                fac = m2("fac", 8).rearrange("p (t u) -> p t u", t=NT)
                otmp = m2("otmp", 512)
                for u in range(UNITS + 3):
                    if u < UNITS:
                        maxima(L, own, u, SCALE, m2("mx", 4), m2("nm", 4))
                    if 1 <= u <= UNITS:
                        keep_turned(L, u - 1, m2("pt", 768))
                    if u >= 3 and (u - 3) % 4 == 3:
                        q = (u - 3) // 4
                        kind, h0 = q // 2, 4 * (q % 2)
                        wait_full(dve, L, ("o", q))
                        own.link(dve.reciprocal(fac, rowsum[:, :, 4 * q:4 * q + 4]))
                        if kind < 2:
                            own.link(dve.tensor_tensor(fac, fac, g4[:, :, 8 + 8 * kind + h0:12 + 8 * kind + h0], ALU.mult))
                        o4 = psum(L, ("o", q))[:].rearrange("p (t h n) -> p t h n", t=NT, h=4)
                        t4 = otmp.rearrange("p (t h n) -> p t h n", t=NT, h=4)
                        for T in range(NT):
                            dst = t4[:, T] if kind < 2 else y4[:, T, 8 + h0:12 + h0, :]
                            ins = dve.tensor_tensor(dst, o4[:, T], bc(fac[:, T, :].unsqueeze(2), [P, 4, HD]), ALU.mult)
                        drained(L, ("o", q), ins)
                        if kind < 2:
                            wait_drained(dve, L, ("o", q))
                            yp = xs[:, :, h0 * HD:(h0 + 4) * HD]
                            own.step(dve.tensor_tensor(yp, yp, otmp.rearrange("p (t n) -> p t n", t=NT), ALU.add))
                            own.wait()
                finish(L, FFN_SLOTS + MIX2)

            dve.sem_inc(split_done, RING)
            dve.sem_inc(xs_ready, NT)
            for b in range(8):
                dve.sem_inc(bank_read[b], 1)
            dve.wait_ge(s_con, 16)
            dve.wait_ge(s_x, 16)
            for n in range(AHEAD):
                split_lo(Layer(0, 0), n)
            for blk, mixer in enumerate((first_mixer, second_mixer)):
                with dve.Fori(0, DEPTH) as l:
                    L = Layer(l, blk)
                    own = Own(dve, dve_own, L)
                    norm(L, own, 0)
                    ffn(L, 0)
                    norm(L, own, 1)
                    mixer(L, own)
                    norm(L, own, 2)
                    ffn(L, 1)
                    own.close()
            last = Layer(DEPTH, 1)
            scale_x(last, Own(dve, dve_own, last), 0)


def constants():
    con = np.zeros((P, CON_W), np.float32)

    def put(name, value):
        con[:, CON[name][0]:CON[name][1]] = value

    p, c = np.arange(P)[:, None], np.arange(P)[None, :]
    put("ident", p == c)
    put("negq", np.where(c <= p, 0, NEG))
    put("negT", np.where(c >= p, 0, NEG))
    put("glam", (c >= p) & (c // HD == p // HD))
    tok = np.arange(SEQ)[None, :]
    put("rreset", np.where((p % 32 >= 2) & (p % 32 < 4) & (tok == P), 0, 1))
    put("greset", np.arange(2 * SEQ)[None, :] % HD != 0)
    sel = np.zeros((P, 15), np.float32)
    e = [np.arange(P) % 32 == i for i in range(4)]
    sel[:, 0] = np.where(e[0] | e[1], -1, 1)
    for at, picks in ((1, ((0, 0, 1), (1, -1, 0))), (3, ((2, 0, 1), (3, -1, 0))), (5, ((2, 1, 0), (3, 0, 1)))):
        for row, factor, shift in picks:
            sel[e[row], at], sel[e[row], at + 1] = factor, shift
    for h in range(H):
        sel[32 * h, 7 + 2 * h], sel[32 * h + 1, 8 + 2 * h] = 1, 1
    put("sel", sel)
    put("half", p // HD == np.arange(2)[None, :])
    put("own", (p // 16 % 2) * 4 + p // 32 == np.arange(8)[None, :])
    n, T = np.arange(16)[None, None, None, :], np.arange(NT)[None, :, None, None]
    seen = np.broadcast_to((n < NCMP) & (16 * n + 31 <= T * P + p[:, :, None, None]), (P, NT, 8, 16))
    put("cmpmask", np.where(seen, 0, NEG).reshape(P, 256))
    inv_freq = np.power(np.float32(500000.0), -(np.arange(0, 16, 2, dtype=np.float32) / np.float32(16)))
    angle = np.arange(SEQ, dtype=np.float32)[:, None] * inv_freq[None, :]
    cos, sin, turn = np.ones((P, SEQ), np.float32), np.zeros((P, SEQ), np.float32), np.zeros((P, P), np.float32)
    for q in range(P):
        d = q % HD
        if d < 16:
            cos[q], sin[q] = np.cos(angle[:, d % 8]), np.sin(angle[:, d % 8])
            turn[q + 8 if d < 8 else q - 8, q] = -1 if d < 8 else 1
    put("ropeC", cos)
    put("ropeS", sin)
    put("ropeR", turn)
    return con


def rows_tiles(w):
    return w.reshape(-1, P, w.shape[1]).transpose(1, 0, 2)


def fm_slot(w):
    return rows_tiles(w).reshape(P, -1)


def tm_slots(w):
    return [rows_tiles(w[half * 512:(half + 1) * 512]).reshape(P, -1) for half in range(2)]


def ffn_slots(gate, up, down):
    out = []
    for i in range(STEPS + 1):
        if i < STEPS:
            out += [fm_slot(gate[:, i * P:(i + 1) * P]), fm_slot(up[:, i * P:(i + 1) * P])]
        if i:
            out.append(down[(i - 1) * P:i * P])
    return out


def scattered(columns):
    out = np.zeros((D, P), np.float32)
    for at, col in columns:
        out[:, at:at + col.shape[1]] = col
    return out


def first_mixer_slots(w_in, w_out):
    names = ["a_q", "a_k", "a_v", "a_g", "a_lr", "b_q", "b_k", "b_v", "b_f", "c_z", "c_xbc", "c_dt", "d_b", "d_c", "d_v"]
    widths = [GW] * 4 + [16] + [GW] * 3 + [H] + [GW, 3 * GW, H] + [GW] * 3
    part = dict(zip(names, np.split(w_in, np.cumsum(widths)[:-1], axis=1)))
    fm = lambda w: [fm_slot(w[:, 0:P]), fm_slot(w[:, P:2 * P])]
    out = []
    for t in range(3):
        out += fm(part["c_xbc"][:, t * GW:(t + 1) * GW])
    out += tm_slots(part["c_z"]) + tm_slots(part["a_g"])
    rows = []
    for h in range(H):
        f, dt = part["b_f"][:, h:h + 1], part["c_dt"][:, h:h + 1]
        rows += [(32 * h, f), (32 * h + 1, f), (32 * h + 2, dt), (32 * h + 3, dt)]
    out += [fm_slot(scattered([(0, part["a_lr"])])), fm_slot(scattered(rows))]
    out += fm(part["a_q"]) + fm(part["a_k"])
    for name in ("b_q", "b_k", "a_v", "b_v"):
        out += tm_slots(part[name])
    for name in ("d_c", "d_v", "d_b"):
        out += fm(part[name])
    return out + [w_out[k * P:(k + 1) * P] for k in range(KD)]


def second_mixer_slots(w_in, w_ck1, w_cv1, w_out):
    q, kv, gates, moba = np.split(w_in, [512, 1280, 1304], axis=1)
    q = q.reshape(D, 2, 4, HD)
    k_cmp, v_cmp, k_slc, v_slc, k_win, v_win = (kv[:, i * P:(i + 1) * P] for i in range(6))
    fm = lambda w: fm_slot(np.ascontiguousarray(w))
    out = [fm(k_cmp), fm(v_cmp), fm(k_slc), fm(k_win)]
    out += [fm(q[:, :, r].reshape(D, P)) for r in range(4)]
    out += tm_slots(np.concatenate([v_slc, v_win], axis=1))
    out += [fm(moba[:, t * P:(t + 1) * P]) for t in range(8)]
    out += tm_slots(moba[:, 1024:1280]) + tm_slots(moba[:, 1280:1536])
    by_branch = gates.reshape(D, 8, 3).transpose(0, 2, 1).reshape(D, 24)
    out.append(fm_slot(scattered([(0, by_branch)])))
    for w in (w_ck1, w_cv1):
        for s in range(CMP_SLOTS):
            t, half = s // 2, s % 2
            out.append(fm_slot(np.ascontiguousarray(w[half * D:(half + 1) * D, t * P:(t + 1) * P])))
    return out + [w_out[k * P:(k + 1) * P] for k in range(KD)]


def stream(a):
    out = []
    for l in range(DEPTH):
        out += ffn_slots(a["ffn1_w_gate"][l], a["ffn1_w_up"][l], a["ffn1_w_down"][l])
        out += first_mixer_slots(a["w_in"][l], a["w_out"][l])
        out += ffn_slots(a["ffn2_w_gate"][l], a["ffn2_w_up"][l], a["ffn2_w_down"][l])
    for l in range(DEPTH):
        out += ffn_slots(a["w_ffn1_gate_2"][l], a["w_ffn1_up_2"][l], a["w_ffn1_down_2"][l])
        out += second_mixer_slots(a["w_in_2"][l], a["w_ck1_2"][l], a["w_cv1_2"][l], a["w_out_2"][l])
        out += ffn_slots(a["w_ffn2_gate_2"][l], a["w_ffn2_up_2"][l], a["w_ffn2_down_2"][l])
    out += [np.zeros((P, SLOT), np.float32)] * TAIL
    assert len(out) == N_SLOTS
    return np.stack(out)


def replicated(row):
    return np.broadcast_to(row, (P,) + row.shape)


def first_parameters(a, l):
    par = np.zeros((P, PAR1_W), np.float32)

    def put(name, value):
        par[:, PAR1[name][0]:PAR1[name][1]] = value

    put("convw", a["ssm_conv_w"][l].reshape(4, 6, P).transpose(2, 1, 0).reshape(P, 24))
    put("convb", a["ssm_conv_b"][l].reshape(6, P).T)
    put("scw", a["sc_conv_w"][l].reshape(3, 2, P).transpose(2, 1, 0).reshape(P, 6))
    put("skip", replicated(a["ssm_D"][l]))
    bias, a_log = np.zeros((P, 1), np.float32), np.zeros((P, 1), np.float32)
    for h in range(H):
        bias[32 * h:32 * h + 2, 0] = a["fox_b_forget"][l, h]
        bias[32 * h + 2:32 * h + 4, 0] = a["ssm_dt_bias"][l, h]
        a_log[32 * h + 2:32 * h + 4, 0] = a["ssm_A_log"][l, h]
    put("rbias", bias)
    put("ralog", a_log)
    put("gbg", a["gla_b_gate"][l].reshape(2, P).T)
    put("fqg", replicated(a["fox_q_norm"][l]))
    put("fkg", replicated(a["fox_k_norm"][l]))
    par[0:16, PAR1["gup"][0]:PAR1["gup"][1]] = a["gla_w_gate_up"][l]
    put("ygain", replicated(np.concatenate([a[n][l] for n in ("gla_norm", "fox_out_norm", "ssm_norm", "sc_out_norm")])))
    return par


def second_parameters(a, l):
    par = np.zeros((P, PAR2_W), np.float32)
    for name, source in (("posk", "pos_ck_2"), ("posv", "pos_cv_2")):
        par[:, PAR2[name][0]:PAR2[name][1]] = a[source][l].reshape(NCT, 2, HD).transpose(1, 2, 0).reshape(P, NCT)
    ck2, cv2 = rows_tiles(a["w_ck2_2"][l]), rows_tiles(a["w_cv2_2"][l])
    par[:, PAR2["ck2"][0]:PAR2["ck2"][1]] = np.concatenate([ck2, ck2], axis=2).reshape(P, 4 * HD)
    par[:, PAR2["cv2"][0]:PAR2["cv2"][1]] = cv2.reshape(P, 2 * HD)
    return par


def kernel(**inputs):
    import concourse.bacc as bacc
    from concourse.bass_utils import run_bass_kernel_spmd

    a = {name: np.asarray(value) for name, value in inputs.items()}
    gains = [a[n][l] for l in range(DEPTH) for n in ("ffn1_norm", "mix_norm", "ffn2_norm")]
    gains += [a[n][l] for l in range(DEPTH) for n in ("norm_ffn1_2", "norm_mix_2", "norm_ffn2_2")] + [a["norm_final_2"]]
    arrays = {
        "x": np.ascontiguousarray(a["x"][0].reshape(NT, P, D).transpose(1, 0, 2)),
        "w": stream(a),
        "gain": np.stack([replicated(g) for g in gains]),
        "par1": np.stack([first_parameters(a, l) for l in range(DEPTH)]),
        "par2": np.stack([second_parameters(a, l) for l in range(DEPTH)]),
        "con": constants(),
    }
    nc = bacc.Bacc("TRN2", target_bir_lowering=False, num_devices=1)
    args = [nc.dram_tensor(f"in_{name}_dram", array.shape, F32, kind="ExternalInput").ap() for name, array in arrays.items()]
    out_d = nc.dram_tensor("out_0_dram", (P, NT, D), F32, kind="ExternalOutput").ap()
    build(nc, *args, out_d)
    result = run_bass_kernel_spmd(nc, [{f"in_{n}_dram": v for n, v in arrays.items()}], core_ids=[0])
    return np.asarray(result.results[0]["out_0_dram"]).transpose(1, 0, 2).reshape(1, SEQ, D)
```

```python
from contextlib import ExitStack

import numpy as np

import concourse.bass as bass
from concourse import mybir

F32 = mybir.dt.float32
F32R = mybir.dt.float32r
I32 = mybir.dt.int32
ALU = mybir.AluOpType
ACT = mybir.ActivationFunctionType
AX = mybir.AxisListType.X

P = 128
SEQ, D, FF, DEPTH = 256, 1024, 2816, 2
NT = SEQ // P
KD = D // P
GW, HD, H = 256, 64, 4
EPS = 1e-6
NEG = -1e30
SCALE = HD ** -0.5
SLOT = 1024
RING = 6
AHEAD = 4
STEPS = FF // P
FFN_SLOTS = 3 * STEPS
IP1 = 15
IP2 = 11
WO_SLOTS = KD
MIX1 = 2 * IP1 + WO_SLOTS
CMP_SLOTS = 4
MIX2 = 2 * IP2 + 1 + 2 * CMP_SLOTS + WO_SLOTS
LAYER1 = 2 * FFN_SLOTS + MIX1
LAYER2 = 2 * FFN_SLOTS + MIX2
TAIL = AHEAD
N_SLOTS = DEPTH * (LAYER1 + LAYER2) + TAIL
NCMP = 15
NCT = 16
MIX_W = 18400
CHAIN = 256

XBC0, XBC1, XBC2, ZG, GG, ROWS, GQ, GK, FQ, FK, GV, FV, DC, DV, DB = range(IP1)
KVC, KSW, Q0, Q1, VSW, MQ0, MQ1, MK0, MK1, MV0, MV1, GATES = range(IP2 + 1)


ROPED = [KSW, Q0, Q1, MQ0, MQ1, MK0, MK1]
UNITS = 24


def positions(mix):
    total = 2 * FFN_SLOTS + mix
    gap = -total % RING
    return [n if n < FFN_SLOTS else n + gap for n in range(total)]


def columns(fields):
    at, out = 0, {}
    for name, width in fields:
        out[name] = (at, at + width)
        at += width
    return out, at


CON, CON_W = columns([("ident", P), ("negq", P), ("negT", P), ("glam", P), ("rreset", SEQ), ("greset", 2 * SEQ),
                      ("sel", 15), ("half", 2), ("own", 8), ("cmpmask", 256), ("ropeC", SEQ), ("ropeS", SEQ), ("ropeR", P)])
PAR1, PAR1_W = columns([("convw", 24), ("convb", 6), ("scw", 6), ("skip", 4), ("rbias", 1), ("ralog", 1), ("gbg", 2),
                        ("fqg", HD), ("fkg", HD), ("gup", GW), ("ygain", D)])
PAR2, PAR2_W = columns([("posk", NCT), ("posv", NCT), ("ck2", 4 * HD), ("cv2", 2 * HD)])


class Turns:

    def __init__(self):
        self.of, self.count, self.fulls = {}, [0] * 8, [0] * 8

    def add(self, name, bank, by_slot=None, times=1):
        self.of[name] = (bank, self.count[bank], self.fulls[bank], by_slot)
        self.count[bank] += times
        self.fulls[bank] += by_slot is None


def norm_turns(t, w):
    for j in range(KD // 2):
        t.add(("norm", w, j), j)


def ffn_turns(t, f, mixer):
    for s in range(2):
        t.add(("gu", f, s), s, by_slot=-1, times=STEPS // 2)
    t.add(("R", f), 2)
    end = FFN_SLOTS - 1 + f * (FFN_SLOTS + mixer)
    for T in range(NT):
        for half in range(2):
            t.add(("acc", f, T, half), 4 + 2 * T + half, by_slot=end if (T, half) == (NT - 1, 1) else None)


def out_turns(t, mixer):
    for j in range(KD // 2):
        t.add(("yT", j), j)
    end = FFN_SLOTS + mixer - 1
    for T in range(NT):
        for half in range(2):
            t.add(("wo", T, half), 4 + 2 * T + half, by_slot=end if (T, half) == (NT - 1, 1) else None)


def attention_turns(t, units, s_banks, pt_banks, o_bank):
    for u in range(units + 2):
        if u < units:
            t.add(("s", u), s_banks[u % 2])
        if 1 <= u <= units:
            t.add(("pt", u - 1), pt_banks[(u - 1) % 2])
        if u >= 2 and (u - 2) % 4 == 0:
            t.add(("o", (u - 2) // 4), o_bank((u - 2) // 4))


def first_turns():
    t = Turns()
    norm_turns(t, 0)
    ffn_turns(t, 0, MIX1)
    norm_turns(t, 1)
    for m in range(IP1):
        t.add(("ip", m), m % 4, by_slot=FFN_SLOTS + 2 * m + 1)
        if m == GK:
            t.add("gla_z", 4)
    for name, bank in (("ssd_xs", 5), ("ssd_b", 6), ("rowsT", 7), ("gla_kend", 4), ("ssd_sc", 3), ("ssd_seg0", 0),
                       ("ssd_seg1", 1), ("ssd_seg2", 2), ("ssd_seg3", 7), ("gla_att0", 5), ("gla_att1", 6), ("gla_kv", 2), ("fox_q", 7), ("fox_k", 4),
                       ("ssd_st", 3), ("ssd_y", 0), ("ssd_yoff", 1), ("gla_o", 5), ("sc_t", 6)):
        t.add(name, bank)
    attention_turns(t, H, (2, 3), (4, 7), lambda g: 0)
    out_turns(t, MIX1)
    norm_turns(t, 2)
    ffn_turns(t, 1, MIX1)
    return t


def second_turns():
    t = Turns()
    norm_turns(t, 0)
    ffn_turns(t, 0, MIX2)
    norm_turns(t, 1)
    for m in range(IP2 + 1):
        t.add(("ip", m), m % 4, by_slot=FFN_SLOTS + min(2 * m + 1, 2 * IP2))
        if m in ROPED:
            t.add(("rot", m), 4 + ROPED.index(m) % 2)
    for c in range(2):
        t.add(("hid", c), 6 + c, by_slot=FFN_SLOTS + 2 * IP2 + CMP_SLOTS * (c + 1))
    for name, bank in (("hidf", 4), ("kc", 4), ("vc", 5), ("cmp_s", 6), ("cmp_pt", 7), ("cmp_o0", 4), ("cmp_o1", 5)):
        t.add(name, bank)
    attention_turns(t, UNITS, (0, 1), (2, 3), lambda g: 6 + g % 2)
    out_turns(t, MIX2)
    norm_turns(t, 2)
    ffn_turns(t, 1, MIX2)
    return t


TURNS1, TURNS2 = first_turns(), second_turns()


class Layer:

    def __init__(self, l, blk):
        self.l, self.blk = l, blk
        self.turns = TURNS2 if blk else TURNS1
        pos = positions(MIX2 if blk else MIX1)
        self.pos = pos + [pos[-1] + 1 + n for n in range(AHEAD)]
        self.one = l + 1
        self.deep = l + blk * DEPTH
        self.each = self.deep + 1
        self.slot0 = l * (LAYER2 if blk else LAYER1) + blk * DEPTH * LAYER1
        self.chain0 = self.deep * CHAIN

    def bank(self, name):
        b, k, _, _ = self.turns.of[name]
        return b, self.l * self.turns.count[b] + (self.blk * DEPTH * TURNS1.count[b] + k)

    def fulls(self, name):
        b, _, k, _ = self.turns.of[name]
        return self.l * self.turns.fulls[b] + (self.blk * DEPTH * TURNS1.fulls[b] + k)

    def raw_use(self, n):
        place = self.pos[n] % RING
        per = [sum(p % RING == place for p in positions(m)) for m in (MIX1, MIX2)]
        return place, self.l * per[self.blk] + (self.blk * DEPTH * per[0] + sum(p % RING == place for p in self.pos[:n]))

    def before(self, n):
        p = self.pos[n] - RING
        while p >= 0 and p not in self.pos:
            p -= RING
        return self.pos.index(p) if p >= 0 else p


def build(nc, x_d, w_d, gain_d, last_gain_d, par1_d, par2_d, con_d, out_d):
    with ExitStack() as ctx:
        def sb(name, shape, dt=F32):
            return ctx.enter_context(nc.sbuf_tensor(name, shape, dt))

        def sem(name):
            return ctx.enter_context(nc.semaphore(name))

        raw = sb("raw", [P, RING, SLOT])
        whi = sb("whi", [P, RING, SLOT], F32R)
        wlo = sb("wlo", [P, RING, SLOT], F32R)
        x = sb("x", [P, NT, D])
        xs = sb("xs", [P, NT, D])
        thi = sb("thi", [P, KD, SEQ], F32R)
        tlo = sb("tlo", [P, KD, SEQ], F32R)
        gain = sb("gain", [P, 3 * KD])
        ones = sb("ones", [P, P])
        diag = sb("diag", [P, SEQ])
        root = sb("root", [P, SEQ])
        par = sb("par", [P, max(PAR1_W, PAR2_W)])
        con = sb("con", [P, CON_W])
        gu = sb("gu", [P, 2, 2, SEQ])
        hhi = sb("hhi", [P, 2 * NCT * 2 * NCMP], F32R)
        hlo = sb("hlo", [P, 2 * NCT * 2 * NCMP], F32R)
        stat = sb("stat", [P, 256])
        mix = sb("mix", [P, MIX_W])
        bank = [ctx.enter_context(nc.psum_tensor(f"bank{b}", [P, 512], F32)) for b in range(8)]

        def c_(name):
            return con[:, CON[name][0]:CON[name][1]]

        def p1(name):
            return par[:, PAR1[name][0]:PAR1[name][1]]

        def p2(name):
            return par[:, PAR2[name][0]:PAR2[name][1]]

        ident = c_("ident")

        class Parts:
            pass

        def carve(fields):
            part, at = {}, 0
            for name, width in fields:
                if isinstance(width, str):
                    part[name] = part[width]
                else:
                    part[name] = at
                    at += width
            assert at <= MIX_W, at
            return part

        M1 = carve([
            ("xbcu", 4 * 260), ("dcu", 2 * 260), ("xbcs", 6 * SEQ), ("siluz", 512), ("silug", 512),
            ("ru", SEQ), ("re", SEQ), ("rs", SEQ), ("rs2", SEQ), ("rp", SEQ),
            ("rsp", SEQ), ("rcs", SEQ), ("rE", SEQ), ("FR", SEQ), ("DL", SEQ), ("DR", SEQ), ("lrT", SEQ),
            ("gq", 512), ("gk", 512), ("zb", 512), ("ge", 512), ("gb", 512), ("eb", 512), ("enb", 512), ("gd", 512),
            ("kend", 512), ("fqk", "xbcu"), ("fsq", 1024), ("fT", "gd"), ("av", 512), ("bv", 512), ("dc", 512),
            ("avs", 256), ("db", 512), ("Bt", 256), ("Mt", 1024), ("St", "lrT"), ("kendT", 768), ("Sg", 384), ("Sbd", 768), ("FL", "Mt"),
            ("P", "gb"), ("Lm", "zb"), ("xd", "ru"), ("xsD", "rs"), ("xdd", "rp"), ("attT", "fsq"), ("ysq", "gb"),
            ("dy", "dc"), ("pt", "xbcs"), ("tmr", 16), ("ralogx", 1), ("mx", 4), ("nm", 4), ("rowsum", 8), ("frec", 8)])
        M2 = carve([
            ("kx", 1024), ("blk", 960), ("kr", 512), ("qraw", 1024), ("qr", 1024), ("mqr", 1024), ("mkr", 1024),
            ("rtmp", 1024), ("rc", 512), ("vsw", 512), ("mv", 1024), ("gate", 64), ("gex", SEQ), ("hidT", 512), ("hid", 128), ("hx2", 128),
            ("hu", 128), ("he", 128), ("hk", 64), ("hv", 128), ("hvr", 256), ("kc", 32), ("vcd", 512), ("cs", 256), ("cpT", 256),
            ("P", 768), ("pt", 768), ("mx", 4), ("nm", 4), ("rowsum", 2 * UNITS), ("fac", 8), ("otmp", 512),
            ("cmx", 16), ("csum", 16), ("cfac", 16)])

        def m1(name, width):
            return mix[:, M1[name]:M1[name] + width]

        def m2(name, width):
            return mix[:, M2[name]:M2[name] + width]

        s_x, s_con, s_par, s_gain, s_out = sem("x_loaded"), sem("con_loaded"), sem("par_loaded"), sem("gain_loaded"), sem("out_stored")
        s_raw = [sem(f"raw_loaded{i}") for i in range(RING)]
        hi_done = sem("hi_done")
        split_done = sem("split_done")
        slot_used = sem("slot_used")
        bank_full = [sem(f"bank_full{b}") for b in range(8)]
        bank_read = [sem(f"bank_read{b}") for b in range(8)]
        sq_done = sem("sq_done")
        xs_ready = sem("xs_ready")
        ones_set = sem("ones_set")
        thi_done = sem("thi_done")
        sg_done = sem("sg_done")
        hf_done = sem("hf_done")
        hhi_done = sem("hhi_done")
        h_ready = sem("h_ready")
        act_own, dve_own = sem("act_own"), sem("dve_own")
        sm_max = sem("sm_max")
        events = {}

        def ev(name):
            if name not in events:
                events[name] = sem(name)
            return events[name]

        def wait_full(eng, L, name):
            b, _, _, by_slot = L.turns.of[name]
            if by_slot is None:
                eng.wait_ge(bank_full[b], L.fulls(name) + 1)
            else:
                eng.wait_ge(slot_used, L.slot0 + (by_slot + 1 + RING))

        def wait_drained(eng, L, name):
            b, k = L.bank(name)
            eng.wait_ge(bank_read[b], k + 2)

        def claim(pe, L, name):
            b, k = L.bank(name)
            pe.wait_ge(bank_read[b], k + 1)
            return bank[b]

        def updated(eng, L, w, T, half):
            if w == 0:
                b, k = L.bank(("acc", 0, T, half))
                eng.wait_ge(bank_read[b], k + 1)
            else:
                wait_drained(eng, L, ("acc", 0, T, half) if w == 1 else ("wo", T, half))

        def ffn_slot(L, w):
            return AHEAD + (FFN_SLOTS + (MIX2 if L.blk else MIX1) if w else 0)

        def gain_of(L, w, k):
            return gain[:, w * KD + k:w * KD + k + 1]

        def psum(L, name):
            return bank[L.bank(name)[0]]

        def full(L, name, ins):
            ins.then_inc(bank_full[L.bank(name)[0]], 1)

        def drained(L, name, ins):
            ins.then_inc(bank_read[L.bank(name)[0]], 1)

        class Own:

            def __init__(self, eng, done, L):
                self.eng, self.done, self.L, self.n = eng, done, L, 0

            def step(self, ins):
                self.n += 1
                ins.then_inc(self.done, 1)

            def wait(self):
                self.eng.wait_ge(self.done, self.L.chain0 + self.n)

            def link(self, ins):
                self.step(ins)
                self.wait()

            def close(self):
                assert self.n <= CHAIN, self.n
                self.eng.sem_inc(self.done, CHAIN - self.n)

        def raw_of(m):
            if m in (Q0, Q1):
                return m2("qraw", 1024)[:, (m - Q0) * 512:(m - Q0 + 1) * 512]
            s = [KSW, MQ0, MQ1, MK0, MK1].index(m) % 2
            return m2("rtmp", 1024)[:, s * 512:(s + 1) * 512]

        block = ctx.enter_context(nc.Block())

        @block.sync
        def _(sp):
            def snap(value):
                return value if isinstance(value, int) else sp.snap(value)

            def load(L, n, i=0):
                place, uses = L.raw_use(n)
                slot = snap(L.slot0 + n + RING * i)
                free = snap(L.slot0 + (L.before(n) + 1 + RING) + RING * i)
                sp.wait_ge(split_done, free)
                sp.dma_start(raw[:, place, :], w_d[bass.ds(slot, 1)].rearrange("a p n -> (a p) n")).then_inc(s_raw[place], 16)

            def layer(l, blk):
                L = Layer(l, blk)
                mixer = MIX2 if blk else MIX1
                with sp.Fori(0, FFN_SLOTS // RING) as i:
                    for n in range(RING):
                        load(L, n, i)
                row = snap(l + 0)
                done = snap(L.slot0 + RING)
                sp.wait_ge(slot_used, done)
                src, width = (par2_d, PAR2_W) if blk else (par1_d, PAR1_W)
                sp.dma_start(par[:, 0:width], src[bass.ds(row, 1)].rearrange("a p n -> (a p) n")).then_inc(s_par, 16)
                for n in range(FFN_SLOTS, FFN_SLOTS + mixer):
                    load(L, n)
                with sp.Fori(0, FFN_SLOTS // RING) as i:
                    for n in range(RING):
                        load(L, FFN_SLOTS + mixer + n, i)
                row = snap(L.deep + 1)
                b, k = L.bank(("norm", 2, KD // 2 - 1))
                used = snap(k + 2)
                sp.wait_ge(bank_read[b], used)
                sp.dma_start(gain[:], gain_d[bass.ds(row, 1)].rearrange("a p n -> (a p) n")).then_inc(s_gain, 16)

            def last_uses(last, place):
                return (sum(p % RING == place for p in positions(MIX1)) + sum(p % RING == place for p in positions(MIX2))) * DEPTH \
                    + sum(p % RING == place for p in last.pos[:TAIL])

            sp.dma_start(x[:], x_d).then_inc(s_x, 16)
            sp.dma_start(con[:], con_d).then_inc(s_con, 16)
            sp.dma_start(gain[:], gain_d[0]).then_inc(s_gain, 16)
            with sp.Fori(0, DEPTH) as l:
                layer(l, 0)
            with sp.Fori(0, DEPTH) as l:
                layer(l, 1)
            last = Layer(DEPTH, 1)
            for n in range(TAIL):
                load(last, n)
            sp.wait_ge(slot_used, last.slot0 + RING)
            sp.dma_start(par[:, 0:D], last_gain_d).then_inc(s_par, 16)
            sp.wait_ge(xs_ready, NT)
            sp.dma_start(out_d, xs[:]).then_inc(s_out, 16)
            sp.wait_ge(s_out, 16)
            sp.wait_ge(s_gain, 16 * (2 * DEPTH + 1))
            for place in range(RING):
                sp.wait_ge(s_raw[place], 16 * last_uses(last, place))


        @block.tensor
        def _(pe):
            def wait_slot(L, n, i=0):
                pe.wait_ge(split_done, L.slot0 + (n + 1 + RING) + RING * i)

            def fm_tile(L, n, out, i=0, fresh=None):
                wait_slot(L, n, i)
                r = L.pos[n] % RING
                for k in range(KD):
                    if fresh is not None and k % 2 == 0:
                        wait_drained(pe, L, ("norm", fresh, k // 2))
                    hi, lo = whi[:, r, k * P:(k + 1) * P], wlo[:, r, k * P:(k + 1) * P]
                    pe.matmul(out, hi, thi[:, k, :], start=(k == 0), stop=False)
                    pe.matmul(out, hi, tlo[:, k, :], start=False, stop=False)
                    mm = pe.matmul(out, lo, thi[:, k, :], start=False, stop=(k == KD - 1))
                mm.then_inc(slot_used, 1)

            def tm_pair(L, n, out):
                wait_slot(L, n + 1)
                for T in range(NT):
                    for k in range(KD):
                        r, c = L.pos[n + k // 4] % RING, (k % 4) * GW
                        hi, lo = whi[:, r, c:c + GW], wlo[:, r, c:c + GW]
                        ahi, alo = thi[:, k, T * P:(T + 1) * P], tlo[:, k, T * P:(T + 1) * P]
                        o = out[:, T * GW:(T + 1) * GW]
                        pe.matmul(o, ahi, hi, start=(k == 0), stop=False)
                        pe.matmul(o, alo, hi, start=False, stop=False)
                        mm = pe.matmul(o, ahi, lo, start=False, stop=(k == KD - 1))
                        if T == NT - 1 and k % 4 == 3:
                            mm.then_inc(slot_used, 1)

            def acc_slot(L, n, ahi, alo, acc, first, last, i=0):
                wait_slot(L, n, i)
                r = L.pos[n] % RING
                if first:
                    for half in range(2):
                        for T in range(NT):
                            claim(pe, L, acc(T, half))
                for half in range(2):
                    for T in range(NT):
                        o = psum(L, acc(T, half))[:]
                        hi, lo = whi[:, r, half * 512:(half + 1) * 512], wlo[:, r, half * 512:(half + 1) * 512]
                        pe.matmul(o, ahi[:, T * P:(T + 1) * P], hi, start=first, stop=False)
                        pe.matmul(o, alo[:, T * P:(T + 1) * P], hi, start=False, stop=False)
                        mm = pe.matmul(o, ahi[:, T * P:(T + 1) * P], lo, start=False, stop=last)
                        if last and (T, half) != (NT - 1, 1):
                            full(L, acc(T, half), mm)
                mm.then_inc(slot_used, 1)

            def turn_pair(L, name, j, source):
                out = claim(pe, L, name)
                for c in range(2):
                    for T in range(NT):
                        k = 2 * j + c
                        mm = pe.transpose(out[:, c * SEQ + T * P:c * SEQ + (T + 1) * P], source[:, T, k * P:(k + 1) * P], ident)
                full(L, name, mm)

            def norm(L, w):
                if w == 1:
                    for T in range(NT):
                        pe.wait_ge(ev(f"scaled{T}"), L.each)
                for j in range(KD // 2):
                    if w != 1 and j % 2 == 0:
                        for T in range(NT):
                            updated(pe, L, w, T, j // 2)
                    turn_pair(L, ("norm", w, j), j, x if w != 1 else xs)

            def ffn(L, f):
                base = f * (FFN_SLOTS + (MIX2 if L.blk else MIX1))
                steps0 = (2 * L.deep + f) * STEPS
                accs = lambda T, half: ("acc", f, T, half)

                def gate_up(n, s, turn, i=0):
                    b, k = L.bank(("gu", f, s))
                    pe.wait_ge(bank_read[b], k + turn + 1)
                    fm_tile(L, base + n, bank[b][:, 0:SEQ], i, fresh=2 * f if n == 0 else None)
                    fm_tile(L, base + n + 1, bank[b][:, SEQ:2 * SEQ], i)

                def down(n, step, i=0, first=False, last=False):
                    pe.wait_ge(h_ready, steps0 + step + 1 + 2 * i)
                    c = (step % 2) * SEQ
                    acc_slot(L, base + n, hhi[:, c:c + SEQ], hlo[:, c:c + SEQ], accs, first, last, i)

                gate_up(0, 0, 0)
                out = claim(pe, L, ("R", f))
                pe.wait_ge(ev("diag_ready"), 2 * L.deep + f + 1)
                full(L, ("R", f), pe.matmul(out[:, 0:SEQ], ones[:], diag[:], start=True, stop=True))
                gate_up(2, 1, 0)
                down(4, 0, first=True)
                with pe.Fori(0, STEPS // 2 - 1) as i:
                    gate_up(5, 0, i + 1, i)
                    down(7, 1, i)
                    gate_up(8, 1, i + 1, i)
                    down(10, 2, i)
                down(FFN_SLOTS - 1, STEPS - 1, last=True)

            def project_out(L, first_slot):
                if L.blk:
                    wait_drained(pe, L, ("o", UNITS // 4 - 1))
                else:
                    pe.wait_ge(ev("y_ready"), L.one)
                for j in range(KD // 2):
                    turn_pair(L, ("yT", j), j, xs)
                for k in range(KD):
                    if k % 2 == 0:
                        wait_drained(pe, L, ("yT", k // 2))
                    acc_slot(L, first_slot + k, thi[:, k, :], tlo[:, k, :], lambda T, half: ("wo", T, half), k == 0, k == KD - 1)

            def attention(L, units, scores, values, probs, turned):
                for u in range(units + 2):
                    if u < units:
                        out = claim(pe, L, ("s", u))
                        scores(u, out)
                        full(L, ("s", u), pe.matmul(out[:, 2 * P:3 * P], ident, c_("negq"), start=False, stop=True))
                    if 1 <= u <= units:
                        out = claim(pe, L, ("pt", u - 1))
                        wait_drained(pe, L, ("s", u - 1))
                        pr = probs((u - 1) % 2)
                        for c in range(3):
                            mm = pe.transpose(out[:, c * P:(c + 1) * P], pr[:, c * P:(c + 1) * P], ident)
                        full(L, ("pt", u - 1), mm)
                    if u >= 2:
                        v = u - 2
                        out = claim(pe, L, ("o", v // 4)) if v % 4 == 0 else psum(L, ("o", v // 4))
                        wait_drained(pe, L, ("pt", v))
                        pt, c = turned(v % 2), (v % 4) * HD
                        pe.matmul(out[:, c:c + HD], pt[:, 0:P], values(v, 0), start=True, stop=True)
                        pe.matmul(out[:, GW + c:GW + c + HD], pt[:, P:2 * P], values(v, 0), start=True, stop=False)
                        mm = pe.matmul(out[:, GW + c:GW + c + HD], pt[:, 2 * P:3 * P], values(v, 1), start=False, stop=True)
                        if v % 4 == 3:
                            full(L, ("o", v // 4), mm)

            def first_mixer(L):
                lrT = m1("lrT", SEQ)
                for m in range(IP1):
                    out = claim(pe, L, ("ip", m))
                    n = FFN_SLOTS + 2 * m
                    if m in (ZG, GG, FQ, FK, GV, FV):
                        tm_pair(L, n, out)
                    else:
                        fm_tile(L, n, out[:, 0:SEQ], fresh=1 if m == 0 else None)
                        fm_tile(L, n + 1, out[:, SEQ:2 * SEQ])
                    if m == GK:
                        out = claim(pe, L, "gla_z")
                        wait_drained(pe, L, ("ip", ROWS))
                        pe.wait_ge(s_par, 16 * L.deep + 16)
                        for t in range(2):
                            mm = pe.matmul(out[:, t * SEQ:(t + 1) * SEQ], p1("gup")[0:16, t * P:(t + 1) * P], lrT[0:16, :],
                                           start=True, stop=True)
                        full(L, "gla_z", mm)
                xbcs = m1("xbcs", 6 * SEQ).rearrange("p (t n) -> p t n", t=6)
                out = claim(pe, L, "ssd_xs")
                for m in range(3):
                    pe.wait_ge(ev(f"xbc_act{m}"), L.one)
                for T in range(NT):
                    for t in range(2):
                        mm = pe.transpose(out[:, T * GW + t * P:T * GW + (t + 1) * P], xbcs[:, t, T * P:(T + 1) * P], ident)
                full(L, "ssd_xs", mm)
                out = claim(pe, L, "ssd_b")
                for g in range(2):
                    mm = pe.transpose(out[:, g * P:(g + 1) * P], xbcs[:, 2 + g, 0:P], ident)
                full(L, "ssd_b", mm)
                out = claim(pe, L, "rowsT")
                pe.wait_ge(ev("rowsE"), L.one)
                for c, part in enumerate(("rsp", "rE")):
                    for T in range(NT):
                        q = 2 * c + T
                        mm = pe.transpose(out[:, q * P:(q + 1) * P], m1(part, SEQ)[:, T * P:(T + 1) * P], ident)
                full(L, "rowsT", mm)
                out = claim(pe, L, "gla_kend")
                pe.wait_ge(ev("gla_dec"), L.one)
                kend = m1("kend", 512)
                for T in range(NT):
                    for t in range(2):
                        mm = pe.transpose(out[:, T * GW + t * P:T * GW + (t + 1) * P], kend[:, t * SEQ + T * P:t * SEQ + (T + 1) * P], ident)
                full(L, "gla_kend", mm)
                out = claim(pe, L, "ssd_sc")
                for T in range(NT):
                    for g in range(2):
                        c = (2 * T + g) * P
                        mm = pe.matmul(out[:, c:c + P], xbcs[:, 2 + g, T * P:(T + 1) * P], xbcs[:, 4 + g, T * P:(T + 1) * P],
                                       start=True, stop=True)
                full(L, "ssd_sc", mm)
                DL, DR = m1("DL", SEQ), m1("DR", SEQ)
                for h in range(H):
                    out = claim(pe, L, f"ssd_seg{h}")
                    for T in range(NT):
                        o, rows, tok = out[:, T * P:(T + 1) * P], slice(32 * h, 32 * h + 4), slice(T * P, (T + 1) * P)
                        pe.matmul(o, ident, c_("negT"), start=True, stop=False)
                        mm = pe.matmul(o, DL[rows, tok], DR[rows, tok], start=False, stop=True)
                    full(L, f"ssd_seg{h}", mm)
                gq, gk = m1("gq", 512), m1("gk", 512)
                claim(pe, L, "gla_kv")
                wait_drained(pe, L, "gla_kend")
                wait_drained(pe, L, ("ip", GV))
                for hh in range(2):
                    out = claim(pe, L, f"gla_att{hh}")
                    rows = slice(HD * hh, HD * hh + HD)
                    for T in range(NT):
                        for t in range(2):
                            c, tok = (2 * T + t) * P, slice(t * SEQ + T * P, t * SEQ + (T + 1) * P)
                            mm = pe.matmul(out[:, c:c + P], gk[rows, tok], gq[rows, tok], start=True, stop=True)
                    full(L, f"gla_att{hh}", mm)
                out = psum(L, "gla_kv")
                kendT = m1("kendT", 768).rearrange("p (c n) -> p c n", c=3)
                av, avs = m1("av", 512), m1("avs", 256)
                chunk_v = [av[0:HD, 0:GW], avs[0:HD, :], av[0:HD, GW:2 * GW]]
                for c in range(3):
                    for h in range(H):
                        o = out[HD * (h % 2):HD * (h % 2) + HD, c * P + (h // 2) * HD:c * P + (h // 2) * HD + HD]
                        mm = pe.matmul(o, kendT[0:HD, c, h * HD:(h + 1) * HD], chunk_v[c][:, h * HD:(h + 1) * HD], start=True, stop=True)
                full(L, "gla_kv", mm)
                fqk = m1("fqk", 1024).rearrange("p (c t n) -> p c t n", c=2, t=NT)
                pe.wait_ge(ev("fqk_ready"), L.one)
                for c, name in enumerate(("fox_q", "fox_k")):
                    out = claim(pe, L, name)
                    for T in range(NT):
                        for t in range(2):
                            mm = pe.transpose(out[:, t * SEQ + T * P:t * SEQ + (T + 1) * P], fqk[:, c, T, t * P:(t + 1) * P], ident)
                    full(L, name, mm)
                out = claim(pe, L, "ssd_st")
                wait_drained(pe, L, "ssd_b")
                pe.wait_ge(ev("xd_ready"), L.one)
                for g in range(2):
                    mm = pe.matmul(out[:, g * P:(g + 1) * P], m1("Bt", 256)[:, g * P:(g + 1) * P], m1("xdd", 256)[:, g * P:(g + 1) * P],
                                   start=True, stop=True)
                full(L, "ssd_st", mm)
                out = claim(pe, L, "ssd_y")
                wait_drained(pe, L, "ssd_sc")
                Mt, xd = m1("Mt", 1024), m1("xd", 512)
                for T in range(NT):
                    for h in range(H):
                        c = T * GW + h * HD
                        mm = pe.matmul(out[:, c:c + HD], Mt[:, T * 512 + h * P:T * 512 + (h + 1) * P], xd[:, c:c + HD], start=True, stop=True)
                full(L, "ssd_y", mm)
                out = claim(pe, L, "ssd_yoff")
                wait_drained(pe, L, "ssd_st")
                for g in range(2):
                    mm = pe.matmul(out[:, g * P:(g + 1) * P], xbcs[:, 4 + g, P:2 * P], m1("St", 256)[:, g * P:(g + 1) * P], start=True, stop=True)
                full(L, "ssd_yoff", mm)
                out = claim(pe, L, "gla_o")
                for hh in range(2):
                    wait_drained(pe, L, f"gla_att{hh}")
                pe.wait_ge(ev("gla_states"), L.one)
                attT, Sbd = m1("attT", 1024), m1("Sbd", 768)
                for T in range(NT):
                    for h in range(H):
                        hh, t = h % 2, h // 2
                        c, a = T * GW + h * HD, hh * 512 + (2 * T + t) * P
                        pe.matmul(out[:, c:c + HD], attT[:, a:a + P], av[:, c:c + HD], start=(T == 0 and h == 0), stop=False,
                                  skip_group_check=True)
                    for t in range(2):
                        for half in range(2):
                            chunk = 2 * T + half
                            if chunk:
                                c, tok, s = T * GW + t * P, t * SEQ + chunk * HD, ((chunk - 1) * 2 + t) * P
                                mm = pe.matmul(out[HD * half:HD * half + HD, c:c + P], gq[:, tok:tok + HD], Sbd[:, s:s + P],
                                               start=False, stop=(half == 1), skip_group_check=True)
                full(L, "gla_o", mm)
                out = claim(pe, L, "sc_t")
                pe.wait_ge(ev("dy_ready"), L.one)
                dy = m1("dy", 512)
                for T in range(NT):
                    for t in range(2):
                        mm = pe.transpose(out[:, T * GW + t * P:T * GW + (t + 1) * P], dy[:, t * SEQ + T * P:t * SEQ + (T + 1) * P], ident)
                full(L, "sc_t", mm)

                fT = m1("fT", 1024).rearrange("p (c t n) -> p c t n", c=2, t=2)
                FL, FR, bv = m1("FL", 4 * SEQ), m1("FR", SEQ), m1("bv", 512)

                def scores(u, out):
                    rows, t, f = slice(HD * (u % 2), HD * (u % 2) + HD), u // 2, u * SEQ
                    pe.matmul(out[:, 0:P], fT[rows, 0, t, 0:P], fT[rows, 1, t, 0:P], start=True, stop=False)
                    pe.matmul(out[:, 0:P], ident, c_("negq"), start=False, stop=False)
                    pe.matmul(out[:, 0:P], FL[:, f:f + P], FR[:, 0:P], start=False, stop=True)
                    pe.matmul(out[:, P:3 * P], fT[rows, 0, t, P:2 * P], fT[rows, 1, t, :], start=True, stop=False)
                    pe.matmul(out[:, P:3 * P], FL[:, f + P:f + 2 * P], FR[:], start=False, stop=False)

                wait_drained(pe, L, "fox_q")
                wait_drained(pe, L, "fox_k")
                pe.wait_ge(ev("FL_ready"), L.one)
                wait_drained(pe, L, ("ip", FV))
                attention(L, H, scores, lambda u, T: bv[:, T * GW + u * HD:T * GW + (u + 1) * HD],
                          lambda s: m1("P", 768)[:, s * 384:(s + 1) * 384], lambda s: m1("pt", 768)[:, s * 384:(s + 1) * 384])
                project_out(L, FFN_SLOTS + 2 * IP1)

            def second_mixer(L):
                def rotate(m):
                    out = claim(pe, L, ("rot", m))
                    wait_drained(pe, L, ("ip", m))
                    full(L, ("rot", m), pe.matmul(out[:], c_("ropeR"), raw_of(m), start=True, stop=True))

                for m in range(IP2 + 1):
                    out = claim(pe, L, ("ip", m))
                    n = FFN_SLOTS + 2 * m
                    if m in (VSW, MV0, MV1):
                        tm_pair(L, n, out)
                    elif m == GATES:
                        fm_tile(L, n, out[:, 0:SEQ])
                    else:
                        fm_tile(L, n, out[:, 0:SEQ], fresh=1 if m == 0 else None)
                        fm_tile(L, n + 1, out[:, SEQ:2 * SEQ])
                    if m - 1 in ROPED:
                        rotate(m - 1)
                for c in range(2):
                    out = claim(pe, L, ("hid", c))[0:2 * NCMP, 0:256]
                    pe.wait_ge(ev(f"blk_ready{c}"), L.one)
                    for s in range(CMP_SLOTS):
                        n = FFN_SLOTS + 2 * IP2 + 1 + c * CMP_SLOTS + s
                        wait_slot(L, n)
                        r = L.pos[n] % RING
                        for k in range(NCT // CMP_SLOTS):
                            step = s * (NCT // CMP_SLOTS) + k
                            hi, lo = whi[:, r, k * 256:(k + 1) * 256], wlo[:, r, k * 256:(k + 1) * 256]
                            block = slice((c * NCT + step) * 2 * NCMP, (c * NCT + step + 1) * 2 * NCMP)
                            pe.matmul(out, hhi[:, block], hi, start=(step == 0), stop=False)
                            pe.matmul(out, hlo[:, block], hi, start=False, stop=False)
                            mm = pe.matmul(out, hhi[:, block], lo, start=False, stop=(step == NCT - 1))
                        mm.then_inc(slot_used, 1)
                out = claim(pe, L, "hidf")
                wait_drained(pe, L, ("ip", GATES))
                for T in range(NT):
                    pe.matmul(out[:, 128 + T * 32:160 + T * 32], m2("gex", SEQ)[0:HD, T * P:(T + 1) * P], ident[0:HD, 0:32], start=True, stop=True)
                for c in range(2):
                    wait_drained(pe, L, ("hid", c))
                    for t in range(2):
                        col = (2 * c + t) * 32
                        mm = pe.matmul(out[:, col:col + 32], m2("hidT", 512)[0:HD, c * 256 + t * P:c * 256 + (t + 1) * P], ident[0:HD, 0:32],
                                       start=True, stop=True)
                full(L, "hidf", mm)
                pe.wait_ge(s_par, 16 * L.deep + 16)
                out = claim(pe, L, "kc")
                pe.wait_ge(ev("gelu0"), L.one)
                for t in range(2):
                    mm = pe.matmul(out[:, 0:2 * NCMP], p2("ck2")[:, t * P:(t + 1) * P], m2("hk", 64)[:, t * 32:t * 32 + 2 * NCMP],
                                   start=(t == 0), stop=(t == 1))
                full(L, "kc", mm)
                out = claim(pe, L, "vc")
                pe.wait_ge(ev("gelu1"), L.one)
                for t in range(2):
                    mm = pe.matmul(out[:, 0:HD], m2("hvr", 256)[:, t * P:(t + 1) * P], p2("cv2")[:, t * HD:(t + 1) * HD],
                                   start=(t == 0), stop=(t == 1))
                full(L, "vc", mm)
                out = claim(pe, L, "cmp_s")
                wait_drained(pe, L, "kc")
                qraw = m2("qraw", 1024)
                pe.matmul(out[:, 0:256], ident, c_("cmpmask"), start=True, stop=False, skip_group_check=True)
                for T in range(NT):
                    for r in range(4):
                        c = (T * 4 + r) * 32
                        mm = pe.matmul(out[:, c:c + 32], qraw[:, r * SEQ + T * P:r * SEQ + (T + 1) * P], m2("kc", 32),
                                       start=False, stop=(T == 1 and r == 3), skip_group_check=True)
                full(L, "cmp_s", mm)
                out = claim(pe, L, "cmp_pt")
                pe.wait_ge(ev("cmp_exp"), L.one)
                for T in range(NT):
                    mm = pe.transpose(out[:, T * P:(T + 1) * P], m2("cs", 256)[:, T * P:(T + 1) * P], ident)
                full(L, "cmp_pt", mm)
                wait_drained(pe, L, "vc")
                wait_drained(pe, L, "cmp_pt")
                for T in range(NT):
                    out = claim(pe, L, f"cmp_o{T}")
                    full(L, f"cmp_o{T}", pe.matmul(out[:], m2("cpT", 256)[:, T * P:(T + 1) * P], m2("vcd", 512), start=True, stop=True))

                kr, qr, mqr, mkr = m2("kr", 512), m2("qr", 1024), m2("mqr", 1024), m2("mkr", 1024)
                vsw, mv = m2("vsw", 512), m2("mv", 1024)

                def scores(u, out):
                    kind, h = u // 8, u % 8
                    if kind < 2:
                        rows, q, k = slice(HD * (h // 4), HD * (h // 4) + HD), qr[:, (h % 4) * SEQ:(h % 4 + 1) * SEQ], kr[:, kind * SEQ:(kind + 1) * SEQ]
                    else:
                        rows, t = slice(HD * (h % 2), HD * (h % 2) + HD), h // 2
                        q, k = mqr[:, t * SEQ:(t + 1) * SEQ], mkr[:, t * SEQ:(t + 1) * SEQ]
                    pe.matmul(out[:, 0:P], q[rows, 0:P], k[rows, 0:P], start=True, stop=False)
                    pe.matmul(out[:, 0:P], ident, c_("negq"), start=False, stop=True)
                    pe.matmul(out[:, P:3 * P], q[rows, P:2 * P], k[rows, :], start=True, stop=False)

                def values(u, T):
                    kind, h = u // 8, u % 8
                    if kind < 2:
                        c = T * GW + kind * P + (h // 4) * HD
                        return vsw[:, c:c + HD]
                    return mv[:, (h // 4) * 512 + T * GW + (h % 4) * HD:(h // 4) * 512 + T * GW + (h % 4 + 1) * HD]

                pe.wait_ge(ev("roped"), L.one)
                wait_drained(pe, L, ("ip", MV1))
                attention(L, UNITS, scores, values, lambda s: m2("P", 768)[:, s * 384:(s + 1) * 384],
                          lambda s: m2("pt", 768)[:, s * 384:(s + 1) * 384])
                project_out(L, FFN_SLOTS + 2 * IP2 + 1 + 2 * CMP_SLOTS)

            pe.sem_inc(slot_used, RING)
            pe.wait_ge(s_con, 16)
            pe.wait_ge(s_x, 16)
            pe.wait_ge(ones_set, 1)
            for blk, mixer in enumerate((first_mixer, second_mixer)):
                with pe.Fori(0, DEPTH) as l:
                    L = Layer(l, blk)
                    norm(L, 0)
                    ffn(L, 0)
                    norm(L, 1)
                    mixer(L)
                    norm(L, 2)
                    ffn(L, 1)

        @block.scalar
        def _(act):
            def split_hi(L, n, i=0):
                place, uses = L.raw_use(n)
                act.wait_ge(s_raw[place], 16 * uses + 16 * i + 16)
                act.wait_ge(slot_used, L.slot0 + (L.before(n) + 1 + RING) + RING * i)
                nc.scalar.copy(whi[:, place, :], raw[:, place, :]).then_inc(hi_done, 1)

            def squares(L, w, half):
                for T in range(NT):
                    updated(act, L, w, T, half)
                    h = slice(half * 512, half * 512 + 512)
                    c = P + NT * half + T
                    nc.scalar.activation(xs[:, T, h], x[:, T, h], ACT.Square, accum_out=stat[:, c:c + 1]).then_inc(sq_done, 1)

            def norm(L, w):
                act.wait_ge(s_gain, 16 * L.deep + 16)
                squares(L, w, 0)
                if w == 1:
                    squares(L, w, 1)
                    for n in range(FFN_SLOTS, FFN_SLOTS + AHEAD):
                        split_hi(L, n)
                    act.wait_ge(ev("root_ready"), L.each)
                    nc.scalar.activation(xs[:, 1, :], x[:, 1, :], ACT.Copy, scale=stat[:, 33:34]).then_inc(ev("scaled1"), 1)
                for j in range(KD // 2):
                    wait_full(act, L, ("norm", w, j))
                    for c in range(2):
                        k = 2 * j + c
                        nc.scalar.activation(thi[:, k, :], psum(L, ("norm", w, j))[:, c * SEQ:(c + 1) * SEQ], ACT.Copy,
                                             scale=gain_of(L, w, k)).then_inc(thi_done, 1)
                if w != 1:
                    squares(L, w, 1)
                    split_hi(L, ffn_slot(L, w))

            def ffn(L, f):
                base = f * (FFN_SLOTS + (MIX2 if L.blk else MIX1))
                steps0 = (2 * L.deep + f) * STEPS
                nc.scalar.preload_act_table_set("silu_and_others")

                def step(s, j, turn, between, behind, i=0):
                    c = s * SEQ
                    b, k = L.bank(("gu", f, s))
                    act.wait_ge(bank_read[b], k + turn + 2)
                    nc.scalar.activation(gu[:, s, 0, :], gu[:, s, 0, :], ACT.Silu).then_inc(sg_done, 1)
                    for n in between:
                        split_hi(L, base + n, i)
                    act.wait_ge(hf_done, steps0 + (j + 1) + 2 * i)
                    nc.scalar.copy(hhi[:, c:c + SEQ], gu[:, s, 1, :]).then_inc(hhi_done, 1)
                    for n in behind:
                        split_hi(L, base + n, i)

                wait_full(act, L, ("R", f))
                drained(L, ("R", f), nc.scalar.copy(root[:], psum(L, ("R", f))[:, 0:SEQ]))
                step(0, 0, 0, (), (5, 6))
                step(1, 1, 0, (7,), (8, 9))
                with act.Fori(0, STEPS // 2 - 2) as i:
                    step(0, 2, i + 1, (10,), (11, 12), i)
                    step(1, 3, i + 1, (13,), (14, 15), i)
                n = FFN_SLOTS
                step(0, STEPS - 2, STEPS // 2 - 1, (n - 2,), (n - 1, n) if f else (n - 1,))
                step(1, STEPS - 1, STEPS // 2 - 1, (), (n + 1, n + 2, n + 3) if f else ())

            def exps(L, u, scale, rows, units, probs, per_layer, nm):
                s = u % 2
                act.wait_ge(sm_max, L.blk * DEPTH * H + L.l * per_layer + (u + 1))
                S, pr = psum(L, ("s", u)), probs[:, s * 384:(s + 1) * 384]
                nc.scalar.activation(pr[:, 0:P], S[:, 0:P], ACT.Exp, scale=scale, bias=nm[:, 2 * s:2 * s + 1], accum_out=rows[:, u:u + 1])
                drained(L, ("s", u), nc.scalar.activation(pr[:, P:3 * P], S[:, P:3 * P], ACT.Exp, scale=scale,
                                                          bias=nm[:, 2 * s + 1:2 * s + 2], accum_out=rows[:, units + u:units + u + 1]))

            def first_mixer(L, own):
                xbcu = m1("xbcu", 6 * 260).rearrange("p (t n) -> p t n", t=6)
                xbcs = m1("xbcs", 6 * SEQ).rearrange("p (t n) -> p t n", t=6)
                keep = {GQ: m1("gq", 512), GK: m1("gk", 512), FQ: m1("fqk", 1024)[:, 0:512], FK: m1("fqk", 1024)[:, 512:1024],
                        GV: m1("av", 512), FV: m1("bv", 512), DC: m1("dc", 512), DB: m1("db", 512)}
                act.wait_ge(s_par, 16 * L.deep + 16)
                for m in range(IP1):
                    out = psum(L, ("ip", m))
                    if m not in (ROWS, DV):
                        wait_full(act, L, ("ip", m))
                    if m <= XBC2:
                        drained(L, ("ip", m), nc.scalar.copy(xbcu[:, 2 * m:2 * m + 2, 3:3 + SEQ], out[:].rearrange("p (t n) -> p t n", t=2)))
                    elif m in (ZG, GG):
                        drained(L, ("ip", m), nc.scalar.activation(m1("siluz" if m == ZG else "silug", 512), out[:], ACT.Silu))
                    elif m in keep:
                        if m == GV:
                            nc.scalar.copy(m1("avs", 256)[0:HD, :], out[HD:2 * HD, 0:GW])
                        drained(L, ("ip", m), nc.scalar.copy(keep[m], out[:]))
                    for n in (2 * m + 4, 2 * m + 5):
                        split_hi(L, FFN_SLOTS + n)
                    if 1 <= m <= 3:
                        act.wait_ge(ev(f"conv{m - 1}"), L.one)
                        for t in (2 * m - 2, 2 * m - 1):
                            ins = nc.scalar.activation(xbcs[:, t, :], xbcs[:, t, :], ACT.Silu, bias=p1("convb")[:, t:t + 1])
                        ins.then_inc(ev(f"xbc_act{m - 1}"), 1)
                    if m == GG:
                        nc.scalar.preload_act_table_set("natural_log_exp_and_others")
                    if m == ROWS:
                        act.wait_ge(ev("rows_na"), L.one)
                        nc.scalar.activation(m1("ralogx", 1), p1("ralog"), ACT.Exp)
                        nc.scalar.activation(m1("re", SEQ), m1("re", SEQ), ACT.Exp).then_inc(ev("rows_e"), 1)
                    if m == FK:
                        act.wait_ge(ev("rows_cs"), L.one)
                        rcs, rE = m1("rcs", SEQ), m1("rE", SEQ)
                        nc.scalar.activation(rE[:, 0:P], rcs[:, 0:P], ACT.Exp, scale=-1.0, bias=rcs[:, P - 1:P])
                        nc.scalar.activation(rE[:, P:2 * P], rcs[:, P:2 * P], ACT.Exp).then_inc(ev("rowsE"), 1)
                    if m == FQ:
                        act.wait_ge(ev("z_na"), L.one)
                        ge = m1("ge", 512)
                        own.link(nc.scalar.activation(ge, ge, ACT.Exp))
                        nc.scalar.activation(ge, ge, ACT.Ln, bias=1.0).then_inc(ev("z_l"), 1)
                    if m == FK:
                        act.wait_ge(ev("gla_b"), L.one)
                        gb, gd = m1("gb", 512), m1("gd", 512)
                        nc.scalar.activation(m1("eb", 512), gb, ACT.Exp, scale=1.0 / 16)
                        nc.scalar.activation(m1("enb", 512), gb, ACT.Exp, scale=-1.0 / 16)
                        nc.scalar.activation(gd, gd, ACT.Exp, scale=1.0 / 16).then_inc(ev("gla_exp"), 1)

                def take(name, dst, src, func=None):
                    wait_full(act, L, name)
                    drained(L, name, nc.scalar.activation(dst, src, func) if func else nc.scalar.copy(dst, src))

                take("ssd_b", m1("Bt", 256), psum(L, "ssd_b")[:, 0:256])
                kend, kendT = psum(L, "gla_kend"), m1("kendT", 768).rearrange("p (c n) -> p c n", c=3)
                wait_full(act, L, "gla_kend")
                for c in range(2):
                    nc.scalar.copy(kendT[0:HD, c, :], kend[HD * c:HD * c + HD, 0:GW])
                drained(L, "gla_kend", nc.scalar.copy(kendT[0:HD, 2, :], kend[0:HD, GW:2 * GW]))
                for h in range(H):
                    take(f"ssd_seg{h}", m1("Lm", 1024).rearrange("p (t h n) -> p t h n", t=NT, h=H)[:, :, h, :],
                         psum(L, f"ssd_seg{h}")[:, 0:2 * P].rearrange("p (t n) -> p t n", t=NT), ACT.Exp)
                take("fox_q", m1("fT", 1024)[:, 0:512], psum(L, "fox_q")[:])
                take("fox_k", m1("fT", 1024)[:, 512:1024], psum(L, "fox_k")[:])
                take("ssd_st", m1("St", 256), psum(L, "ssd_st")[:, 0:256])
                for name, c in (("gla_o", 0), ("sc_t", 3 * GW)):
                    take(name, xs[:, :, c:c + GW], psum(L, name)[:].rearrange("p (t n) -> p t n", t=NT))
                for u in range(H):
                    exps(L, u, 1.0, m1("rowsum", 8), H, m1("P", 768), H, m1("nm", 4))
                finish(L, FFN_SLOTS + MIX1)

            def finish(L, end):
                for j in range(KD // 2):
                    wait_full(act, L, ("yT", j))
                    nc.scalar.copy(thi[:, 2 * j:2 * j + 2, :], psum(L, ("yT", j))[:].rearrange("p (k n) -> p k n", k=2)).then_inc(thi_done, 1)
                for n in range(end - 4, end + AHEAD):
                    split_hi(L, n)

            def second_mixer(L, own):
                nc.scalar.preload_act_table_set("exp_and_others")
                kx = m2("kx", 1024).rearrange("p (c g n) -> p c g n", c=2, g=2)
                keep = {VSW: m2("vsw", 512), MV0: m2("mv", 1024)[:, 0:512], MV1: m2("mv", 1024)[:, 512:1024]}
                for m in range(IP2 + 1):
                    out = psum(L, ("ip", m))
                    wait_full(act, L, ("ip", m))
                    if m == KVC:
                        src = out[:].rearrange("p (c n) -> p c n", c=2)
                        for g in range(2):
                            nc.scalar.copy(kx[0:HD, :, g, :], src[HD * g:HD * g + HD, :, :])
                            ins = nc.scalar.copy(kx[HD:P, :, g, 0:SEQ - 1], src[HD * g:HD * g + HD, :, 1:SEQ])
                        drained(L, ("ip", m), ins)
                    elif m in ROPED:
                        if m in (MQ1, MK0, MK1):
                            wait_drained(act, L, ("rot", {MQ1: KSW, MK0: MQ0, MK1: MQ1}[m]))
                        drained(L, ("ip", m), nc.scalar.copy(raw_of(m), out[:]))
                    elif m == GATES:
                        drained(L, ("ip", m), nc.scalar.activation(m2("gex", SEQ)[0:HD, :], out[0:HD, 0:SEQ], ACT.Exp, scale=-1.0))
                    else:
                        drained(L, ("ip", m), nc.scalar.copy(keep[m], out[:]))
                    for n in (2 * m + 4, 2 * m + 5) if m != GATES else (2 * m + 4,):
                        split_hi(L, FFN_SLOTS + n)
                for c in range(2):
                    act.wait_ge(ev(f"blk{c}"), L.one)
                    nc.scalar.copy(hhi[:, c * 480:(c + 1) * 480], m2("blk", 960)[:, c * 480:(c + 1) * 480]).then_inc(ev(f"blk_hi{c}"), 1)
                first = FFN_SLOTS + 2 * IP2 + 1
                for n in range(first + AHEAD, first + 2 * CMP_SLOTS):
                    split_hi(L, n)
                for n in range(first + 2 * CMP_SLOTS, first + 2 * CMP_SLOTS + AHEAD):
                    split_hi(L, n)
                act.wait_ge(ev("gelu_in"), L.one)
                nc.scalar.activation(m2("he", 128), m2("hu", 128), ACT.Exp, scale=-2.0 * (2.0 / np.pi) ** 0.5).then_inc(ev("gelu_e"), 1)
                wait_drained(act, L, "cmp_s")
                nc.scalar.activation(m2("cs", 256), m2("cs", 256), ACT.Exp, scale=SCALE).then_inc(ev("cmp_exp"), 1)
                wait_full(act, L, "cmp_pt")
                drained(L, "cmp_pt", nc.scalar.copy(m2("cpT", 256), psum(L, "cmp_pt")[:, 0:256]))
                for u in range(UNITS):
                    exps(L, u, SCALE, m2("rowsum", 2 * UNITS), UNITS, m2("P", 768), UNITS, m2("nm", 4))
                finish(L, FFN_SLOTS + MIX2)

            act.wait_ge(s_x, 16)
            for n in range(AHEAD):
                split_hi(Layer(0, 0), n)
            for blk, mixer in enumerate((first_mixer, second_mixer)):
                with act.Fori(0, DEPTH) as l:
                    L = Layer(l, blk)
                    own = Own(act, act_own, L)
                    norm(L, 0)
                    ffn(L, 0)
                    norm(L, 1)
                    mixer(L, own)
                    norm(L, 2)
                    ffn(L, 1)
                    own.close()
            for half in range(2):
                squares(Layer(DEPTH, 1), 0, half)

        @block.vector
        def _(dve):
            def split_lo(L, n, i=0):
                place, _ = L.raw_use(n)
                dve.wait_ge(hi_done, L.slot0 + (n + 1) + RING * i)
                dve.tensor_tensor(wlo[:, place, :], raw[:, place, :], whi[:, place, :].bitcast(F32), ALU.subtract).then_inc(split_done, 1)

            def inverse_root(own, sums, n, count, ready=None):
                v, y, t, vh = (stat[:, 32 * i:32 * i + n] for i in range(4))
                own.link(dve.tensor_scalar(v, sums, 1.0 / count, EPS, ALU.mult, ALU.add))
                own.step(dve.tensor_scalar(vh, v, -0.5, None, ALU.mult))
                own.link(dve.tensor_scalar(t.bitcast(I32), v.bitcast(I32), 1, None, ALU.logical_shift_right))
                own.link(dve.tensor_scalar(y.bitcast(I32), t.bitcast(I32), -1.0, float(0x5f3759df), ALU.mult, ALU.add))
                for step in range(3):
                    own.link(dve.tensor_tensor(t, y, y, ALU.mult))
                    own.link(dve.tensor_tensor(t, t, vh, ALU.mult))
                    ins = dve.scalar_tensor_tensor(y, t, 1.5, y, ALU.add, ALU.mult)
                    if step == 2 and ready is not None:
                        ins.then_inc(ready, 1)
                        dve.wait_ge(ready, own.L.each)
                    else:
                        own.link(ins)
                return y

            def roots(L, own, w, ready=None):
                dve.wait_ge(sq_done, L.deep * (6 * NT) + (w + 1) * 2 * NT)
                sums = stat[:, P:P + NT]
                own.link(dve.tensor_tensor(sums, sums, stat[:, P + NT:P + 2 * NT], ALU.add))
                return inverse_root(own, sums, NT, D, ready)

            def remainders(L, w):
                for j in range(KD // 2):
                    dve.wait_ge(thi_done, 28 * L.deep + ((0, 8, 20)[w] + 2 * j + 2))
                    for c in range(2):
                        k = 2 * j + c
                        ins = dve.scalar_tensor_tensor(tlo[:, k, :], psum(L, ("norm", w, j))[:, c * SEQ:(c + 1) * SEQ], gain_of(L, w, k),
                                                       thi[:, k, :].bitcast(F32), ALU.mult, ALU.subtract)
                    drained(L, ("norm", w, j), ins)

            def norm(L, own, w):
                if w == 1:
                    rstd = roots(L, own, w, ev("root_ready"))
                    dve.tensor_scalar(xs[:, 0, :], x[:, 0, :], rstd[:, 0:1], None, ALU.mult).then_inc(ev("scaled0"), 1)
                    split_lo(L, FFN_SLOTS)
                    remainders(L, w)
                    for n in range(FFN_SLOTS + 1, FFN_SLOTS + AHEAD):
                        split_lo(L, n)
                else:
                    remainders(L, w)
                    rstd = roots(L, own, w)
                    for T in range(NT):
                        ins = dve.tensor_scalar(diag[:, T * P:(T + 1) * P], ident, rstd[:, T:T + 1], None, ALU.mult)
                    ins.then_inc(ev("diag_ready"), 1)
                    split_lo(L, ffn_slot(L, w))

            def add_to_x(L, name, factor):
                for half in range(2):
                    for T in range(NT):
                        wait_full(dve, L, name(T, half))
                        part = x[:, T, half * 512:(half + 1) * 512]
                        drained(L, name(T, half), dve.scalar_tensor_tensor(part, psum(L, name(T, half))[:], factor, part, ALU.mult, ALU.add))

            def ffn(L, f):
                base = f * (FFN_SLOTS + (MIX2 if L.blk else MIX1))
                steps0 = (2 * L.deep + f) * STEPS

                def step(s, j, up, between, behind, i=0):
                    c = s * SEQ
                    b = L.bank(("gu", f, s))[0]
                    dve.wait_ge(slot_used, L.slot0 + (base + up + 1 + RING) + RING * i)
                    dve.tensor_tensor(gu[:, s], bank[b][:].rearrange("p (c n) -> p c n", c=2), root[:].unsqueeze(1).to_broadcast([P, 2, SEQ]),
                                      ALU.mult).then_inc(bank_read[b], 1)
                    for n in between:
                        split_lo(L, base + n, i)
                    dve.wait_ge(sg_done, steps0 + (j + 1) + 2 * i)
                    dve.tensor_tensor(gu[:, s, 1, :], gu[:, s, 0, :], gu[:, s, 1, :], ALU.mult).then_inc(hf_done, 1)
                    dve.wait_ge(hhi_done, steps0 + (j + 1) + 2 * i)
                    dve.tensor_tensor(hlo[:, c:c + SEQ], gu[:, s, 1, :], hhi[:, c:c + SEQ].bitcast(F32), ALU.subtract).then_inc(h_ready, 1)
                    for n in behind:
                        split_lo(L, base + n, i)

                wait_drained(dve, L, ("R", f))
                step(0, 0, 1, (), (5, 6))
                step(1, 1, 3, (7,), (8, 9))
                with dve.Fori(0, STEPS // 2 - 2) as i:
                    step(0, 2, 6, (10,), (11, 12), i)
                    step(1, 3, 9, (13,), (14, 15), i)
                n = FFN_SLOTS
                step(0, STEPS - 2, n - 6, (n - 2,), (n - 1, n) if f else (n - 1,))
                step(1, STEPS - 1, n - 3, (), (n + 1, n + 2, n + 3) if f else ())
                add_to_x(L, lambda T, half: ("acc", f, T, half), 0.5)

            def maxima(L, own, u, scale, mx, nm):
                s = u % 2
                wait_full(dve, L, ("s", u))
                S = psum(L, ("s", u))
                own.step(dve.tensor_reduce(mx[:, 2 * s:2 * s + 1], S[:, 0:P], AX, ALU.max))
                own.link(dve.tensor_reduce(mx[:, 2 * s + 1:2 * s + 2], S[:, P:3 * P], AX, ALU.max))
                dve.tensor_scalar(nm[:, 2 * s:2 * s + 2], mx[:, 2 * s:2 * s + 2], -scale, None, ALU.mult).then_inc(sm_max, 1)

            def keep_turned(L, u, pt):
                wait_full(dve, L, ("pt", u))
                s = u % 2
                drained(L, ("pt", u), dve.tensor_copy(pt[:, s * 384:(s + 1) * 384], psum(L, ("pt", u))[:, 0:384]))

            def finish(L, end):
                for j in range(KD // 2):
                    pair = slice(2 * j, 2 * j + 2)
                    dve.wait_ge(thi_done, 28 * L.deep + (16 + j + 1))
                    drained(L, ("yT", j), dve.tensor_tensor(tlo[:, pair, :], psum(L, ("yT", j))[:].rearrange("p (k n) -> p k n", k=2),
                                                            thi[:, pair, :].bitcast(F32), ALU.subtract))
                for n in range(end - 4, end + AHEAD):
                    split_lo(L, n)
                add_to_x(L, lambda T, half: ("wo", T, half), 1.0)

            def bc(ap, shape):
                return ap.to_broadcast(shape)

            def convolve(own, dst, src, weights, taps):
                for k in range(taps):
                    for t, d in enumerate(dst):
                        s, w = src[t][:, k:k + SEQ], weights[:, t * taps + k:t * taps + k + 1]
                        if k == 0:
                            ins = dve.tensor_scalar(d, s, w, None, ALU.mult)
                        else:
                            ins = dve.scalar_tensor_tensor(d, s, w, d, ALU.mult, ALU.add)
                        if k < taps - 1:
                            own.step(ins)
                    if k < taps - 1:
                        own.wait()
                return ins

            def first_mixer(L, own):
                xbcu = m1("xbcu", 6 * 260).rearrange("p (t n) -> p t n", t=6)
                xbcs = m1("xbcs", 6 * SEQ).rearrange("p (t n) -> p t n", t=6)
                dcu = m1("dcu", 520).rearrange("p (t n) -> p t n", t=2)
                sel = c_("sel")
                zb, ge, gb, gd = m1("zb", 512), m1("ge", 512), m1("gb", 512), m1("gd", 512)
                gq, gk = m1("gq", 512), m1("gk", 512)
                ru, re, rs, rs2, rp, rsp, rcs = (m1(n, SEQ) for n in ("ru", "re", "rs", "rs2", "rp", "rsp", "rcs"))
                rows_bank = psum(L, ("ip", ROWS))
                own.link(dve.memset(xbcu[:, :, 0:3], 0.0))
                dve.wait_ge(s_par, 16 * L.deep + 16)
                for m in range(IP1):
                    if m == ROWS:
                        wait_full(dve, L, ("ip", ROWS))
                        dve.tensor_copy(m1("lrT", SEQ)[0:16, :], rows_bank[0:16, 0:SEQ])
                        drained(L, ("ip", ROWS), dve.tensor_scalar(ru, rows_bank[:, SEQ:2 * SEQ], p1("rbias"), sel[:, 0:1], ALU.add, ALU.mult))
                    if m == DV:
                        own.link(dve.memset(dcu[:, :, 0:2], 0.0))
                        wait_full(dve, L, ("ip", DV))
                        wait_drained(dve, L, ("ip", DC))
                        drained(L, ("ip", DV), dve.tensor_tensor(dcu[:, :, 2:2 + SEQ], m1("dc", 512).rearrange("p (t n) -> p t n", t=2),
                                                                 psum(L, ("ip", DV))[:].rearrange("p (t n) -> p t n", t=2), ALU.mult))
                    for n in (2 * m + 4, 2 * m + 5):
                        split_lo(L, FFN_SLOTS + n)
                    if m <= XBC2:
                        wait_drained(dve, L, ("ip", m))
                        tiles = (2 * m, 2 * m + 1)
                        convolve(own, [xbcs[:, t, :] for t in tiles], [xbcu[:, t, :] for t in tiles],
                                 p1("convw")[:, 8 * m:8 * m + 8], 4).then_inc(ev(f"conv{m}"), 1)
                    if m == ROWS:
                        wait_drained(dve, L, ("ip", ROWS))
                        dve.scalar_tensor_tensor(re, ru, -1.0, ru, ALU.mult, ALU.min).then_inc(ev("rows_na"), 1)
                    if m == GQ:
                        dve.wait_ge(ev("rows_e"), L.one)
                        own.link(dve.tensor_scalar(rs, re, 2.0, None, ALU.add))
                        own.link(dve.reciprocal(rs, rs))
                        own.link(dve.tensor_tensor(rs, rs, re, ALU.mult))
                        own.link(dve.tensor_tensor(rs2, rs, rs, ALU.mult))
                        own.link(dve.tensor_scalar(rp, rs2, 1.0 / 17, None, ALU.mult))
                    if m == GK:
                        for odd in (15, 13, 11, 9, 7, 5, 3):
                            own.link(dve.scalar_tensor_tensor(rp, rp, 1.0 / odd, rs2, ALU.add, ALU.mult))
                        own.link(dve.scalar_tensor_tensor(rp, rp, 1.0, rs, ALU.add, ALU.mult))
                    if m == FQ:
                        own.step(dve.tensor_scalar(ru, ru, 0.0, None, ALU.max))
                        own.link(dve.tensor_scalar(rp, rp, 2.0, None, ALU.mult))
                        own.link(dve.tensor_tensor(rsp, rp, ru, ALU.add))
                        own.link(dve.tensor_scalar(rp, rsp, m1("ralogx", 1), -1.0, ALU.mult, ALU.mult))
                        own.link(dve.tensor_tensor_scan(rcs, c_("rreset"), rp, 0.0, ALU.mult, ALU.add))
                        for i, name in enumerate(("FR", "DL", "DR")):
                            ins = dve.tensor_scalar(m1(name, SEQ), rcs, sel[:, 1 + 2 * i:2 + 2 * i], sel[:, 2 + 2 * i:3 + 2 * i], ALU.mult, ALU.add)
                        ins.then_inc(ev("rows_cs"), 1)
                    if m == FQ:
                        wait_full(dve, L, "gla_z")
                        z = psum(L, "gla_z")
                        own.step(dve.tensor_scalar(zb[:, 0:SEQ], z[:, 0:SEQ], p1("gbg")[:, 0:1], None, ALU.add))
                        drained(L, "gla_z", dve.tensor_scalar(zb[:, SEQ:512], z[:, SEQ:512], p1("gbg")[:, 1:2], None, ALU.add))
                        wait_drained(dve, L, "gla_z")
                        dve.scalar_tensor_tensor(ge, zb, -1.0, zb, ALU.mult, ALU.min).then_inc(ev("z_na"), 1)
                    if m == FK:
                        dve.wait_ge(ev("z_l"), L.one)
                        own.link(dve.scalar_tensor_tensor(zb, zb, 0.0, ge, ALU.min, ALU.subtract))
                        own.link(dve.tensor_tensor_scan(gb, c_("greset"), zb, 0.0, ALU.mult, ALU.add))
                        b3 = gb.rearrange("p (c n) -> p c n", n=HD)
                        dve.tensor_tensor(gd.rearrange("p (c n) -> p c n", n=HD), bc(b3[:, :, HD - 1:HD], [P, 8, HD]), b3,
                                          ALU.subtract).then_inc(ev("gla_b"), 1)
                    if m == GV:
                        dve.wait_ge(ev("gla_exp"), L.one)
                        wait_drained(dve, L, ("ip", GQ))
                        wait_drained(dve, L, ("ip", GK))
                        dve.scalar_tensor_tensor(gq, gq, SCALE, m1("eb", 512), ALU.mult, ALU.mult)
                        dve.tensor_tensor(m1("kend", 512), gk, gd, ALU.mult)
                        dve.tensor_tensor(gk, gk, m1("enb", 512), ALU.mult).then_inc(ev("gla_dec"), 1)
                    if m == FV:
                        wait_drained(dve, L, ("ip", FQ))
                        wait_drained(dve, L, ("ip", FK))
                        fqk, fsq = m1("fqk", 1024), m1("fsq", 1024)
                        own.link(dve.tensor_tensor(fsq, fqk, fqk, ALU.mult))
                        own.link(dve.tensor_reduce(stat[:, 160:176], fsq.rearrange("p (g n) -> p g n", n=HD), AX, ALU.add))
                        rstd = inverse_root(own, stat[:, 160:176], 16, HD)
                    if m == DC:
                        own.link(dve.tensor_scalar(rstd[:, 0:8], rstd[:, 0:8], SCALE, None, ALU.mult))
                        f3 = fqk.rearrange("p (g n) -> p g n", n=HD)
                        own.link(dve.tensor_tensor(f3, f3, bc(rstd.unsqueeze(2), [P, 16, HD]), ALU.mult))
                        for c, name in enumerate(("fqg", "fkg")):
                            part = f3[:, 8 * c:8 * c + 8, :]
                            ins = dve.tensor_tensor(part, part, bc(p1(name).unsqueeze(1), [P, 8, HD]), ALU.mult)
                        ins.then_inc(ev("fqk_ready"), 1)
                    if m == DB:
                        wait_drained(dve, L, ("ip", DV))
                        wait_drained(dve, L, ("ip", DB))
                        dy, db = m1("dy", 512), m1("db", 512)
                        own.link(convolve(own, [dy[:, 0:SEQ], dy[:, SEQ:512]], [dcu[:, 0, :], dcu[:, 1, :]], p1("scw"), 3))
                        dve.tensor_tensor(dy, dy, db, ALU.mult).then_inc(ev("dy_ready"), 1)

                tmr = m1("tmr", 16)
                wait_full(dve, L, "rowsT")
                drained(L, "rowsT", dve.tensor_copy(tmr.rearrange("p (q h) -> p q h", q=4),
                                                    psum(L, "rowsT")[:].rearrange("p (q h e) -> p q h e", q=4, h=H)[:, :, :, 2]))
                wait_full(dve, L, "ssd_xs")
                wait_drained(dve, L, "rowsT")
                x3 = psum(L, "ssd_xs")[:].rearrange("p (g n) -> p g n", n=HD)
                xd, xsD, xdd = m1("xd", 512), m1("xsD", 512), m1("xdd", 256)
                own.step(dve.tensor_tensor(xd.rearrange("p (g n) -> p g n", n=HD), x3, bc(tmr[:, 0:8].unsqueeze(2), [P, 8, HD]), ALU.mult))
                for T in range(NT):
                    ins = dve.tensor_tensor(xsD.rearrange("p (g n) -> p g n", n=HD)[:, 4 * T:4 * T + 4, :], x3[:, 4 * T:4 * T + 4, :],
                                            bc(p1("skip").unsqueeze(2), [P, H, HD]), ALU.mult)
                drained(L, "ssd_xs", ins)
                own.wait()
                dve.tensor_tensor(xdd.rearrange("p (g n) -> p g n", n=HD), xd[:, 0:256].rearrange("p (g n) -> p g n", n=HD),
                                  bc(tmr[:, 8:12].unsqueeze(2), [P, H, HD]), ALU.mult).then_inc(ev("xd_ready"), 1)
                wait_full(dve, L, "ssd_sc")
                sc = psum(L, "ssd_sc")[:].rearrange("p (g n) -> p g n", n=P)
                Mt, Lm = (m1(n, 1024).rearrange("p (g e n) -> p g e n", g=4, e=2) for n in ("Mt", "Lm"))
                for h in range(H):
                    wait_drained(dve, L, f"ssd_seg{h}")
                for g in range(4):
                    ins = dve.tensor_tensor(Mt[:, g], sc[:, g, :].unsqueeze(1).to_broadcast([P, 2, P]), Lm[:, g], ALU.mult)
                drained(L, "ssd_sc", ins)
                for hh in range(2):
                    wait_full(dve, L, f"gla_att{hh}")
                    drained(L, f"gla_att{hh}", dve.tensor_tensor(
                        m1("attT", 1024)[:, hh * 512:(hh + 1) * 512].rearrange("p (g n) -> p g n", g=4),
                        psum(L, f"gla_att{hh}")[:].rearrange("p (g n) -> p g n", g=4), bc(c_("glam").unsqueeze(1), [P, 4, P]), ALU.mult))
                wait_full(dve, L, "gla_kv")
                kv = psum(L, "gla_kv")[:, 0:384].rearrange("p (c t n) -> p c t n", c=3, t=2)
                Sg = m1("Sg", 384).rearrange("p (c t n) -> p c t n", c=3, t=2)
                eb = m1("eb", 512).rearrange("p (t c n) -> p t c n", t=2, c=4)
                own.link(dve.tensor_copy(Sg[:, 0], kv[:, 0]))
                for t in range(2):
                    own.step(dve.scalar_tensor_tensor(Sg[:, 1, t, :], Sg[:, 0, t, :], eb[:, t, 1, HD - 1:HD], kv[:, 1, t, :], ALU.mult, ALU.add))
                own.wait()
                for t in range(2):
                    ins = dve.scalar_tensor_tensor(Sg[:, 2, t, :], Sg[:, 1, t, :], eb[:, t, 2, HD - 1:HD], kv[:, 2, t, :], ALU.mult, ALU.add)
                drained(L, "gla_kv", ins)
                wait_drained(dve, L, "gla_kv")
                dve.tensor_tensor(m1("Sbd", 768).rearrange("p (g e n) -> p g e n", g=6, e=2),
                                  bc(m1("Sg", 384).rearrange("p (g n) -> p g n", g=6).unsqueeze(2), [P, 6, 2, HD]),
                                  bc(c_("half").unsqueeze(1).unsqueeze(3), [P, 6, 2, HD]), ALU.mult).then_inc(ev("gla_states"), 1)
                wait_full(dve, L, "ssd_y")
                drained(L, "ssd_y", dve.tensor_tensor(xsD, psum(L, "ssd_y")[:], xsD, ALU.add))
                for h in range(H):
                    ins = dve.tensor_scalar(m1("FL", 4 * SEQ)[:, h * SEQ:(h + 1) * SEQ], rcs, sel[:, 7 + 2 * h:8 + 2 * h],
                                            sel[:, 8 + 2 * h:9 + 2 * h], ALU.mult, ALU.add)
                ins.then_inc(ev("FL_ready"), 1)
                wait_full(dve, L, "ssd_yoff")
                drained(L, "ssd_yoff", dve.tensor_tensor(xdd.rearrange("p (g n) -> p g n", n=HD), psum(L, "ssd_yoff")[:, 0:256].rearrange("p (g n) -> p g n", n=HD),
                                                         bc(tmr[:, 12:16].unsqueeze(2), [P, H, HD]), ALU.mult))
                wait_drained(dve, L, "ssd_y")
                wait_drained(dve, L, "ssd_yoff")
                own.link(dve.tensor_tensor(xsD[:, 256:512], xsD[:, 256:512], xdd, ALU.add))
                own.step(dve.tensor_tensor(xs[:, :, 2 * GW:3 * GW], xsD.rearrange("p (t n) -> p t n", t=NT),
                                           m1("siluz", 512).rearrange("p (t n) -> p t n", t=NT), ALU.mult))
                for u in range(H + 1):
                    if u < H:
                        maxima(L, own, u, 1.0, m1("mx", 4), m1("nm", 4))
                    if u >= 1:
                        keep_turned(L, u - 1, m1("pt", 768))
                wait_full(dve, L, ("o", 0))
                rec = m1("frec", 8)
                own.link(dve.reciprocal(rec, m1("rowsum", 8)))
                o4 = psum(L, ("o", 0))[:].rearrange("p (t h n) -> p t h n", t=NT, h=H)
                y5 = xs[:].rearrange("p t (g n) -> p t g n", n=HD)
                for T in range(NT):
                    ins = dve.tensor_tensor(y5[:, T, 4:8, :], o4[:, T], bc(rec[:, 4 * T:4 * T + 4].unsqueeze(2), [P, H, HD]), ALU.mult)
                drained(L, ("o", 0), ins)
                for name in ("gla_o", "sc_t", ("o", 0)):
                    wait_drained(dve, L, name)
                own.wait()
                ysq = m1("ysq", 2048).rearrange("p (t n) -> p t n", t=NT)
                own.link(dve.tensor_tensor(ysq, xs[:], xs[:], ALU.mult))
                ss = stat[:, 160:192]
                own.link(dve.tensor_reduce(ss, ysq.rearrange("p t (g n) -> p (t g) n", n=HD), AX, ALU.add))
                s3 = ss.rearrange("p (t g) -> p t g", t=NT)[:, :, 8:12].rearrange("p t (a b) -> p t a b", b=2)
                pair = stat[:, 196:200].rearrange("p (t a) -> p t a", t=NT)
                own.link(dve.tensor_tensor(pair, s3[:, :, :, 0], s3[:, :, :, 1], ALU.add))
                own.link(dve.tensor_scalar(s3, bc(pair.unsqueeze(3), [P, NT, 2, 2]), 0.5, None, ALU.mult))
                rstd = inverse_root(own, ss, 32, HD)
                y3 = xs[:].rearrange("p t (g n) -> p (t g) n", n=HD)
                own.link(dve.tensor_tensor(y3, y3, bc(rstd.unsqueeze(2), [P, 32, HD]), ALU.mult))
                own.link(dve.tensor_tensor(xs[:], xs[:], bc(p1("ygain").unsqueeze(1), [P, NT, D]), ALU.mult))
                dve.tensor_tensor(xs[:, :, 0:GW], xs[:, :, 0:GW], m1("silug", 512).rearrange("p (t n) -> p t n", t=NT),
                                  ALU.mult).then_inc(ev("y_ready"), 1)
                finish(L, FFN_SLOTS + MIX1)

            def second_mixer(L, own):
                rotated = {KSW: m2("kr", 512), Q0: m2("qr", 1024)[:, 0:512], Q1: m2("qr", 1024)[:, 512:1024],
                           MQ0: m2("mqr", 1024)[:, 0:512], MQ1: m2("mqr", 1024)[:, 512:1024],
                           MK0: m2("mkr", 1024)[:, 0:512], MK1: m2("mkr", 1024)[:, 512:1024]}
                two = lambda ap: ap.rearrange("p (t n) -> p t n", t=2)
                dve.wait_ge(s_par, 16 * L.deep + 16)
                dve.memset(m2("hvr", 256), 0.0)
                dve.memset(m2("hu", 128), 0.0)
                dve.memset(m2("hidT", 512), 0.0)
                own.link(dve.memset(m2("kc", 32), 0.0))

                def rotate(m):
                    own.wait()
                    wait_full(dve, L, ("rot", m))
                    own.step(dve.tensor_tensor(two(m2("rc", 512)), two(raw_of(m)), bc(c_("ropeC").unsqueeze(1), [P, 2, SEQ]), ALU.mult))
                    drained(L, ("rot", m), dve.tensor_tensor(two(rotated[m]), two(psum(L, ("rot", m))[:]), bc(c_("ropeS").unsqueeze(1), [P, 2, SEQ]), ALU.mult))
                    own.wait()
                    wait_drained(dve, L, ("rot", m))
                    ins = dve.tensor_tensor(rotated[m], rotated[m], m2("rc", 512), ALU.add)
                    if m == MK1:
                        ins.then_inc(ev("roped"), 1)
                    else:
                        own.step(ins)

                for m in range(IP2 + 1):
                    for n in (2 * m + 4, 2 * m + 5) if m != GATES else (2 * m + 4,):
                        split_lo(L, FFN_SLOTS + n)
                    if m - 1 in ROPED:
                        rotate(m - 1)
                    if m == KSW:
                        wait_drained(dve, L, ("ip", KVC))
                        for c, pos in enumerate(("posk", "posv")):
                            for g in range(2):
                                src = m2("kx", 1024)[:, (2 * c + g) * SEQ:(2 * c + g + 1) * SEQ]
                                src = bass.AP(src.tensor, src.offset, [src.ap[0], (2, NCT), (NCT, NCMP)])
                                dst = m2("blk", 960)[:, c * 480:(c + 1) * 480].rearrange("p (k g n) -> p k g n", k=NCT, g=2)[:, :, g, :]
                                ins = dve.tensor_tensor(dst, src, bc(p2(pos).unsqueeze(2), [P, NCT, NCMP]), ALU.add)
                            ins.then_inc(ev(f"blk{c}"), 1)
                gate = m2("gate", 64)
                for c in range(2):
                    dve.wait_ge(ev(f"blk_hi{c}"), L.one)
                    dve.tensor_tensor(hlo[:, c * 480:(c + 1) * 480], m2("blk", 960)[:, c * 480:(c + 1) * 480],
                                      hhi[:, c * 480:(c + 1) * 480].bitcast(F32), ALU.subtract).then_inc(ev(f"blk_ready{c}"), 1)
                first = FFN_SLOTS + 2 * IP2 + 1
                for n in range(first + AHEAD, first + 2 * CMP_SLOTS):
                    split_lo(L, n)
                for c in range(2):
                    wait_full(dve, L, ("hid", c))
                    drained(L, ("hid", c), dve.tensor_copy(m2("hidT", 512)[0:2 * NCMP, c * 256:(c + 1) * 256], psum(L, ("hid", c))[0:2 * NCMP, 0:256]))
                hid, hx2, hu, he, hv = (m2(n, 128) for n in ("hid", "hx2", "hu", "he", "hv"))
                part = lambda ap: ap.rearrange("p (t n) -> p t n", n=32)[:, :, 0:2 * NCMP]
                wait_full(dve, L, "hidf")
                dve.tensor_scalar(gate, psum(L, "hidf")[:, 128:192], 1.0, None, ALU.add)
                drained(L, "hidf", dve.tensor_copy(part(hid), part(psum(L, "hidf")[:, 0:128])))
                wait_drained(dve, L, "hidf")
                own.link(dve.tensor_tensor(part(hx2), part(hid), part(hid), ALU.mult))
                own.link(dve.tensor_scalar(part(hx2), part(hx2), 0.044715, 1.0, ALU.mult, ALU.add))
                own.link(dve.tensor_tensor(part(hu), part(hx2), part(hid), ALU.mult))
                dve.tensor_scalar(part(hu), part(hu), -50.0, None, ALU.max).then_inc(ev("gelu_in"), 1)
                own.link(dve.reciprocal(gate, gate))
                dve.wait_ge(ev("gelu_e"), L.one)
                own.link(dve.tensor_scalar(part(hv), part(he), 1.0, None, ALU.add))
                own.link(dve.reciprocal(part(hv), part(hv)))
                dve.tensor_tensor(part(m2("hk", 64)), part(hv)[:, 0:2], part(hid)[:, 0:2], ALU.mult).then_inc(ev("gelu0"), 1)
                for t in range(2):
                    a, b = (ap[:, (2 + t) * 32:(2 + t) * 32 + 2 * NCMP].rearrange("p (g n) -> p g n", g=2).unsqueeze(1).to_broadcast([P, 4, 2, NCMP])
                            for ap in (hv, hid))
                    dst = m2("hvr", 256)[:, t * P:(t + 1) * P].rearrange("p (r g n) -> p r g n", r=4, g=2)[:, :, :, 0:NCMP]
                    ins = dve.tensor_tensor(dst, a, b, ALU.mult)
                ins.then_inc(ev("gelu1"), 1)
                wait_full(dve, L, "kc")
                drained(L, "kc", dve.tensor_tensor(m2("kc", 32).rearrange("p (g n) -> p g n", g=2)[:, :, 0:NCMP],
                                                   psum(L, "kc")[:, 0:2 * NCMP].rearrange("p (g n) -> p g n", g=2),
                                                   bc(c_("half").unsqueeze(2), [P, 2, NCMP]), ALU.mult))
                wait_full(dve, L, "vc")
                drained(L, "vc", dve.tensor_tensor(m2("vcd", 512).rearrange("p (g n) -> p g n", g=8), bc(psum(L, "vc")[:, 0:HD].unsqueeze(1), [P, 8, HD]),
                                                   bc(c_("own").unsqueeze(2), [P, 8, HD]), ALU.mult))
                wait_full(dve, L, "cmp_s")
                cs, cmx, csum, cfac = m2("cs", 256), m2("cmx", 16), m2("csum", 16), m2("cfac", 16)
                s3 = psum(L, "cmp_s")[:, 0:256].rearrange("p (g n) -> p g n", n=16)
                own.link(dve.tensor_reduce(cmx, s3, AX, ALU.max))
                own.link(dve.tensor_scalar(cmx, cmx, NEG / 10, None, ALU.max))
                drained(L, "cmp_s", dve.tensor_tensor(cs.rearrange("p (g n) -> p g n", n=16), s3, bc(cmx.unsqueeze(2), [P, 16, 16]), ALU.subtract))
                dve.wait_ge(ev("cmp_exp"), L.one)
                own.link(dve.tensor_reduce(csum, cs.rearrange("p (g n) -> p g n", n=16), AX, ALU.add))
                own.link(dve.tensor_scalar(csum, csum, 1.0, None, ALU.max))
                own.link(dve.reciprocal(csum, csum))
                g4 = gate.rearrange("p (t n) -> p t n", t=NT)
                for T in range(NT):
                    heads = lambda ap: ap.rearrange("p (g r) -> p g r", g=2)
                    own.step(dve.tensor_tensor(heads(cfac[:, 8 * T:8 * T + 8]), csum[:, 8 * T:8 * T + 8].rearrange("p (r g) -> p g r", g=2),
                                               heads(g4[:, T, 0:8]), ALU.mult))
                own.wait()
                y4 = xs[:].rearrange("p t (g n) -> p t g n", n=HD)
                for n in range(first + 2 * CMP_SLOTS, first + 2 * CMP_SLOTS + AHEAD):
                    split_lo(L, n)
                for T in range(NT):
                    wait_full(dve, L, f"cmp_o{T}")
                    drained(L, f"cmp_o{T}", dve.tensor_tensor(
                        y4[:, T, 0:8, :], psum(L, f"cmp_o{T}")[:].rearrange("p (g n) -> p g n", g=8),
                        bc(cfac[:, 8 * T:8 * T + 8].unsqueeze(2), [P, 8, HD]), ALU.mult))
                rowsum = m2("rowsum", 2 * UNITS).rearrange("p (t u) -> p t u", t=NT)
                fac = m2("fac", 8).rearrange("p (t u) -> p t u", t=NT)
                otmp = m2("otmp", 512)
                for u in range(UNITS + 3):
                    if u < UNITS:
                        maxima(L, own, u, SCALE, m2("mx", 4), m2("nm", 4))
                    if 1 <= u <= UNITS:
                        keep_turned(L, u - 1, m2("pt", 768))
                    if u >= 3 and (u - 3) % 4 == 3:
                        q = (u - 3) // 4
                        kind, h0 = q // 2, 4 * (q % 2)
                        wait_full(dve, L, ("o", q))
                        own.link(dve.reciprocal(fac, rowsum[:, :, 4 * q:4 * q + 4]))
                        if kind < 2:
                            own.link(dve.tensor_tensor(fac, fac, g4[:, :, 8 + 8 * kind + h0:12 + 8 * kind + h0], ALU.mult))
                        o4 = psum(L, ("o", q))[:].rearrange("p (t h n) -> p t h n", t=NT, h=4)
                        t4 = otmp.rearrange("p (t h n) -> p t h n", t=NT, h=4)
                        for T in range(NT):
                            dst = t4[:, T] if kind < 2 else y4[:, T, 8 + h0:12 + h0, :]
                            ins = dve.tensor_tensor(dst, o4[:, T], bc(fac[:, T, :].unsqueeze(2), [P, 4, HD]), ALU.mult)
                        drained(L, ("o", q), ins)
                        if kind < 2:
                            wait_drained(dve, L, ("o", q))
                            yp = xs[:, :, h0 * HD:(h0 + 4) * HD]
                            own.step(dve.tensor_tensor(yp, yp, otmp.rearrange("p (t n) -> p t n", t=NT), ALU.add))
                            own.wait()
                finish(L, FFN_SLOTS + MIX2)

            dve.sem_inc(split_done, RING)
            dve.memset(ones[:], 1.0).then_inc(ones_set, 1)
            for b in range(8):
                dve.sem_inc(bank_read[b], 1)
            dve.wait_ge(s_con, 16)
            dve.wait_ge(s_x, 16)
            for n in range(AHEAD):
                split_lo(Layer(0, 0), n)
            for blk, mixer in enumerate((first_mixer, second_mixer)):
                with dve.Fori(0, DEPTH) as l:
                    L = Layer(l, blk)
                    own = Own(dve, dve_own, L)
                    norm(L, own, 0)
                    ffn(L, 0)
                    norm(L, own, 1)
                    mixer(L, own)
                    norm(L, own, 2)
                    ffn(L, 1)
                    own.close()
            last = Layer(DEPTH, 1)
            rstd = roots(last, Own(dve, dve_own, last), 0)
            dve.wait_ge(s_par, 16 * 2 * DEPTH + 16)
            for T in range(NT):
                dve.scalar_tensor_tensor(xs[:, T, :], x[:, T, :], rstd[:, T:T + 1], par[:, 0:D], ALU.mult, ALU.mult).then_inc(xs_ready, 1)


def constants():
    con = np.zeros((P, CON_W), np.float32)

    def put(name, value):
        con[:, CON[name][0]:CON[name][1]] = value

    p, c = np.arange(P)[:, None], np.arange(P)[None, :]
    put("ident", p == c)
    put("negq", np.where(c <= p, 0, NEG))
    put("negT", np.where(c >= p, 0, NEG))
    put("glam", (c >= p) & (c // HD == p // HD))
    tok = np.arange(SEQ)[None, :]
    put("rreset", np.where((p % 32 >= 2) & (p % 32 < 4) & (tok == P), 0, 1))
    put("greset", np.arange(2 * SEQ)[None, :] % HD != 0)
    sel = np.zeros((P, 15), np.float32)
    e = [np.arange(P) % 32 == i for i in range(4)]
    sel[:, 0] = np.where(e[0] | e[1], -1, 1)
    for at, picks in ((1, ((0, 0, 1), (1, -1, 0))), (3, ((2, 0, 1), (3, -1, 0))), (5, ((2, 1, 0), (3, 0, 1)))):
        for row, factor, shift in picks:
            sel[e[row], at], sel[e[row], at + 1] = factor, shift
    for h in range(H):
        sel[32 * h, 7 + 2 * h], sel[32 * h + 1, 8 + 2 * h] = 1, 1
    put("sel", sel)
    put("half", p // HD == np.arange(2)[None, :])
    put("own", (p // 16 % 2) * 4 + p // 32 == np.arange(8)[None, :])
    n, T = np.arange(16)[None, None, None, :], np.arange(NT)[None, :, None, None]
    seen = np.broadcast_to((n < NCMP) & (16 * n + 31 <= T * P + p[:, :, None, None]), (P, NT, 8, 16))
    put("cmpmask", np.where(seen, 0, NEG).reshape(P, 256))
    inv_freq = np.power(np.float32(500000.0), -(np.arange(0, 16, 2, dtype=np.float32) / np.float32(16)))
    angle = np.arange(SEQ, dtype=np.float32)[:, None] * inv_freq[None, :]
    cos, sin, turn = np.ones((P, SEQ), np.float32), np.zeros((P, SEQ), np.float32), np.zeros((P, P), np.float32)
    for q in range(P):
        d = q % HD
        if d < 16:
            cos[q], sin[q] = np.cos(angle[:, d % 8]), np.sin(angle[:, d % 8])
            turn[q + 8 if d < 8 else q - 8, q] = -1 if d < 8 else 1
    put("ropeC", cos)
    put("ropeS", sin)
    put("ropeR", turn)
    return con


def rows_tiles(w):
    return w.reshape(-1, P, w.shape[1]).transpose(1, 0, 2)


def fm_slot(w):
    return rows_tiles(w).reshape(P, -1)


def tm_slots(w):
    return [rows_tiles(w[half * 512:(half + 1) * 512]).reshape(P, -1) for half in range(2)]


def ffn_slots(gate, up, down):
    out = []
    for i in range(STEPS + 1):
        if i < STEPS:
            out += [fm_slot(gate[:, i * P:(i + 1) * P]), fm_slot(up[:, i * P:(i + 1) * P])]
        if i:
            out.append(down[(i - 1) * P:i * P])
    return out


def scattered(columns):
    out = np.zeros((D, P), np.float32)
    for at, col in columns:
        out[:, at:at + col.shape[1]] = col
    return out


def first_mixer_slots(w_in, w_out):
    names = ["a_q", "a_k", "a_v", "a_g", "a_lr", "b_q", "b_k", "b_v", "b_f", "c_z", "c_xbc", "c_dt", "d_b", "d_c", "d_v"]
    widths = [GW] * 4 + [16] + [GW] * 3 + [H] + [GW, 3 * GW, H] + [GW] * 3
    part = dict(zip(names, np.split(w_in, np.cumsum(widths)[:-1], axis=1)))
    fm = lambda w: [fm_slot(w[:, 0:P]), fm_slot(w[:, P:2 * P])]
    out = []
    for t in range(3):
        out += fm(part["c_xbc"][:, t * GW:(t + 1) * GW])
    out += tm_slots(part["c_z"]) + tm_slots(part["a_g"])
    rows = []
    for h in range(H):
        f, dt = part["b_f"][:, h:h + 1], part["c_dt"][:, h:h + 1]
        rows += [(32 * h, f), (32 * h + 1, f), (32 * h + 2, dt), (32 * h + 3, dt)]
    out += [fm_slot(scattered([(0, part["a_lr"])])), fm_slot(scattered(rows))]
    out += fm(part["a_q"]) + fm(part["a_k"])
    for name in ("b_q", "b_k", "a_v", "b_v"):
        out += tm_slots(part[name])
    for name in ("d_c", "d_v", "d_b"):
        out += fm(part[name])
    return out + [w_out[k * P:(k + 1) * P] for k in range(KD)]


def second_mixer_slots(w_in, w_ck1, w_cv1, w_out):
    q, kv, gates, moba = np.split(w_in, [512, 1280, 1304], axis=1)
    q = q.reshape(D, 2, 4, HD)
    k_cmp, v_cmp, k_slc, v_slc, k_win, v_win = (kv[:, i * P:(i + 1) * P] for i in range(6))
    fm = lambda w: fm_slot(np.ascontiguousarray(w))
    out = [fm(k_cmp), fm(v_cmp), fm(k_slc), fm(k_win)]
    out += [fm(q[:, :, r].reshape(D, P)) for r in range(4)]
    out += tm_slots(np.concatenate([v_slc, v_win], axis=1))
    out += [fm(moba[:, t * P:(t + 1) * P]) for t in range(8)]
    out += tm_slots(moba[:, 1024:1280]) + tm_slots(moba[:, 1280:1536])
    by_branch = gates.reshape(D, 8, 3).transpose(0, 2, 1).reshape(D, 24)
    out.append(fm_slot(scattered([(0, by_branch)])))
    for w in (w_ck1, w_cv1):
        out += [rows_tiles(w[s * 512:(s + 1) * 512]).reshape(P, -1) for s in range(CMP_SLOTS)]
    return out + [w_out[k * P:(k + 1) * P] for k in range(KD)]


def stream(a):
    out = []
    for l in range(DEPTH):
        out += ffn_slots(a["ffn1_w_gate"][l], a["ffn1_w_up"][l], a["ffn1_w_down"][l])
        out += first_mixer_slots(a["w_in"][l], a["w_out"][l])
        out += ffn_slots(a["ffn2_w_gate"][l], a["ffn2_w_up"][l], a["ffn2_w_down"][l])
    for l in range(DEPTH):
        out += ffn_slots(a["w_ffn1_gate_2"][l], a["w_ffn1_up_2"][l], a["w_ffn1_down_2"][l])
        out += second_mixer_slots(a["w_in_2"][l], a["w_ck1_2"][l], a["w_cv1_2"][l], a["w_out_2"][l])
        out += ffn_slots(a["w_ffn2_gate_2"][l], a["w_ffn2_up_2"][l], a["w_ffn2_down_2"][l])
    out += [np.zeros((P, SLOT), np.float32)] * TAIL
    assert len(out) == N_SLOTS
    return np.stack(out)


def replicated(row):
    return np.broadcast_to(row, (P,) + row.shape)


def first_parameters(a, l):
    par = np.zeros((P, PAR1_W), np.float32)

    def put(name, value):
        par[:, PAR1[name][0]:PAR1[name][1]] = value

    put("convw", a["ssm_conv_w"][l].reshape(4, 6, P).transpose(2, 1, 0).reshape(P, 24))
    put("convb", a["ssm_conv_b"][l].reshape(6, P).T)
    put("scw", a["sc_conv_w"][l].reshape(3, 2, P).transpose(2, 1, 0).reshape(P, 6))
    put("skip", replicated(a["ssm_D"][l]))
    bias, a_log = np.zeros((P, 1), np.float32), np.zeros((P, 1), np.float32)
    for h in range(H):
        bias[32 * h:32 * h + 2, 0] = a["fox_b_forget"][l, h]
        bias[32 * h + 2:32 * h + 4, 0] = a["ssm_dt_bias"][l, h]
        a_log[32 * h + 2:32 * h + 4, 0] = a["ssm_A_log"][l, h]
    put("rbias", bias)
    put("ralog", a_log)
    put("gbg", a["gla_b_gate"][l].reshape(2, P).T)
    put("fqg", replicated(a["fox_q_norm"][l]))
    put("fkg", replicated(a["fox_k_norm"][l]))
    par[0:16, PAR1["gup"][0]:PAR1["gup"][1]] = a["gla_w_gate_up"][l]
    put("ygain", replicated(np.concatenate([a[n][l] for n in ("gla_norm", "fox_out_norm", "ssm_norm", "sc_out_norm")])))
    return par


def second_parameters(a, l):
    par = np.zeros((P, PAR2_W), np.float32)
    for name, source in (("posk", "pos_ck_2"), ("posv", "pos_cv_2")):
        par[:, PAR2[name][0]:PAR2[name][1]] = a[source][l].reshape(NCT, 2, HD).transpose(1, 2, 0).reshape(P, NCT)
    ck2, cv2 = rows_tiles(a["w_ck2_2"][l]), rows_tiles(a["w_cv2_2"][l])
    par[:, PAR2["ck2"][0]:PAR2["ck2"][1]] = np.concatenate([ck2, ck2], axis=2).reshape(P, 4 * HD)
    par[:, PAR2["cv2"][0]:PAR2["cv2"][1]] = cv2.reshape(P, 2 * HD)
    return par


def kernel(**inputs):
    import concourse.bacc as bacc
    from concourse.bass_utils import run_bass_kernel_spmd

    a = {name: np.asarray(value) for name, value in inputs.items()}
    gains = [a[n][l] for l in range(DEPTH) for n in ("ffn1_norm", "mix_norm", "ffn2_norm")]
    gains += [a[n][l] for l in range(DEPTH) for n in ("norm_ffn1_2", "norm_mix_2", "norm_ffn2_2")]
    arrays = {
        "x": np.ascontiguousarray(a["x"][0].reshape(NT, P, D).transpose(1, 0, 2)),
        "w": stream(a),
        "gain": np.concatenate([np.stack(gains).reshape(2 * DEPTH, 3 * KD, P).transpose(0, 2, 1),
                                np.zeros((1, P, 3 * KD), np.float32)]),
        "last_gain": np.ascontiguousarray(replicated(a["norm_final_2"])),
        "par1": np.stack([first_parameters(a, l) for l in range(DEPTH)]),
        "par2": np.stack([second_parameters(a, l) for l in range(DEPTH)]),
        "con": constants(),
    }
    nc = bacc.Bacc("TRN2", target_bir_lowering=False, num_devices=1)
    args = [nc.dram_tensor(f"in_{name}_dram", array.shape, F32, kind="ExternalInput").ap() for name, array in arrays.items()]
    out_d = nc.dram_tensor("out_0_dram", (P, NT, D), F32, kind="ExternalOutput").ap()
    build(nc, *args, out_d)
    result = run_bass_kernel_spmd(nc, [{f"in_{n}_dram": v for n, v in arrays.items()}], core_ids=[0])
    return np.asarray(result.results[0]["out_0_dram"]).transpose(1, 0, 2).reshape(1, SEQ, D)
```

```python
from contextlib import ExitStack

import numpy as np

import concourse.bass as bass
from concourse import mybir

F32 = mybir.dt.float32
F32R = mybir.dt.float32r
I32 = mybir.dt.int32
ALU = mybir.AluOpType
ACT = mybir.ActivationFunctionType
AX = mybir.AxisListType.X

P = 128
SEQ, D, FF, DEPTH = 256, 1024, 2816, 2
NT = SEQ // P
KD = D // P
GW, HD, H = 256, 64, 4
EPS = 1e-6
NEG = -1e30
SCALE = HD ** -0.5
SLOT = 1024
RING = 6
AHEAD = 4
STEPS = FF // P
FFN_SLOTS = 3 * STEPS
IP1 = 15
IP2 = 11
WO_SLOTS = KD
MIX1 = 2 * IP1 + WO_SLOTS
CMP_SLOTS = 4
MIX2 = 2 * IP2 + 1 + 2 * CMP_SLOTS + WO_SLOTS
LAYER1 = 2 * FFN_SLOTS + MIX1
LAYER2 = 2 * FFN_SLOTS + MIX2
TAIL = AHEAD
N_SLOTS = DEPTH * (LAYER1 + LAYER2) + TAIL
NCMP = 15
NCT = 16
MIX_W = 18400
ORDER1 = (0, 2, 3, 1)
ORDER2 = (0, 1, 2, 3)
CHAIN = 256

XBC0, XBC1, XBC2, ZG, GG, ROWS, GQ, GK, FQ, FK, GV, DC, DV, DB, FV = range(IP1)
KVC, KSW, Q0, Q1, GATES, VSW, MQ0, MQ1, MK0, MK1, MV0, MV1 = range(IP2 + 1)
CMP0 = FFN_SLOTS + 2 * GATES + 1
SHARED = [[FFN_SLOTS, FFN_SLOTS + 2, FFN_SLOTS + 2 * ZG, FFN_SLOTS + 2 * GV],
          [FFN_SLOTS, FFN_SLOTS + 2] + list(range(CMP0, CMP0 + 2 * CMP_SLOTS + 1, 2))]
ROPED = [KSW, Q0, Q1, MQ0, MQ1, MK0, MK1]
COMPRESSED = {VSW: [("hidf", 4)], MQ0: [("kc", 4), ("vc", 5)], MQ1: [("cmp_s", 6)], MK0: [("cmp_pt", 7)], MK1: [("cmp_o0", 6), ("cmp_o1", 7)]}
UNITS = 24


def positions(mix):
    total = 2 * FFN_SLOTS + mix
    gap = -total % RING
    return [n if n < FFN_SLOTS else n + gap for n in range(total)]


def columns(fields):
    at, out = 0, {}
    for name, width in fields:
        out[name] = (at, at + width)
        at += width
    return out, at


CON, CON_W = columns([("ident", P), ("negq", P), ("negT", P), ("glam", P), ("rreset", SEQ), ("greset", 2 * SEQ),
                      ("sel", 15), ("half", 2), ("own", 8), ("cmpmask", 256), ("ropeC", SEQ), ("ropeS", SEQ), ("ropeR", P)])
PAR1, PAR1_W = columns([("convw", 24), ("convb", 6), ("scw", 6), ("skip", 4), ("rbias", 1), ("ralog", 1), ("gbg", 2),
                        ("fqg", HD), ("fkg", HD), ("gup", GW), ("ygain", D)])
PAR2, PAR2_W = columns([("posk", NCT), ("posv", NCT), ("ck2", 4 * HD), ("cv2", 2 * HD)])


class Turns:

    def __init__(self):
        self.of, self.count, self.fulls = {}, [0] * 8, [0] * 8

    def add(self, name, bank, by_slot=None, times=1):
        self.of[name] = (bank, self.count[bank], self.fulls[bank], by_slot)
        self.count[bank] += times
        self.fulls[bank] += by_slot is None


def norm_turns(t, w):
    for j in range(KD // 2):
        t.add(("norm", w, j), j)


def ffn_turns(t, f, mixer):
    for s in range(2):
        t.add(("gu", f, s), s, by_slot=-1, times=STEPS // 2)
    t.add(("R", f), 2)
    end = FFN_SLOTS - 1 + f * (FFN_SLOTS + mixer)
    for T in range(NT):
        for half in range(2):
            t.add(("acc", f, T, half), 4 + 2 * T + half, by_slot=end if (T, half) == (NT - 1, 1) else None)


def out_turns(t, mixer, order, banks):
    for j, bank in zip(order, banks):
        t.add(("yT", j), bank)
    end = FFN_SLOTS + mixer - 1
    for T in range(NT):
        for half in range(2):
            t.add(("wo", T, half), 4 + 2 * T + half, by_slot=end if (T, half) == (NT - 1, 1) else None)


def attention_turns(t, units, s_banks, pt_banks, o_bank):
    for u in range(units + 2):
        if u < units:
            t.add(("s", u), s_banks[u % 2])
        if 1 <= u <= units:
            t.add(("pt", u - 1), pt_banks[(u - 1) % 2])
        if u >= 2 and (u - 2) % 4 == 0:
            t.add(("o", (u - 2) // 4), o_bank((u - 2) // 4))


def pair_slots(m):
    return FFN_SLOTS + (2 * m if m <= GATES else 2 * m - 1 + 2 * CMP_SLOTS), 1 if m == GATES else 2


def first_turns():
    t = Turns()
    norm_turns(t, 0)
    ffn_turns(t, 0, MIX1)
    norm_turns(t, 1)
    for m in range(FV):
        t.add(("ip", m), m % 4, by_slot=FFN_SLOTS + 2 * m + 1)
        if m == GK:
            t.add("gla_z", 4)
    for name, bank in (("ssd_xs", 5), ("ssd_b", 6), ("rowsT", 7), ("gla_kend", 4), ("ssd_sc", 3), ("ssd_seg0", 0),
                       ("ssd_seg1", 1), ("ssd_seg2", 2), ("ssd_seg3", 7), ("gla_att0", 5), ("gla_att1", 6), ("gla_kv", 2), ("fox_q", 7), ("fox_k", 4),
                       ("ssd_st", 3), ("ssd_y", 0), ("ssd_yoff", 1), ("gla_o", 5), ("sc_t", 6)):
        t.add(name, bank)
    t.add(("ip", FV), 1, by_slot=FFN_SLOTS + 2 * FV + 1)
    attention_turns(t, H, (2, 3), (4, 7), lambda g: 0)
    out_turns(t, MIX1, ORDER1, (1, 2, 3, 0))
    norm_turns(t, 2)
    ffn_turns(t, 1, MIX1)
    return t


def second_turns():
    t = Turns()
    norm_turns(t, 0)
    ffn_turns(t, 0, MIX2)
    norm_turns(t, 1)
    for m in range(IP2 + 1):
        t.add(("ip", m), m % 4, by_slot=sum(pair_slots(m)) - 1)
        if m - 1 in ROPED:
            t.add(("rot", m - 1), 4 + ROPED.index(m - 1) % 2)
        if m == GATES:
            for c in range(2):
                t.add(("hid", c), 6 + c, by_slot=CMP0 + CMP_SLOTS * (c + 1) - 1)
        for name, bank in COMPRESSED.get(m, ()):
            t.add(name, bank)
    attention_turns(t, UNITS, (0, 1), (2, 3), lambda g: 6 + g % 2)
    out_turns(t, MIX2, ORDER2, (0, 1, 2, 3))
    norm_turns(t, 2)
    ffn_turns(t, 1, MIX2)
    return t


TURNS1, TURNS2 = first_turns(), second_turns()


class Layer:

    def __init__(self, l, blk):
        self.l, self.blk = l, blk
        self.turns = TURNS2 if blk else TURNS1
        self.shared = SHARED[blk]
        self.order = ORDER2 if blk else ORDER1
        pos = positions(MIX2 if blk else MIX1)
        self.pos = pos + [pos[-1] + 1 + n for n in range(AHEAD)]
        self.one = l + 1
        self.deep = l + blk * DEPTH
        self.each = self.deep + 1
        self.slot0 = l * (LAYER2 if blk else LAYER1) + blk * DEPTH * LAYER1
        self.chain0 = self.deep * CHAIN

    def bank(self, name):
        b, k, _, _ = self.turns.of[name]
        return b, self.l * self.turns.count[b] + (self.blk * DEPTH * TURNS1.count[b] + k)

    def fulls(self, name):
        b, _, k, _ = self.turns.of[name]
        return self.l * self.turns.fulls[b] + (self.blk * DEPTH * TURNS1.fulls[b] + k)

    def raw_use(self, n):
        place = self.pos[n] % RING
        per = [sum(p % RING == place for p in positions(m)) for m in (MIX1, MIX2)]
        return place, self.l * per[self.blk] + (self.blk * DEPTH * per[0] + sum(p % RING == place for p in self.pos[:n]))

    def splits(self, n):
        per = [LAYER1 - len(SHARED[0]), LAYER2 - len(SHARED[1])]
        return self.l * per[self.blk] + (self.blk * DEPTH * per[0] + n + 1 + RING - sum(m <= n for m in self.shared))

    def shares(self, n):
        return self.l * len(self.shared) + (self.blk * DEPTH * len(SHARED[0]) + self.shared.index(n) + 1)

    def before(self, n):
        p = self.pos[n] - RING
        while p >= 0 and p not in self.pos:
            p -= RING
        return self.pos.index(p) if p >= 0 else p


def build(nc, x_d, w_d, gain_d, last_gain_d, par1_d, par2_d, con_d, out_d):
    with ExitStack() as ctx:
        def sb(name, shape, dt=F32):
            return ctx.enter_context(nc.sbuf_tensor(name, shape, dt))

        def sem(name):
            return ctx.enter_context(nc.semaphore(name))

        raw = sb("raw", [P, RING, SLOT])
        whi = sb("whi", [P, RING, SLOT], F32R)
        wlo = sb("wlo", [P, RING, SLOT], F32R)
        x = sb("x", [P, NT, D])
        xs = sb("xs", [P, NT, D])
        thi = sb("thi", [P, KD, SEQ], F32R)
        tlo = sb("tlo", [P, KD, SEQ], F32R)
        gain = sb("gain", [P, 3 * KD])
        ones = sb("ones", [P, P])
        diag = sb("diag", [P, SEQ])
        root = sb("root", [P, SEQ])
        par = sb("par", [P, max(PAR1_W, PAR2_W)])
        con = sb("con", [P, CON_W])
        identR = sb("identR", [P, P], F32R)
        maskR = sb("maskR", [P, 3 * P], F32R)
        hhi = sb("hhi", [P, 2 * NCT * 2 * NCMP], F32R)
        hlo = sb("hlo", [P, 2 * NCT * 2 * NCMP], F32R)
        stat = sb("stat", [P, 256])
        mix = sb("mix", [P, MIX_W])
        gu = mix[:, 0:4 * SEQ].rearrange("p (s c n) -> p s c n", s=2, c=2)
        bank = [ctx.enter_context(nc.psum_tensor(f"bank{b}", [P, 512], F32)) for b in range(8)]

        def c_(name):
            return con[:, CON[name][0]:CON[name][1]]

        def p1(name):
            return par[:, PAR1[name][0]:PAR1[name][1]]

        def p2(name):
            return par[:, PAR2[name][0]:PAR2[name][1]]

        ident = c_("ident")

        class Parts:
            pass

        def carve(fields):
            part, at = {}, 0
            for name, width in fields:
                if isinstance(width, str):
                    part[name] = part[width]
                else:
                    part[name] = at
                    at += width
            assert at <= MIX_W, at
            return part

        M1 = carve([
            ("xbcu", 4 * 260), ("dcu", 2 * 260), ("xbcs", 6 * SEQ), ("siluz", 512), ("silug", 512),
            ("ru", SEQ), ("re", SEQ), ("rs", SEQ), ("rs2", SEQ), ("rp", SEQ),
            ("rsp", SEQ), ("rcs", SEQ), ("rE", SEQ), ("FR", SEQ), ("DL", SEQ), ("DR", SEQ), ("lrT", SEQ),
            ("gq", 512), ("gk", 512), ("zb", 512), ("ge", 512), ("gb", 512), ("eb", 512), ("enb", 512), ("gd", 512),
            ("kend", 512), ("fqk", "xbcu"), ("fsq", 1024), ("fT", "gd"), ("av", 512), ("bv", 512), ("dc", 512),
            ("avs", 256), ("db", 512), ("Bt", 256), ("Mt", 1024), ("St", "lrT"), ("kendT", 768), ("Sg", 384), ("Sbd", 768), ("FL", "Mt"),
            ("P", "gb"), ("Lm", "zb"), ("xd", "ru"), ("xsD", "rs"), ("xdd", "rp"), ("attT", "fsq"),
            ("dy", "dc"), ("pt", "xbcs"), ("tmr", 16), ("ralogx", 1), ("mx", 4), ("nm", 4), ("rowsum", 8), ("frec", 8)])
        M2 = carve([
            ("kx", 1024), ("blk", 960), ("kr", 512), ("qraw", 1024), ("qr", 1024), ("mqr", 1024), ("mkr", 1024),
            ("rtmp", 1024), ("rc", 512), ("vsw", 512), ("mv", 1024), ("gate", 64), ("gex", SEQ), ("hidT", 512), ("hid", 128), ("hx2", 128),
            ("hu", 128), ("he", 128), ("hk", 64), ("hv", 128), ("hvr", 256), ("kc", 32), ("vcd", 512), ("cs", 256), ("cpT", 256),
            ("P", 768), ("pt", 768), ("mx", 4), ("nm", 4), ("rowsum", 2 * UNITS), ("fac", 8), ("otmp", 512),
            ("cmx", 16), ("csum", 16), ("cfac", 16)])

        def m1(name, width):
            return mix[:, M1[name]:M1[name] + width]

        def m2(name, width):
            return mix[:, M2[name]:M2[name] + width]

        s_rest = sem("rest_of_con_loaded")
        s_x, s_con, s_par, s_gain, s_out = sem("x_loaded"), sem("con_loaded"), sem("par_loaded"), sem("gain_loaded"), sem("out_stored")
        s_raw = [sem(f"raw_loaded{i}") for i in range(RING)]
        hi_done = sem("hi_done")
        split_done = sem("split_done")
        shared_done = sem("shared_done")
        slot_used = sem("slot_used")
        bank_full = [sem(f"bank_full{b}") for b in range(8)]
        bank_read = [sem(f"bank_read{b}") for b in range(8)]
        sq_done = sem("sq_done")
        xs_ready = sem("xs_ready")
        ones_set = sem("ones_set")
        thi_done = sem("thi_done")
        sg_done = sem("sg_done")
        hf_done = sem("hf_done")
        hhi_done = sem("hhi_done")
        h_ready = sem("h_ready")
        act_own, dve_own = sem("act_own"), sem("dve_own")
        sm_max = sem("sm_max")
        events = {}

        def ev(name):
            if name not in events:
                events[name] = sem(name)
            return events[name]

        def wait_full(eng, L, name):
            b, _, _, by_slot = L.turns.of[name]
            if by_slot is None:
                eng.wait_ge(bank_full[b], L.fulls(name) + 1)
            else:
                eng.wait_ge(slot_used, L.slot0 + (by_slot + 1 + RING))

        def wait_drained(eng, L, name):
            b, k = L.bank(name)
            eng.wait_ge(bank_read[b], k + 2)

        def claim(pe, L, name):
            b, k = L.bank(name)
            pe.wait_ge(bank_read[b], k + 1)
            return bank[b]

        def updated(eng, L, w, T, half):
            if w == 0:
                b, k = L.bank(("acc", 0, T, half))
                eng.wait_ge(bank_read[b], k + 1)
            else:
                wait_drained(eng, L, ("acc", 0, T, half) if w == 1 else ("wo", T, half))

        def ffn_slot(L, w):
            return AHEAD + (FFN_SLOTS + (MIX2 if L.blk else MIX1) if w else 0)

        def gain_of(L, w, k):
            return gain[:, w * KD + k:w * KD + k + 1]

        def psum(L, name):
            return bank[L.bank(name)[0]]

        def full(L, name, ins):
            ins.then_inc(bank_full[L.bank(name)[0]], 1)

        def drained(L, name, ins):
            ins.then_inc(bank_read[L.bank(name)[0]], 1)

        class Own:

            def __init__(self, eng, done, L):
                self.eng, self.done, self.L, self.n = eng, done, L, 0

            def step(self, ins):
                self.n += 1
                ins.then_inc(self.done, 1)

            def wait(self):
                self.eng.wait_ge(self.done, self.L.chain0 + self.n)

            def link(self, ins):
                self.step(ins)
                self.wait()

            def close(self):
                assert self.n <= CHAIN, self.n
                self.eng.sem_inc(self.done, CHAIN - self.n)

        def raw_of(m):
            if m in (Q0, Q1):
                return m2("qraw", 1024)[:, (m - Q0) * 512:(m - Q0 + 1) * 512]
            s = [KSW, MQ0, MQ1, MK0, MK1].index(m) % 2
            return m2("rtmp", 1024)[:, s * 512:(s + 1) * 512]

        block = ctx.enter_context(nc.Block())

        @block.sync
        def _(sp):
            def snap(value):
                return value if isinstance(value, int) else sp.snap(value)

            def load(L, n, i=0):
                place, uses = L.raw_use(n)
                slot = snap(L.slot0 + n + RING * i)
                last = L.before(n)
                if last in L.shared:
                    free = snap(L.shares(last))
                    sp.wait_ge(shared_done, free)
                else:
                    free = snap(L.splits(last) + RING * i)
                    sp.wait_ge(split_done, free)
                sp.dma_start(raw[:, place, :], w_d[bass.ds(slot, 1)].rearrange("a p n -> (a p) n")).then_inc(s_raw[place], 16)

            def layer(l, blk):
                L = Layer(l, blk)
                mixer = MIX2 if blk else MIX1
                with sp.Fori(0, FFN_SLOTS // RING) as i:
                    for n in range(RING):
                        load(L, n, i)
                row = snap(l + 0)
                done = snap(L.slot0 + RING)
                sp.wait_ge(slot_used, done)
                src, width = (par2_d, PAR2_W) if blk else (par1_d, PAR1_W)
                sp.dma_start(par[:, 0:width], src[bass.ds(row, 1)].rearrange("a p n -> (a p) n")).then_inc(s_par, 16)
                for n in range(FFN_SLOTS, FFN_SLOTS + mixer):
                    load(L, n)
                with sp.Fori(0, FFN_SLOTS // RING) as i:
                    for n in range(RING):
                        load(L, FFN_SLOTS + mixer + n, i)
                row = snap(L.deep + 1)
                b, k = L.bank(("norm", 2, KD // 2 - 1))
                used = snap(k + 2)
                sp.wait_ge(bank_read[b], used)
                sp.dma_start(gain[:], gain_d[bass.ds(row, 1)].rearrange("a p n -> (a p) n")).then_inc(s_gain, 16)

            def last_uses(last, place):
                return (sum(p % RING == place for p in positions(MIX1)) + sum(p % RING == place for p in positions(MIX2))) * DEPTH \
                    + sum(p % RING == place for p in last.pos[:TAIL])

            sp.dma_start(x[:], x_d).then_inc(s_x, 16)
            sp.dma_start(ident, con_d[:, 0:P]).then_inc(s_con, 16)
            sp.dma_start(gain[:], gain_d[0]).then_inc(s_gain, 16)
            with sp.Fori(0, DEPTH) as l:
                layer(l, 0)
            with sp.Fori(0, DEPTH) as l:
                layer(l, 1)
            last = Layer(DEPTH, 1)
            for n in range(TAIL):
                load(last, n)
            sp.wait_ge(slot_used, last.slot0 + RING)
            sp.dma_start(par[:, 0:D], last_gain_d).then_inc(s_par, 16)
            for T in range(NT):
                for half in range(2):
                    cols = slice(half * 512, half * 512 + 512)
                    sp.wait_ge(xs_ready, 2 * T + half + 1)
                    sp.dma_start(out_d[:, T, cols], xs[:, T, cols]).then_inc(s_out, 16)
            sp.wait_ge(s_out, 2 * NT * 16)
            sp.wait_ge(s_gain, 16 * (2 * DEPTH + 1))
            for place in range(RING):
                sp.wait_ge(s_raw[place], 16 * last_uses(last, place))


        @block.gpsimd
        def _(pool):
            def split_lo(L, n, i=0):
                place, _ = L.raw_use(n)
                pool.wait_ge(hi_done, L.slot0 + (n + 1) + RING * i)
                nc.gpsimd.tensor_tensor(wlo[:, place, :], raw[:, place, :], whi[:, place, :].bitcast(F32), ALU.subtract).then_inc(split_done, 1)

            pool.sem_inc(split_done, RING)
            for blk, mixer in enumerate((MIX1, MIX2)):
                with pool.Fori(0, DEPTH) as l:
                    L = Layer(l, blk)
                    with pool.Fori(0, FFN_SLOTS // RING) as i:
                        for n in range(RING):
                            split_lo(L, n, i)
                    for n in range(FFN_SLOTS, FFN_SLOTS + mixer):
                        if n not in L.shared:
                            split_lo(L, n)
                    with pool.Fori(0, FFN_SLOTS // RING) as i:
                        for n in range(RING):
                            split_lo(L, FFN_SLOTS + mixer + n, i)
            for n in range(TAIL):
                split_lo(Layer(DEPTH, 1), n)

        @block.tensor
        def _(pe):
            def wait_slot(L, n, i=0):
                if n in L.shared:
                    pe.wait_ge(shared_done, L.shares(n))
                else:
                    pe.wait_ge(split_done, L.splits(n) + RING * i)

            def fm_tile(L, n, out, i=0, fresh=None):
                wait_slot(L, n, i)
                r = L.pos[n] % RING
                for k in range(KD):
                    if fresh is not None and k % 2 == 0:
                        wait_drained(pe, L, ("norm", fresh, k // 2))
                    hi, lo = whi[:, r, k * P:(k + 1) * P], wlo[:, r, k * P:(k + 1) * P]
                    pe.matmul(out, hi, thi[:, k, :], start=(k == 0), stop=False)
                    pe.matmul(out, hi, tlo[:, k, :], start=False, stop=False)
                    mm = pe.matmul(out, lo, thi[:, k, :], start=False, stop=(k == KD - 1))
                mm.then_inc(slot_used, 1)

            def tm_pair(L, n, out):
                wait_slot(L, n)
                wait_slot(L, n + 1)
                for T in range(NT):
                    for k in range(KD):
                        r, c = L.pos[n + k // 4] % RING, (k % 4) * GW
                        hi, lo = whi[:, r, c:c + GW], wlo[:, r, c:c + GW]
                        ahi, alo = thi[:, k, T * P:(T + 1) * P], tlo[:, k, T * P:(T + 1) * P]
                        o = out[:, T * GW:(T + 1) * GW]
                        pe.matmul(o, ahi, hi, start=(k == 0), stop=False)
                        pe.matmul(o, alo, hi, start=False, stop=False)
                        mm = pe.matmul(o, ahi, lo, start=False, stop=(k == KD - 1))
                        if T == NT - 1 and k % 4 == 3:
                            mm.then_inc(slot_used, 1)

            def acc_slot(L, n, ahi, alo, acc, first, last, i=0):
                wait_slot(L, n, i)
                r = L.pos[n] % RING
                for half in range(2):
                    for T in range(NT):
                        o = (claim(pe, L, acc(T, half)) if first else psum(L, acc(T, half)))[:]
                        hi, lo = whi[:, r, half * 512:(half + 1) * 512], wlo[:, r, half * 512:(half + 1) * 512]
                        pe.matmul(o, ahi[:, T * P:(T + 1) * P], hi, start=first, stop=False)
                        pe.matmul(o, alo[:, T * P:(T + 1) * P], hi, start=False, stop=False)
                        mm = pe.matmul(o, ahi[:, T * P:(T + 1) * P], lo, start=False, stop=last)
                        if last and (T, half) != (NT - 1, 1):
                            full(L, acc(T, half), mm)
                mm.then_inc(slot_used, 1)

            def turn_pair(L, name, j, source):
                out = claim(pe, L, name)
                for c in range(2):
                    for T in range(NT):
                        k = 2 * j + c
                        mm = pe.transpose(out[:, c * SEQ + T * P:c * SEQ + (T + 1) * P], source[:, T, k * P:(k + 1) * P], ident)
                full(L, name, mm)

            def norm(L, w):
                for j in range(KD // 2):
                    if w == 1 and j < 2:
                        for T in range(NT):
                            pe.wait_ge(ev(f"scaled{T}"), 2 * L.deep + j + 1)
                    if w != 1 and j % 2 == 0:
                        for T in range(NT):
                            updated(pe, L, w, T, j // 2)
                    turn_pair(L, ("norm", w, j), j, x if w != 1 else xs)

            def ffn(L, f):
                base = f * (FFN_SLOTS + (MIX2 if L.blk else MIX1))
                steps0 = (2 * L.deep + f) * STEPS
                accs = lambda T, half: ("acc", f, T, half)

                def gate_up(n, s, turn, i=0):
                    b, k = L.bank(("gu", f, s))
                    pe.wait_ge(bank_read[b], k + turn + 1)
                    fm_tile(L, base + n, bank[b][:, 0:SEQ], i, fresh=2 * f if n == 0 else None)
                    fm_tile(L, base + n + 1, bank[b][:, SEQ:2 * SEQ], i)

                def down(n, step, i=0, first=False, last=False):
                    pe.wait_ge(h_ready, steps0 + step + 1 + 2 * i)
                    c = (step % 2) * SEQ
                    acc_slot(L, base + n, hhi[:, c:c + SEQ], hlo[:, c:c + SEQ], accs, first, last, i)

                gate_up(0, 0, 0)
                out = claim(pe, L, ("R", f))
                pe.wait_ge(ev("diag_ready"), 2 * L.deep + f + 1)
                full(L, ("R", f), pe.matmul(out[:, 0:SEQ], ones[:], diag[:], start=True, stop=True))
                gate_up(2, 1, 0)
                down(4, 0, first=True)
                with pe.Fori(0, STEPS // 2 - 1) as i:
                    gate_up(5, 0, i + 1, i)
                    down(7, 1, i)
                    gate_up(8, 1, i + 1, i)
                    down(10, 2, i)
                down(FFN_SLOTS - 1, STEPS - 1, last=True)

            def project_out(L, first_slot):
                if L.blk:
                    wait_drained(pe, L, ("o", UNITS // 4 - 2))
                else:
                    pe.wait_ge(ev("others_ready"), L.one)
                late = L.order[-1]
                for j in L.order[:-1]:
                    turn_pair(L, ("yT", j), j, xs)
                for n in range(KD):
                    k = 2 * L.order[n // 2] + n % 2
                    if n == KD - 3:
                        if L.blk:
                            wait_drained(pe, L, ("o", UNITS // 4 - 1))
                        else:
                            pe.wait_ge(ev("y_ready"), L.one)
                        turn_pair(L, ("yT", late), late, xs)
                    if n % 2 == 0:
                        wait_drained(pe, L, ("yT", k // 2))
                    acc_slot(L, first_slot + n, thi[:, k, :], tlo[:, k, :], lambda T, half: ("wo", T, half), n == 0, n == KD - 1)

            def unit_scores(L, u, scores):
                out = claim(pe, L, ("s", u))
                pe.matmul(out[:, 0:3 * P], identR[:], maskR[:], start=True, stop=False, skip_group_check=True)
                full(L, ("s", u), scores(u, out))

            def attention(L, units, scores, values, probs, turned, begun=0):
                for u in range(units + 2):
                    if begun <= u < units:
                        unit_scores(L, u, scores)
                    if 1 <= u <= units:
                        out = claim(pe, L, ("pt", u - 1))
                        wait_drained(pe, L, ("s", u - 1))
                        pr = probs((u - 1) % 2)
                        for c in range(3):
                            mm = pe.transpose(out[:, c * P:(c + 1) * P], pr[:, c * P:(c + 1) * P], ident)
                        full(L, ("pt", u - 1), mm)
                    if u >= 2:
                        v = u - 2
                        out = claim(pe, L, ("o", v // 4)) if v % 4 == 0 else psum(L, ("o", v // 4))
                        wait_drained(pe, L, ("pt", v))
                        pt, c = turned(v % 2), (v % 4) * HD
                        pe.matmul(out[:, c:c + HD], pt[:, 0:P], values(v, 0), start=True, stop=True)
                        pe.matmul(out[:, GW + c:GW + c + HD], pt[:, P:2 * P], values(v, 0), start=True, stop=False)
                        mm = pe.matmul(out[:, GW + c:GW + c + HD], pt[:, 2 * P:3 * P], values(v, 1), start=False, stop=True)
                        if v % 4 == 3:
                            full(L, ("o", v // 4), mm)

            def first_mixer(L):
                lrT = m1("lrT", SEQ)
                for m in range(FV):
                    out = claim(pe, L, ("ip", m))
                    n = FFN_SLOTS + 2 * m
                    if m in (ZG, GG, FQ, FK, GV):
                        tm_pair(L, n, out)
                    else:
                        fm_tile(L, n, out[:, 0:SEQ], fresh=1 if m == 0 else None)
                        fm_tile(L, n + 1, out[:, SEQ:2 * SEQ])
                    if m == GK:
                        out = claim(pe, L, "gla_z")
                        wait_drained(pe, L, ("ip", ROWS))
                        pe.wait_ge(s_par, 16 * L.deep + 16)
                        for t in range(2):
                            mm = pe.matmul(out[:, t * SEQ:(t + 1) * SEQ], p1("gup")[0:16, t * P:(t + 1) * P], lrT[0:16, :],
                                           start=True, stop=True)
                        full(L, "gla_z", mm)
                xbcs = m1("xbcs", 6 * SEQ).rearrange("p (t n) -> p t n", t=6)
                out = claim(pe, L, "ssd_xs")
                for m in range(3):
                    pe.wait_ge(ev(f"xbc_act{m}"), L.one)
                for T in range(NT):
                    for t in range(2):
                        mm = pe.transpose(out[:, T * GW + t * P:T * GW + (t + 1) * P], xbcs[:, t, T * P:(T + 1) * P], ident)
                full(L, "ssd_xs", mm)
                out = claim(pe, L, "ssd_b")
                for g in range(2):
                    mm = pe.transpose(out[:, g * P:(g + 1) * P], xbcs[:, 2 + g, 0:P], ident)
                full(L, "ssd_b", mm)
                out = claim(pe, L, "rowsT")
                pe.wait_ge(ev("rowsE"), L.one)
                for c, part in enumerate(("rsp", "rE")):
                    for T in range(NT):
                        q = 2 * c + T
                        mm = pe.transpose(out[:, q * P:(q + 1) * P], m1(part, SEQ)[:, T * P:(T + 1) * P], ident)
                full(L, "rowsT", mm)
                out = claim(pe, L, "gla_kend")
                pe.wait_ge(ev("gla_dec"), L.one)
                kend = m1("kend", 512)
                for T in range(NT):
                    for t in range(2):
                        mm = pe.transpose(out[:, T * GW + t * P:T * GW + (t + 1) * P], kend[:, t * SEQ + T * P:t * SEQ + (T + 1) * P], ident)
                full(L, "gla_kend", mm)
                out = claim(pe, L, "ssd_sc")
                for T in range(NT):
                    for g in range(2):
                        c = (2 * T + g) * P
                        mm = pe.matmul(out[:, c:c + P], xbcs[:, 2 + g, T * P:(T + 1) * P], xbcs[:, 4 + g, T * P:(T + 1) * P],
                                       start=True, stop=True)
                full(L, "ssd_sc", mm)
                DL, DR = m1("DL", SEQ), m1("DR", SEQ)
                for h in range(H):
                    out = claim(pe, L, f"ssd_seg{h}")
                    for T in range(NT):
                        o, rows, tok = out[:, T * P:(T + 1) * P], slice(32 * h, 32 * h + 4), slice(T * P, (T + 1) * P)
                        pe.matmul(o, ident, c_("negT"), start=True, stop=False)
                        mm = pe.matmul(o, DL[rows, tok], DR[rows, tok], start=False, stop=True)
                    full(L, f"ssd_seg{h}", mm)
                gq, gk = m1("gq", 512), m1("gk", 512)
                claim(pe, L, "gla_kv")
                wait_drained(pe, L, "gla_kend")
                wait_drained(pe, L, ("ip", GV))
                for hh in range(2):
                    out = claim(pe, L, f"gla_att{hh}")
                    rows = slice(HD * hh, HD * hh + HD)
                    for T in range(NT):
                        for t in range(2):
                            c, tok = (2 * T + t) * P, slice(t * SEQ + T * P, t * SEQ + (T + 1) * P)
                            mm = pe.matmul(out[:, c:c + P], gk[rows, tok], gq[rows, tok], start=True, stop=True)
                    full(L, f"gla_att{hh}", mm)
                out = psum(L, "gla_kv")
                kendT = m1("kendT", 768).rearrange("p (c n) -> p c n", c=3)
                av, avs = m1("av", 512), m1("avs", 256)
                chunk_v = [av[0:HD, 0:GW], avs[0:HD, :], av[0:HD, GW:2 * GW]]
                for c in range(3):
                    for h in range(H):
                        o = out[HD * (h % 2):HD * (h % 2) + HD, c * P + (h // 2) * HD:c * P + (h // 2) * HD + HD]
                        mm = pe.matmul(o, kendT[0:HD, c, h * HD:(h + 1) * HD], chunk_v[c][:, h * HD:(h + 1) * HD], start=True, stop=True)
                full(L, "gla_kv", mm)
                fqk = m1("fqk", 1024).rearrange("p (c t n) -> p c t n", c=2, t=NT)
                pe.wait_ge(ev("fqk_ready"), L.one)
                for c, name in enumerate(("fox_q", "fox_k")):
                    out = claim(pe, L, name)
                    for T in range(NT):
                        for t in range(2):
                            mm = pe.transpose(out[:, t * SEQ + T * P:t * SEQ + (T + 1) * P], fqk[:, c, T, t * P:(t + 1) * P], ident)
                    full(L, name, mm)
                out = claim(pe, L, "ssd_st")
                wait_drained(pe, L, "ssd_b")
                pe.wait_ge(ev("xd_ready"), L.one)
                for g in range(2):
                    mm = pe.matmul(out[:, g * P:(g + 1) * P], m1("Bt", 256)[:, g * P:(g + 1) * P], m1("xdd", 256)[:, g * P:(g + 1) * P],
                                   start=True, stop=True)
                full(L, "ssd_st", mm)
                out = claim(pe, L, "ssd_y")
                wait_drained(pe, L, "ssd_sc")
                Mt, xd = m1("Mt", 1024), m1("xd", 512)
                for T in range(NT):
                    for h in range(H):
                        c = T * GW + h * HD
                        mm = pe.matmul(out[:, c:c + HD], Mt[:, T * 512 + h * P:T * 512 + (h + 1) * P], xd[:, c:c + HD], start=True, stop=True)
                full(L, "ssd_y", mm)
                out = claim(pe, L, "ssd_yoff")
                wait_drained(pe, L, "ssd_st")
                for g in range(2):
                    mm = pe.matmul(out[:, g * P:(g + 1) * P], xbcs[:, 4 + g, P:2 * P], m1("St", 256)[:, g * P:(g + 1) * P], start=True, stop=True)
                full(L, "ssd_yoff", mm)
                out = claim(pe, L, "gla_o")
                for hh in range(2):
                    wait_drained(pe, L, f"gla_att{hh}")
                pe.wait_ge(ev("gla_states"), L.one)
                attT, Sbd = m1("attT", 1024), m1("Sbd", 768)
                for T in range(NT):
                    for h in range(H):
                        hh, t = h % 2, h // 2
                        c, a = T * GW + h * HD, hh * 512 + (2 * T + t) * P
                        pe.matmul(out[:, c:c + HD], attT[:, a:a + P], av[:, c:c + HD], start=(T == 0 and h == 0), stop=False,
                                  skip_group_check=True)
                    for t in range(2):
                        for half in range(2):
                            chunk = 2 * T + half
                            if chunk:
                                c, tok, s = T * GW + t * P, t * SEQ + chunk * HD, ((chunk - 1) * 2 + t) * P
                                mm = pe.matmul(out[HD * half:HD * half + HD, c:c + P], gq[:, tok:tok + HD], Sbd[:, s:s + P],
                                               start=False, stop=(half == 1), skip_group_check=True)
                full(L, "gla_o", mm)
                out = claim(pe, L, "sc_t")
                pe.wait_ge(ev("dy_ready"), L.one)
                dy = m1("dy", 512)
                for T in range(NT):
                    for t in range(2):
                        mm = pe.transpose(out[:, T * GW + t * P:T * GW + (t + 1) * P], dy[:, t * SEQ + T * P:t * SEQ + (T + 1) * P], ident)
                full(L, "sc_t", mm)

                fT = m1("fT", 1024).rearrange("p (c t n) -> p c t n", c=2, t=2)
                FL, FR, bv = m1("FL", 4 * SEQ), m1("FR", SEQ), m1("bv", 512)

                def scores(u, out):
                    rows, t, f = slice(HD * (u % 2), HD * (u % 2) + HD), u // 2, u * SEQ
                    pe.matmul(out[:, 0:P], fT[rows, 0, t, 0:P], fT[rows, 1, t, 0:P], start=False, stop=False, skip_group_check=True)
                    pe.matmul(out[:, 0:P], FL[:, f:f + P], FR[:, 0:P], start=False, stop=False, skip_group_check=True)
                    pe.matmul(out[:, P:3 * P], fT[rows, 0, t, P:2 * P], fT[rows, 1, t, :], start=False, stop=False, skip_group_check=True)
                    return pe.matmul(out[:, P:3 * P], FL[:, f + P:f + 2 * P], FR[:], start=False, stop=True, skip_group_check=True)

                wait_drained(pe, L, "fox_q")
                wait_drained(pe, L, "fox_k")
                pe.wait_ge(ev("FL_ready"), L.one)
                pe.wait_ge(ev("mask_ready"), L.each)
                for u in range(2):
                    unit_scores(L, u, scores)
                tm_pair(L, FFN_SLOTS + 2 * FV, claim(pe, L, ("ip", FV)))

                def values(u, T):
                    wait_drained(pe, L, ("ip", FV))
                    return bv[:, T * GW + u * HD:T * GW + (u + 1) * HD]

                attention(L, H, scores, values,
                          lambda s: m1("P", 768)[:, s * 384:(s + 1) * 384], lambda s: m1("pt", 768)[:, s * 384:(s + 1) * 384], begun=2)
                project_out(L, FFN_SLOTS + 2 * IP1)

            def second_mixer(L):
                def rotate(m):
                    out = claim(pe, L, ("rot", m))
                    wait_drained(pe, L, ("ip", m))
                    full(L, ("rot", m), pe.matmul(out[:], c_("ropeR"), raw_of(m), start=True, stop=True))

                kr, qr, mqr, mkr = m2("kr", 512), m2("qr", 1024), m2("mqr", 1024), m2("mkr", 1024)
                vsw, mv = m2("vsw", 512), m2("mv", 1024)

                def scores(u, out):
                    kind, h = u // 8, u % 8
                    if kind == 2:
                        pe.wait_ge(ev("roped"), L.one)
                    if kind < 2:
                        rows, q, k = slice(HD * (h // 4), HD * (h // 4) + HD), qr[:, (h % 4) * SEQ:(h % 4 + 1) * SEQ], kr[:, kind * SEQ:(kind + 1) * SEQ]
                    else:
                        rows, t = slice(HD * (h % 2), HD * (h % 2) + HD), h // 2
                        q, k = mqr[:, t * SEQ:(t + 1) * SEQ], mkr[:, t * SEQ:(t + 1) * SEQ]
                    pe.matmul(out[:, 0:P], q[rows, 0:P], k[rows, 0:P], start=False, stop=False, skip_group_check=True)
                    return pe.matmul(out[:, P:3 * P], q[rows, P:2 * P], k[rows, :], start=False, stop=True, skip_group_check=True)

                def values(u, T):
                    kind, h = u // 8, u % 8
                    if kind == 2:
                        wait_drained(pe, L, ("ip", MV1))
                    if kind < 2:
                        c = T * GW + kind * P + (h // 4) * HD
                        return vsw[:, c:c + HD]
                    return mv[:, (h // 4) * 512 + T * GW + (h % 4) * HD:(h // 4) * 512 + T * GW + (h % 4 + 1) * HD]

                for m in range(IP2 + 1):
                    if m == MV1:
                        pe.wait_ge(ev("mask_ready"), L.each)
                        pe.wait_ge(ev("first_roped"), L.one)
                        for u in range(2):
                            unit_scores(L, u, scores)
                    out = claim(pe, L, ("ip", m))
                    n, _ = pair_slots(m)
                    if m in (VSW, MV0, MV1):
                        tm_pair(L, n, out)
                    elif m == GATES:
                        fm_tile(L, n, out[:, 0:SEQ])
                    else:
                        fm_tile(L, n, out[:, 0:SEQ], fresh=1 if m == 0 else None)
                        fm_tile(L, n + 1, out[:, SEQ:2 * SEQ])
                    if m - 1 in ROPED:
                        rotate(m - 1)
                    if m == GATES:
                        for c in range(2):
                            out = claim(pe, L, ("hid", c))[0:2 * NCMP, 0:256]
                            pe.wait_ge(ev(f"blk_ready{c}"), L.one)
                            for s in range(CMP_SLOTS):
                                n = CMP0 + c * CMP_SLOTS + s
                                wait_slot(L, n)
                                r = L.pos[n] % RING
                                for k in range(NCT // CMP_SLOTS):
                                    step = s * (NCT // CMP_SLOTS) + k
                                    hi, lo = whi[:, r, k * 256:(k + 1) * 256], wlo[:, r, k * 256:(k + 1) * 256]
                                    block = slice((c * NCT + step) * 2 * NCMP, (c * NCT + step + 1) * 2 * NCMP)
                                    pe.matmul(out, hhi[:, block], hi, start=(step == 0), stop=False)
                                    pe.matmul(out, hlo[:, block], hi, start=False, stop=False)
                                    mm = pe.matmul(out, hhi[:, block], lo, start=False, stop=(step == NCT - 1))
                                mm.then_inc(slot_used, 1)
                    if m == VSW:
                        out = claim(pe, L, "hidf")
                        wait_drained(pe, L, ("ip", GATES))
                        for T in range(NT):
                            pe.matmul(out[:, 128 + T * 32:160 + T * 32], m2("gex", SEQ)[0:HD, T * P:(T + 1) * P], ident[0:HD, 0:32], start=True, stop=True)
                        for c in range(2):
                            wait_drained(pe, L, ("hid", c))
                            for t in range(2):
                                col = (2 * c + t) * 32
                                mm = pe.matmul(out[:, col:col + 32], m2("hidT", 512)[0:HD, c * 256 + t * P:c * 256 + (t + 1) * P], ident[0:HD, 0:32],
                                               start=True, stop=True)
                        full(L, "hidf", mm)
                    if m == MQ0:
                        pe.wait_ge(s_par, 16 * L.deep + 16)
                        out = claim(pe, L, "kc")
                        pe.wait_ge(ev("gelu0"), L.one)
                        for t in range(2):
                            mm = pe.matmul(out[:, 0:2 * NCMP], p2("ck2")[:, t * P:(t + 1) * P], m2("hk", 64)[:, t * 32:t * 32 + 2 * NCMP],
                                           start=(t == 0), stop=(t == 1))
                        full(L, "kc", mm)
                        out = claim(pe, L, "vc")
                        pe.wait_ge(ev("gelu1"), L.one)
                        for t in range(2):
                            mm = pe.matmul(out[:, 0:HD], m2("hvr", 256)[:, t * P:(t + 1) * P], p2("cv2")[:, t * HD:(t + 1) * HD],
                                           start=(t == 0), stop=(t == 1))
                        full(L, "vc", mm)
                    if m == MQ1:
                        out = claim(pe, L, "cmp_s")
                        wait_drained(pe, L, "kc")
                        qraw = m2("qraw", 1024)
                        pe.matmul(out[:, 0:256], ident, c_("cmpmask"), start=True, stop=False, skip_group_check=True)
                        for T in range(NT):
                            for r in range(4):
                                c = (T * 4 + r) * 32
                                mm = pe.matmul(out[:, c:c + 32], qraw[:, r * SEQ + T * P:r * SEQ + (T + 1) * P], m2("kc", 32),
                                               start=False, stop=(T == 1 and r == 3), skip_group_check=True)
                        full(L, "cmp_s", mm)
                    if m == MK0:
                        out = claim(pe, L, "cmp_pt")
                        pe.wait_ge(ev("cmp_exp"), L.one)
                        for T in range(NT):
                            mm = pe.transpose(out[:, T * P:(T + 1) * P], m2("cs", 256)[:, T * P:(T + 1) * P], ident)
                        full(L, "cmp_pt", mm)
                    if m == MK1:
                        wait_drained(pe, L, "vc")
                        wait_drained(pe, L, "cmp_pt")
                        for T in range(NT):
                            out = claim(pe, L, f"cmp_o{T}")
                            full(L, f"cmp_o{T}", pe.matmul(out[:], m2("cpT", 256)[:, T * P:(T + 1) * P], m2("vcd", 512), start=True, stop=True))

                attention(L, UNITS, scores, values, lambda s: m2("P", 768)[:, s * 384:(s + 1) * 384],
                          lambda s: m2("pt", 768)[:, s * 384:(s + 1) * 384], begun=2)
                project_out(L, FFN_SLOTS + 2 * IP2 + 1 + 2 * CMP_SLOTS)

            pe.sem_inc(slot_used, RING)
            pe.wait_ge(s_con, 16)
            pe.wait_ge(s_x, 16)
            pe.wait_ge(ones_set, 1)
            for blk, mixer in enumerate((first_mixer, second_mixer)):
                with pe.Fori(0, DEPTH) as l:
                    L = Layer(l, blk)
                    norm(L, 0)
                    ffn(L, 0)
                    norm(L, 1)
                    mixer(L)
                    norm(L, 2)
                    ffn(L, 1)

        @block.scalar
        def _(act):
            def split_hi(L, n, i=0):
                place, uses = L.raw_use(n)
                act.wait_ge(s_raw[place], 16 * uses + 16 * i + 16)
                act.wait_ge(slot_used, L.slot0 + (L.before(n) + 1 + RING) + RING * i)
                nc.scalar.copy(whi[:, place, :], raw[:, place, :]).then_inc(hi_done, 1)

            def squares(L, w, half):
                for T in range(NT):
                    updated(act, L, w, T, half)
                    h = slice(half * 512, half * 512 + 512)
                    c = P + NT * half + T
                    nc.scalar.activation(xs[:, T, h], x[:, T, h], ACT.Square, scale=D ** -0.5,
                                     accum_out=stat[:, c:c + 1]).then_inc(sq_done, 1)

            def norm(L, w):
                act.wait_ge(s_gain, 16 * L.deep + 16)
                squares(L, w, 0)
                if w == 1:
                    squares(L, w, 1)
                    split_hi(L, FFN_SLOTS)
                    split_hi(L, FFN_SLOTS + 1)
                    act.wait_ge(ev("root_ready"), L.each)
                    for cols in (slice(0, GW), slice(GW, D)):
                        nc.scalar.activation(xs[:, 1, cols], x[:, 1, cols], ACT.Copy, scale=stat[:, 33:34]).then_inc(ev("scaled1"), 1)
                    split_hi(L, FFN_SLOTS + 2)
                for j in range(KD // 2):
                    wait_full(act, L, ("norm", w, j))
                    for c in range(2):
                        k = 2 * j + c
                        nc.scalar.activation(thi[:, k, :], psum(L, ("norm", w, j))[:, c * SEQ:(c + 1) * SEQ], ACT.Copy,
                                             scale=gain_of(L, w, k)).then_inc(thi_done, 1)
                if w == 1:
                    split_hi(L, FFN_SLOTS + 3)
                else:
                    squares(L, w, 1)
                    split_hi(L, ffn_slot(L, w))

            def ffn(L, f):
                base = f * (FFN_SLOTS + (MIX2 if L.blk else MIX1))
                steps0 = (2 * L.deep + f) * STEPS
                nc.scalar.preload_act_table_set("silu_and_others")

                def step(s, j, turn, between, behind, i=0):
                    c = s * SEQ
                    b, k = L.bank(("gu", f, s))
                    act.wait_ge(bank_read[b], k + turn + 2)
                    nc.scalar.activation(gu[:, s, 0, :], gu[:, s, 0, :], ACT.Silu).then_inc(sg_done, 1)
                    for n in between:
                        split_hi(L, base + n, i)
                    act.wait_ge(hf_done, steps0 + (j + 1) + 2 * i)
                    nc.scalar.copy(hhi[:, c:c + SEQ], gu[:, s, 1, :]).then_inc(hhi_done, 1)
                    for n in behind:
                        split_hi(L, base + n, i)

                wait_full(act, L, ("R", f))
                drained(L, ("R", f), nc.scalar.copy(root[:], psum(L, ("R", f))[:, 0:SEQ]))
                step(0, 0, 0, (), (5, 6))
                step(1, 1, 0, (7,), (8, 9))
                with act.Fori(0, STEPS // 2 - 2) as i:
                    step(0, 2, i + 1, (10,), (11, 12), i)
                    step(1, 3, i + 1, (13,), (14, 15), i)
                n = FFN_SLOTS
                step(0, STEPS - 2, STEPS // 2 - 1, (n - 2,), (n - 1, n) if f else (n - 1,))
                step(1, STEPS - 1, STEPS // 2 - 1, (), (n + 1, n + 2, n + 3) if f else ())

            def exps(L, u, scale, rows, units, probs, per_layer, nm):
                s = u % 2
                act.wait_ge(sm_max, L.blk * DEPTH * H + L.l * per_layer + (u + 1))
                S, pr = psum(L, ("s", u)), probs[:, s * 384:(s + 1) * 384]
                nc.scalar.activation(pr[:, 0:P], S[:, 0:P], ACT.Exp, scale=scale, bias=nm[:, 2 * s:2 * s + 1], accum_out=rows[:, u:u + 1])
                drained(L, ("s", u), nc.scalar.activation(pr[:, P:3 * P], S[:, P:3 * P], ACT.Exp, scale=scale,
                                                          bias=nm[:, 2 * s + 1:2 * s + 2], accum_out=rows[:, units + u:units + u + 1]))

            def first_mixer(L, own):
                xbcu = m1("xbcu", 6 * 260).rearrange("p (t n) -> p t n", t=6)
                xbcs = m1("xbcs", 6 * SEQ).rearrange("p (t n) -> p t n", t=6)
                keep = {GQ: m1("gq", 512), GK: m1("gk", 512), FQ: m1("fqk", 1024)[:, 0:512], FK: m1("fqk", 1024)[:, 512:1024],
                        GV: m1("av", 512), FV: m1("bv", 512), DC: m1("dc", 512), DB: m1("db", 512)}
                act.wait_ge(s_par, 16 * L.deep + 16)
                for m in range(FV):
                    out = psum(L, ("ip", m))
                    if m not in (ROWS, DV):
                        wait_full(act, L, ("ip", m))
                    if m <= XBC2:
                        drained(L, ("ip", m), nc.scalar.copy(xbcu[:, 2 * m:2 * m + 2, 3:3 + SEQ], out[:].rearrange("p (t n) -> p t n", t=2)))
                    elif m in (ZG, GG):
                        drained(L, ("ip", m), nc.scalar.activation(m1("siluz" if m == ZG else "silug", 512), out[:], ACT.Silu))
                    elif m in keep:
                        if m == GV:
                            nc.scalar.copy(m1("avs", 256)[0:HD, :], out[HD:2 * HD, 0:GW])
                        drained(L, ("ip", m), nc.scalar.copy(keep[m], out[:]))
                    for n in (2 * m + 4, 2 * m + 5):
                        split_hi(L, FFN_SLOTS + n)
                    if 1 <= m <= 3:
                        act.wait_ge(ev(f"conv{m - 1}"), L.one)
                        for t in (2 * m - 2, 2 * m - 1):
                            ins = nc.scalar.activation(xbcs[:, t, :], xbcs[:, t, :], ACT.Silu, bias=p1("convb")[:, t:t + 1])
                        ins.then_inc(ev(f"xbc_act{m - 1}"), 1)
                    if m == GG:
                        nc.scalar.preload_act_table_set("natural_log_exp_and_others")
                    if m == ROWS:
                        act.wait_ge(ev("rows_na"), L.one)
                        nc.scalar.activation(m1("ralogx", 1), p1("ralog"), ACT.Exp)
                        nc.scalar.activation(m1("re", SEQ), m1("re", SEQ), ACT.Exp).then_inc(ev("rows_e"), 1)
                    if m == FK:
                        act.wait_ge(ev("rows_cs"), L.one)
                        rcs, rE = m1("rcs", SEQ), m1("rE", SEQ)
                        nc.scalar.activation(rE[:, 0:P], rcs[:, 0:P], ACT.Exp, scale=-1.0, bias=rcs[:, P - 1:P])
                        nc.scalar.activation(rE[:, P:2 * P], rcs[:, P:2 * P], ACT.Exp).then_inc(ev("rowsE"), 1)
                    if m == FQ:
                        act.wait_ge(ev("z_na"), L.one)
                        ge = m1("ge", 512)
                        own.link(nc.scalar.activation(ge, ge, ACT.Exp))
                        nc.scalar.activation(ge, ge, ACT.Ln, bias=1.0).then_inc(ev("z_l"), 1)
                    if m == FK:
                        act.wait_ge(ev("gla_b"), L.one)
                        gb, gd = m1("gb", 512), m1("gd", 512)
                        nc.scalar.activation(m1("eb", 512), gb, ACT.Exp, scale=1.0 / 16)
                        nc.scalar.activation(m1("enb", 512), gb, ACT.Exp, scale=-1.0 / 16)
                        nc.scalar.activation(gd, gd, ACT.Exp, scale=1.0 / 16).then_inc(ev("gla_exp"), 1)

                def take(name, dst, src, func=None):
                    wait_full(act, L, name)
                    drained(L, name, nc.scalar.activation(dst, src, func) if func else nc.scalar.copy(dst, src))

                take("ssd_b", m1("Bt", 256), psum(L, "ssd_b")[:, 0:256])
                kend, kendT = psum(L, "gla_kend"), m1("kendT", 768).rearrange("p (c n) -> p c n", c=3)
                wait_full(act, L, "gla_kend")
                for c in range(2):
                    nc.scalar.copy(kendT[0:HD, c, :], kend[HD * c:HD * c + HD, 0:GW])
                drained(L, "gla_kend", nc.scalar.copy(kendT[0:HD, 2, :], kend[0:HD, GW:2 * GW]))
                for h in range(H):
                    take(f"ssd_seg{h}", m1("Lm", 1024).rearrange("p (t h n) -> p t h n", t=NT, h=H)[:, :, h, :],
                         psum(L, f"ssd_seg{h}")[:, 0:2 * P].rearrange("p (t n) -> p t n", t=NT), ACT.Exp)
                take("fox_q", m1("fT", 1024)[:, 0:512], psum(L, "fox_q")[:])
                take("fox_k", m1("fT", 1024)[:, 512:1024], psum(L, "fox_k")[:])
                take("ssd_st", m1("St", 256), psum(L, "ssd_st")[:, 0:256])
                for name, c in (("gla_o", 0), ("sc_t", 3 * GW)):
                    take(name, xs[:, :, c:c + GW], psum(L, name)[:].rearrange("p (t n) -> p t n", t=NT))
                for u in range(H):
                    exps(L, u, 1.0, m1("rowsum", 8), H, m1("P", 768), H, m1("nm", 4))
                    if u == 1:
                        take(("ip", FV), keep[FV], psum(L, ("ip", FV))[:])
                        for n in (2 * FV + 4, 2 * FV + 5):
                            split_hi(L, FFN_SLOTS + n)
                for u in range(2, H):
                    take(("pt", u), m1("pt", 768)[:, (u % 2) * 384:(u % 2 + 1) * 384], psum(L, ("pt", u))[:, 0:384])
                finish(L, FFN_SLOTS + MIX1)

            def finish(L, end):
                def upper_half(j):
                    wait_full(act, L, ("yT", j))
                    nc.scalar.copy(thi[:, 2 * j:2 * j + 2, :], psum(L, ("yT", j))[:].rearrange("p (k n) -> p k n", k=2)).then_inc(thi_done, 1)

                for j in L.order[:-1]:
                    upper_half(j)
                for n in range(end - 4, end):
                    split_hi(L, n)
                upper_half(L.order[-1])
                for n in range(end, end + AHEAD):
                    split_hi(L, n)

            def second_mixer(L, own):
                nc.scalar.preload_act_table_set("exp_and_others")
                kx = m2("kx", 1024).rearrange("p (c g n) -> p c g n", c=2, g=2)
                keep = {VSW: m2("vsw", 512), MV0: m2("mv", 1024)[:, 0:512], MV1: m2("mv", 1024)[:, 512:1024]}
                unit_exps = lambda u: exps(L, u, SCALE, m2("rowsum", 2 * UNITS), UNITS, m2("P", 768), UNITS, m2("nm", 4))
                ahead = FFN_SLOTS + AHEAD
                for m in range(IP2 + 1):
                    if m == MV1:
                        for u in range(2):
                            unit_exps(u)
                    out = psum(L, ("ip", m))
                    wait_full(act, L, ("ip", m))
                    if m == KVC:
                        src = out[:].rearrange("p (c n) -> p c n", c=2)
                        for g in range(2):
                            nc.scalar.copy(kx[0:HD, :, g, :], src[HD * g:HD * g + HD, :, :])
                            ins = nc.scalar.copy(kx[HD:P, :, g, 0:SEQ - 1], src[HD * g:HD * g + HD, :, 1:SEQ])
                        drained(L, ("ip", m), ins)
                    elif m in ROPED:
                        if m in (MQ1, MK0, MK1):
                            wait_drained(act, L, ("rot", {MQ1: KSW, MK0: MQ0, MK1: MQ1}[m]))
                        drained(L, ("ip", m), nc.scalar.copy(raw_of(m), out[:]))
                    elif m == GATES:
                        drained(L, ("ip", m), nc.scalar.activation(m2("gex", SEQ)[0:HD, :], out[0:HD, 0:SEQ], ACT.Exp, scale=-1.0))
                    else:
                        drained(L, ("ip", m), nc.scalar.copy(keep[m], out[:]))
                    end = sum(pair_slots(m)) + AHEAD
                    for n in range(ahead, end if m != GATES else CMP0 + 2 * CMP_SLOTS + AHEAD):
                        split_hi(L, n)
                        ahead = n + 1
                    if m in (Q0, Q1):
                        c = m - Q0
                        act.wait_ge(ev(f"blk{c}"), L.one)
                        nc.scalar.copy(hhi[:, c * 480:(c + 1) * 480], m2("blk", 960)[:, c * 480:(c + 1) * 480]).then_inc(ev(f"blk_hi{c}"), 1)
                    if m == VSW:
                        act.wait_ge(ev("gelu_in"), L.one)
                        nc.scalar.activation(m2("he", 128), m2("hu", 128), ACT.Exp, scale=-2.0 * (2.0 / np.pi) ** 0.5).then_inc(ev("gelu_e"), 1)
                    if m == MQ1:
                        wait_drained(act, L, "cmp_s")
                        nc.scalar.activation(m2("cs", 256), m2("cs", 256), ACT.Exp, scale=SCALE).then_inc(ev("cmp_exp"), 1)
                    if m == MK0:
                        wait_full(act, L, "cmp_pt")
                        drained(L, "cmp_pt", nc.scalar.copy(m2("cpT", 256), psum(L, "cmp_pt")[:, 0:256]))
                for u in range(2, UNITS):
                    unit_exps(u)
                finish(L, FFN_SLOTS + MIX2)

            for n in range(AHEAD):
                split_hi(Layer(0, 0), n)
            nc.scalar.dma_start(con[:, P:CON_W], con_d[:, P:CON_W]).then_inc(s_rest, 16)
            act.wait_ge(s_x, 16)
            for blk, mixer in enumerate((first_mixer, second_mixer)):
                with act.Fori(0, DEPTH) as l:
                    L = Layer(l, blk)
                    own = Own(act, act_own, L)
                    norm(L, 0)
                    ffn(L, 0)
                    norm(L, 1)
                    mixer(L, own)
                    norm(L, 2)
                    ffn(L, 1)
                    own.close()
            for half in range(2):
                squares(Layer(DEPTH, 1), 0, half)

        @block.vector
        def _(dve):
            def split_shared(L, n):
                place, _ = L.raw_use(n)
                dve.wait_ge(hi_done, L.slot0 + (n + 1))
                dve.tensor_tensor(wlo[:, place, :], raw[:, place, :], whi[:, place, :].bitcast(F32), ALU.subtract).then_inc(shared_done, 1)

            def inverse_root(own, sums, n, count):
                v, y, t, vh = (stat[:, 32 * i:32 * i + n] for i in range(4))
                own.link(dve.tensor_scalar(v, sums, 1.0 / count, EPS, ALU.mult, ALU.add))
                own.step(dve.tensor_scalar(vh, v, -0.5, None, ALU.mult))
                own.link(dve.tensor_scalar(t.bitcast(I32), v.bitcast(I32), 1, None, ALU.logical_shift_right))
                own.link(dve.tensor_scalar(y.bitcast(I32), t.bitcast(I32), -1.0, float(0x5f3759df), ALU.mult, ALU.add))
                for step in range(3):
                    own.link(dve.tensor_tensor(t, y, y, ALU.mult))
                    own.link(dve.tensor_tensor(t, t, vh, ALU.mult))
                    own.link(dve.scalar_tensor_tensor(y, t, 1.5, y, ALU.add, ALU.mult))
                return y

            def roots(L, own, w, ready=None):
                dve.wait_ge(sq_done, L.deep * (6 * NT) + (w + 1) * 2 * NT)
                v, y, t, vh = (stat[:, 32 * i:32 * i + NT] for i in range(4))
                own.link(dve.scalar_tensor_tensor(v, stat[:, P:P + NT], EPS, stat[:, P + NT:P + 2 * NT], ALU.add, ALU.add))
                own.step(dve.tensor_scalar(vh, v, -0.5, None, ALU.mult))
                own.link(dve.tensor_scalar(t.bitcast(I32), v.bitcast(I32), 1, None, ALU.logical_shift_right))
                own.link(dve.tensor_scalar(y.bitcast(I32), t.bitcast(I32), -1.0, float(0x5f3759df), ALU.mult, ALU.add))
                for step in range(3):
                    for T in range(NT):
                        c = slice(T, T + 1)
                        own.step(dve.scalar_tensor_tensor(t[:, c], y[:, c], vh[:, c], y[:, c], ALU.mult, ALU.mult))
                    own.wait()
                    ins = dve.scalar_tensor_tensor(y, t, 1.5, y, ALU.add, ALU.mult)
                    if step == 2 and ready is not None:
                        ins.then_inc(ready, 1)
                        dve.wait_ge(ready, own.L.each)
                    else:
                        own.link(ins)
                return y

            def remainders(L, w):
                for j in range(KD // 2):
                    dve.wait_ge(thi_done, 28 * L.deep + ((0, 8, 20)[w] + 2 * j + 2))
                    for c in range(2):
                        k = 2 * j + c
                        ins = dve.scalar_tensor_tensor(tlo[:, k, :], psum(L, ("norm", w, j))[:, c * SEQ:(c + 1) * SEQ], gain_of(L, w, k),
                                                       thi[:, k, :].bitcast(F32), ALU.mult, ALU.subtract)
                    drained(L, ("norm", w, j), ins)

            def norm(L, own, w):
                if w == 1:
                    rstd = roots(L, own, w, ev("root_ready"))
                    for cols in (slice(0, GW), slice(GW, D)):
                        dve.tensor_scalar(xs[:, 0, cols], x[:, 0, cols], rstd[:, 0:1], None, ALU.mult).then_inc(ev("scaled0"), 1)
                    split_shared(L, FFN_SLOTS)
                    remainders(L, w)
                    split_shared(L, FFN_SLOTS + 2)
                else:
                    remainders(L, w)
                    rstd = roots(L, own, w)
                    for T in range(NT):
                        ins = dve.tensor_scalar(diag[:, T * P:(T + 1) * P], ident, rstd[:, T:T + 1], None, ALU.mult)
                    ins.then_inc(ev("diag_ready"), 1)

            def add_to_x(L, name, factor):
                for half in range(2):
                    for T in range(NT):
                        wait_full(dve, L, name(T, half))
                        part = x[:, T, half * 512:(half + 1) * 512]
                        drained(L, name(T, half), dve.scalar_tensor_tensor(part, psum(L, name(T, half))[:], factor, part, ALU.mult, ALU.add))

            def ffn(L, f):
                base = f * (FFN_SLOTS + (MIX2 if L.blk else MIX1))
                steps0 = (2 * L.deep + f) * STEPS

                def step(s, j, up, i=0):
                    c = s * SEQ
                    b = L.bank(("gu", f, s))[0]
                    dve.wait_ge(slot_used, L.slot0 + (base + up + 1 + RING) + RING * i)
                    dve.tensor_tensor(gu[:, s], bank[b][:].rearrange("p (c n) -> p c n", c=2), root[:].unsqueeze(1).to_broadcast([P, 2, SEQ]),
                                      ALU.mult).then_inc(bank_read[b], 1)
                    dve.wait_ge(sg_done, steps0 + (j + 1) + 2 * i)
                    dve.tensor_tensor(gu[:, s, 1, :], gu[:, s, 0, :], gu[:, s, 1, :], ALU.mult).then_inc(hf_done, 1)
                    dve.wait_ge(hhi_done, steps0 + (j + 1) + 2 * i)
                    dve.tensor_tensor(hlo[:, c:c + SEQ], gu[:, s, 1, :], hhi[:, c:c + SEQ].bitcast(F32), ALU.subtract).then_inc(h_ready, 1)

                wait_drained(dve, L, ("R", f))
                step(0, 0, 1)
                step(1, 1, 3)
                with dve.Fori(0, STEPS // 2 - 2) as i:
                    step(0, 2, 6, i)
                    step(1, 3, 9, i)
                step(0, STEPS - 2, FFN_SLOTS - 6)
                step(1, STEPS - 1, FFN_SLOTS - 3)
                add_to_x(L, lambda T, half: ("acc", f, T, half), 0.5)

            def maxima(L, own, u, scale, mx, nm):
                s = u % 2
                wait_full(dve, L, ("s", u))
                S = psum(L, ("s", u))
                own.step(dve.tensor_reduce(mx[:, 2 * s:2 * s + 1], S[:, 0:P], AX, ALU.max))
                own.link(dve.tensor_reduce(mx[:, 2 * s + 1:2 * s + 2], S[:, P:3 * P], AX, ALU.max))
                dve.tensor_scalar(nm[:, 2 * s:2 * s + 2], mx[:, 2 * s:2 * s + 2], -scale, None, ALU.mult).then_inc(sm_max, 1)

            def keep_turned(L, u, pt):
                wait_full(dve, L, ("pt", u))
                s = u % 2
                drained(L, ("pt", u), dve.tensor_copy(pt[:, s * 384:(s + 1) * 384], psum(L, ("pt", u))[:, 0:384]))

            def y_remainders(L, first, last):
                for i in range(first, last):
                    j = L.order[i]
                    pair = slice(2 * j, 2 * j + 2)
                    dve.wait_ge(thi_done, 28 * L.deep + (16 + i + 1))
                    drained(L, ("yT", j), dve.tensor_tensor(tlo[:, pair, :], psum(L, ("yT", j))[:].rearrange("p (k n) -> p k n", k=2),
                                                            thi[:, pair, :].bitcast(F32), ALU.subtract))

            def finish(L):
                add_to_x(L, lambda T, half: ("wo", T, half), 1.0)

            def bc(ap, shape):
                return ap.to_broadcast(shape)

            def set_masks():
                dve.wait_ge(s_rest, 16)
                dve.tensor_copy(identR[:], ident)
                for c in (0, 2):
                    dve.tensor_copy(maskR[:, c * P:(c + 1) * P], c_("negq"))
                dve.tensor_scalar(maskR[:, P:2 * P], ident, 0.0, None, ALU.mult).then_inc(ev("mask_ready"), 1)

            def convolve(own, dst, src, weights, taps):
                for k in range(taps):
                    for t, d in enumerate(dst):
                        s, w = src[t][:, k:k + SEQ], weights[:, t * taps + k:t * taps + k + 1]
                        if k == 0:
                            ins = dve.tensor_scalar(d, s, w, None, ALU.mult)
                        else:
                            ins = dve.scalar_tensor_tensor(d, s, w, d, ALU.mult, ALU.add)
                        if k < taps - 1:
                            own.step(ins)
                    if k < taps - 1:
                        own.wait()
                return ins

            def first_mixer(L, own):
                xbcu = m1("xbcu", 6 * 260).rearrange("p (t n) -> p t n", t=6)
                xbcs = m1("xbcs", 6 * SEQ).rearrange("p (t n) -> p t n", t=6)
                dcu = m1("dcu", 520).rearrange("p (t n) -> p t n", t=2)
                sel = c_("sel")
                zb, ge, gb, gd = m1("zb", 512), m1("ge", 512), m1("gb", 512), m1("gd", 512)
                gq, gk = m1("gq", 512), m1("gk", 512)
                ru, re, rs, rs2, rp, rsp, rcs = (m1(n, SEQ) for n in ("ru", "re", "rs", "rs2", "rp", "rsp", "rcs"))
                rows_bank = psum(L, ("ip", ROWS))
                set_masks()
                own.link(dve.memset(xbcu[:, :, 0:3], 0.0))
                dve.wait_ge(s_par, 16 * L.deep + 16)
                for m in range(FV):
                    if m + 1 in (ZG, GV):
                        split_shared(L, FFN_SLOTS + 2 * (m + 1))
                    if m == ROWS:
                        wait_full(dve, L, ("ip", ROWS))
                        dve.tensor_copy(m1("lrT", SEQ)[0:16, :], rows_bank[0:16, 0:SEQ])
                        drained(L, ("ip", ROWS), dve.tensor_scalar(ru, rows_bank[:, SEQ:2 * SEQ], p1("rbias"), sel[:, 0:1], ALU.add, ALU.mult))
                    if m == DV:
                        own.link(dve.memset(dcu[:, :, 0:2], 0.0))
                        wait_full(dve, L, ("ip", DV))
                        wait_drained(dve, L, ("ip", DC))
                        drained(L, ("ip", DV), dve.tensor_tensor(dcu[:, :, 2:2 + SEQ], m1("dc", 512).rearrange("p (t n) -> p t n", t=2),
                                                                 psum(L, ("ip", DV))[:].rearrange("p (t n) -> p t n", t=2), ALU.mult))
                    if m <= XBC2:
                        wait_drained(dve, L, ("ip", m))
                        tiles = (2 * m, 2 * m + 1)
                        convolve(own, [xbcs[:, t, :] for t in tiles], [xbcu[:, t, :] for t in tiles],
                                 p1("convw")[:, 8 * m:8 * m + 8], 4).then_inc(ev(f"conv{m}"), 1)
                    if m == ROWS:
                        wait_drained(dve, L, ("ip", ROWS))
                        dve.scalar_tensor_tensor(re, ru, -1.0, ru, ALU.mult, ALU.min).then_inc(ev("rows_na"), 1)
                    if m == GQ:
                        dve.wait_ge(ev("rows_e"), L.one)
                        own.link(dve.tensor_scalar(rs, re, 2.0, None, ALU.add))
                        own.link(dve.reciprocal(rs, rs))
                        own.link(dve.tensor_tensor(rs, rs, re, ALU.mult))
                        own.link(dve.tensor_tensor(rs2, rs, rs, ALU.mult))
                        own.link(dve.tensor_scalar(rp, rs2, 1.0 / 17, None, ALU.mult))
                    if m == GK:
                        for odd in (15, 13, 11, 9, 7, 5, 3):
                            own.link(dve.scalar_tensor_tensor(rp, rp, 1.0 / odd, rs2, ALU.add, ALU.mult))
                        own.link(dve.scalar_tensor_tensor(rp, rp, 1.0, rs, ALU.add, ALU.mult))
                    if m == FQ:
                        own.step(dve.tensor_scalar(ru, ru, 0.0, None, ALU.max))
                        own.link(dve.tensor_scalar(rp, rp, 2.0, None, ALU.mult))
                        own.link(dve.tensor_tensor(rsp, rp, ru, ALU.add))
                        own.link(dve.tensor_scalar(rp, rsp, m1("ralogx", 1), -1.0, ALU.mult, ALU.mult))
                        own.link(dve.tensor_tensor_scan(rcs, c_("rreset"), rp, 0.0, ALU.mult, ALU.add))
                        for i, name in enumerate(("FR", "DL", "DR")):
                            ins = dve.tensor_scalar(m1(name, SEQ), rcs, sel[:, 1 + 2 * i:2 + 2 * i], sel[:, 2 + 2 * i:3 + 2 * i], ALU.mult, ALU.add)
                        ins.then_inc(ev("rows_cs"), 1)
                    if m == FQ:
                        wait_full(dve, L, "gla_z")
                        z = psum(L, "gla_z")
                        own.step(dve.tensor_scalar(zb[:, 0:SEQ], z[:, 0:SEQ], p1("gbg")[:, 0:1], None, ALU.add))
                        drained(L, "gla_z", dve.tensor_scalar(zb[:, SEQ:512], z[:, SEQ:512], p1("gbg")[:, 1:2], None, ALU.add))
                        wait_drained(dve, L, "gla_z")
                        dve.scalar_tensor_tensor(ge, zb, -1.0, zb, ALU.mult, ALU.min).then_inc(ev("z_na"), 1)
                    if m == FK:
                        dve.wait_ge(ev("z_l"), L.one)
                        own.link(dve.scalar_tensor_tensor(zb, zb, 0.0, ge, ALU.min, ALU.subtract))
                        own.link(dve.tensor_tensor_scan(gb, c_("greset"), zb, 0.0, ALU.mult, ALU.add))
                        b3 = gb.rearrange("p (c n) -> p c n", n=HD)
                        dve.tensor_tensor(gd.rearrange("p (c n) -> p c n", n=HD), bc(b3[:, :, HD - 1:HD], [P, 8, HD]), b3,
                                          ALU.subtract).then_inc(ev("gla_b"), 1)
                    if m == GV:
                        dve.wait_ge(ev("gla_exp"), L.one)
                        wait_drained(dve, L, ("ip", GQ))
                        wait_drained(dve, L, ("ip", GK))
                        dve.scalar_tensor_tensor(gq, gq, SCALE, m1("eb", 512), ALU.mult, ALU.mult)
                        dve.tensor_tensor(m1("kend", 512), gk, gd, ALU.mult)
                        dve.tensor_tensor(gk, gk, m1("enb", 512), ALU.mult).then_inc(ev("gla_dec"), 1)
                    if m == DC:
                        wait_drained(dve, L, ("ip", FQ))
                        wait_drained(dve, L, ("ip", FK))
                        fqk, fsq = m1("fqk", 1024), m1("fsq", 1024)
                        own.link(dve.tensor_tensor(fsq, fqk, fqk, ALU.mult))
                        own.link(dve.tensor_reduce(stat[:, 160:176], fsq.rearrange("p (g n) -> p g n", n=HD), AX, ALU.add))
                        rstd = inverse_root(own, stat[:, 160:176], 16, HD)
                    if m == DV:
                        own.link(dve.tensor_scalar(rstd[:, 0:8], rstd[:, 0:8], SCALE, None, ALU.mult))
                        f3 = fqk.rearrange("p (g n) -> p g n", n=HD)
                        own.link(dve.tensor_tensor(f3, f3, bc(rstd.unsqueeze(2), [P, 16, HD]), ALU.mult))
                        for c, name in enumerate(("fqg", "fkg")):
                            part = f3[:, 8 * c:8 * c + 8, :]
                            ins = dve.tensor_tensor(part, part, bc(p1(name).unsqueeze(1), [P, 8, HD]), ALU.mult)
                        ins.then_inc(ev("fqk_ready"), 1)
                    if m == DB:
                        wait_drained(dve, L, ("ip", DV))
                        wait_drained(dve, L, ("ip", DB))
                        dy, db = m1("dy", 512), m1("db", 512)
                        own.link(convolve(own, [dy[:, 0:SEQ], dy[:, SEQ:512]], [dcu[:, 0, :], dcu[:, 1, :]], p1("scw"), 3))
                        dve.tensor_tensor(dy, dy, db, ALU.mult).then_inc(ev("dy_ready"), 1)

                tmr = m1("tmr", 16)
                wait_full(dve, L, "rowsT")
                drained(L, "rowsT", dve.tensor_copy(tmr.rearrange("p (q h) -> p q h", q=4),
                                                    psum(L, "rowsT")[:].rearrange("p (q h e) -> p q h e", q=4, h=H)[:, :, :, 2]))
                wait_full(dve, L, "ssd_xs")
                wait_drained(dve, L, "rowsT")
                x3 = psum(L, "ssd_xs")[:].rearrange("p (g n) -> p g n", n=HD)
                xd, xsD, xdd = m1("xd", 512), m1("xsD", 512), m1("xdd", 256)
                own.step(dve.tensor_tensor(xd.rearrange("p (g n) -> p g n", n=HD), x3, bc(tmr[:, 0:8].unsqueeze(2), [P, 8, HD]), ALU.mult))
                for T in range(NT):
                    ins = dve.tensor_tensor(xsD.rearrange("p (g n) -> p g n", n=HD)[:, 4 * T:4 * T + 4, :], x3[:, 4 * T:4 * T + 4, :],
                                            bc(p1("skip").unsqueeze(2), [P, H, HD]), ALU.mult)
                drained(L, "ssd_xs", ins)
                own.wait()
                dve.tensor_tensor(xdd.rearrange("p (g n) -> p g n", n=HD), xd[:, 0:256].rearrange("p (g n) -> p g n", n=HD),
                                  bc(tmr[:, 8:12].unsqueeze(2), [P, H, HD]), ALU.mult).then_inc(ev("xd_ready"), 1)
                wait_full(dve, L, "ssd_sc")
                sc = psum(L, "ssd_sc")[:].rearrange("p (g n) -> p g n", n=P)
                Mt, Lm = (m1(n, 1024).rearrange("p (g e n) -> p g e n", g=4, e=2) for n in ("Mt", "Lm"))
                for h in range(H):
                    wait_drained(dve, L, f"ssd_seg{h}")
                for g in range(4):
                    ins = dve.tensor_tensor(Mt[:, g], sc[:, g, :].unsqueeze(1).to_broadcast([P, 2, P]), Lm[:, g], ALU.mult)
                drained(L, "ssd_sc", ins)
                for hh in range(2):
                    wait_full(dve, L, f"gla_att{hh}")
                    drained(L, f"gla_att{hh}", dve.tensor_tensor(
                        m1("attT", 1024)[:, hh * 512:(hh + 1) * 512].rearrange("p (g n) -> p g n", g=4),
                        psum(L, f"gla_att{hh}")[:].rearrange("p (g n) -> p g n", g=4), bc(c_("glam").unsqueeze(1), [P, 4, P]), ALU.mult))
                wait_full(dve, L, "gla_kv")
                kv = psum(L, "gla_kv")[:, 0:384].rearrange("p (c t n) -> p c t n", c=3, t=2)
                Sg = m1("Sg", 384).rearrange("p (c t n) -> p c t n", c=3, t=2)
                eb = m1("eb", 512).rearrange("p (t c n) -> p t c n", t=2, c=4)
                own.link(dve.tensor_copy(Sg[:, 0], kv[:, 0]))
                for t in range(2):
                    own.step(dve.scalar_tensor_tensor(Sg[:, 1, t, :], Sg[:, 0, t, :], eb[:, t, 1, HD - 1:HD], kv[:, 1, t, :], ALU.mult, ALU.add))
                own.wait()
                for t in range(2):
                    ins = dve.scalar_tensor_tensor(Sg[:, 2, t, :], Sg[:, 1, t, :], eb[:, t, 2, HD - 1:HD], kv[:, 2, t, :], ALU.mult, ALU.add)
                drained(L, "gla_kv", ins)
                wait_drained(dve, L, "gla_kv")
                dve.tensor_tensor(m1("Sbd", 768).rearrange("p (g e n) -> p g e n", g=6, e=2),
                                  bc(m1("Sg", 384).rearrange("p (g n) -> p g n", g=6).unsqueeze(2), [P, 6, 2, HD]),
                                  bc(c_("half").unsqueeze(1).unsqueeze(3), [P, 6, 2, HD]), ALU.mult).then_inc(ev("gla_states"), 1)
                wait_full(dve, L, "ssd_y")
                drained(L, "ssd_y", dve.tensor_tensor(xsD, psum(L, "ssd_y")[:], xsD, ALU.add))
                for h in range(H):
                    ins = dve.tensor_scalar(m1("FL", 4 * SEQ)[:, h * SEQ:(h + 1) * SEQ], rcs, sel[:, 7 + 2 * h:8 + 2 * h],
                                            sel[:, 8 + 2 * h:9 + 2 * h], ALU.mult, ALU.add)
                ins.then_inc(ev("FL_ready"), 1)
                wait_full(dve, L, "ssd_yoff")
                drained(L, "ssd_yoff", dve.tensor_tensor(xdd.rearrange("p (g n) -> p g n", n=HD), psum(L, "ssd_yoff")[:, 0:256].rearrange("p (g n) -> p g n", n=HD),
                                                         bc(tmr[:, 12:16].unsqueeze(2), [P, H, HD]), ALU.mult))
                wait_drained(dve, L, "ssd_y")
                wait_drained(dve, L, "ssd_yoff")
                own.link(dve.tensor_tensor(xsD[:, 256:512], xsD[:, 256:512], xdd, ALU.add))
                own.step(dve.tensor_tensor(xs[:, :, 2 * GW:3 * GW], xsD.rearrange("p (t n) -> p t n", t=NT),
                                           m1("siluz", 512).rearrange("p (t n) -> p t n", t=NT), ALU.mult))
                y4 = xs[:].rearrange("p t (g n) -> p t g n", n=HD)
                groups = ((slice(0, 4), slice(0, 4), m1("kendT", 512)), (slice(8, 16), slice(4, 12), m1("zb", 1024)))
                ss = stat[:, 160:184].rearrange("p (t g) -> p t g", t=NT)

                def squares():
                    for name in ("gla_o", "sc_t"):
                        wait_drained(dve, L, name)
                    own.wait()
                    for at, to, square in groups:
                        sq = square.rearrange("p (t g n) -> p t g n", t=NT, n=HD)
                        own.step(dve.tensor_tensor(sq, y4[:, :, at], y4[:, :, at], ALU.mult))

                def sums():
                    own.wait()
                    for at, to, square in groups:
                        sq = square.rearrange("p (t g n) -> p t g n", t=NT, n=HD)
                        own.step(dve.tensor_reduce(ss[:, :, to], sq, AX, ALU.add))
                    own.wait()
                    s3 = ss[:, :, 4:8].rearrange("p t (a b) -> p t a b", b=2)
                    pair = stat[:, 196:200].rearrange("p (t a) -> p t a", t=NT)
                    own.link(dve.tensor_tensor(pair, s3[:, :, :, 0], s3[:, :, :, 1], ALU.add))
                    own.step(dve.tensor_scalar(s3, bc(pair.unsqueeze(3), [P, NT, 2, 2]), 0.5, None, ALU.mult))

                def other_roots():
                    own.wait()
                    inverse_root(own, stat[:, 160:184], 24, HD)

                def normalised():
                    rstd = stat[:, 32:56].rearrange("p (t g) -> p t g", t=NT)
                    for at, to, _ in groups:
                        n = at.stop - at.start
                        own.step(dve.tensor_tensor(y4[:, :, at], y4[:, :, at], bc(rstd[:, :, to].unsqueeze(3), [P, NT, n, HD]), ALU.mult))

                def gains():
                    own.wait()
                    for at, to, _ in groups:
                        cols = slice(at.start * HD, at.stop * HD)
                        own.step(dve.tensor_tensor(xs[:, :, cols], xs[:, :, cols], bc(p1("ygain")[:, cols].unsqueeze(1), [P, NT, cols.stop - cols.start]), ALU.mult))
                    own.wait()
                    dve.tensor_tensor(xs[:, :, 0:GW], xs[:, :, 0:GW], m1("silug", 512).rearrange("p (t n) -> p t n", t=NT),
                                      ALU.mult).then_inc(ev("others_ready"), 1)

                pieces = ((squares,), (sums, other_roots), (normalised,), (gains,))
                for u in range(H):
                    maxima(L, own, u, 1.0, m1("mx", 4), m1("nm", 4))
                    if u == 2:
                        keep_turned(L, 1, m1("pt", 768))
                    for piece in pieces[u]:
                        piece()
                    if u == 1:
                        keep_turned(L, 0, m1("pt", 768))
                y_remainders(L, 0, KD // 2 - 1)
                wait_full(dve, L, ("o", 0))
                rec = m1("frec", 8)
                own.link(dve.reciprocal(rec, m1("rowsum", 8)))
                o4 = psum(L, ("o", 0))[:].rearrange("p (t h n) -> p t h n", t=NT, h=H)
                fox = y4[:, :, 4:8, :]
                drained(L, ("o", 0), dve.tensor_tensor(fox, o4, bc(rec.rearrange("p (t h) -> p t h", t=NT).unsqueeze(3), [P, NT, H, HD]), ALU.mult))
                wait_drained(dve, L, ("o", 0))
                sq = m1("kendT", 512).rearrange("p (t g n) -> p t g n", t=NT, n=HD)
                own.link(dve.tensor_tensor(sq, fox, fox, ALU.mult))
                own.link(dve.tensor_reduce(stat[:, 184:192], m1("kendT", 512).rearrange("p (g n) -> p g n", n=HD), AX, ALU.add))
                rstd = inverse_root(own, stat[:, 184:192], 8, HD)
                own.link(dve.tensor_tensor(fox, fox, bc(rstd.rearrange("p (t h) -> p t h", t=NT).unsqueeze(3), [P, NT, H, HD]), ALU.mult))
                dve.tensor_tensor(xs[:, :, GW:2 * GW], xs[:, :, GW:2 * GW], bc(p1("ygain")[:, GW:2 * GW].unsqueeze(1), [P, NT, GW]),
                                  ALU.mult).then_inc(ev("y_ready"), 1)
                y_remainders(L, KD // 2 - 1, KD // 2)
                finish(L)

            def second_mixer(L, own):
                rotated = {KSW: m2("kr", 512), Q0: m2("qr", 1024)[:, 0:512], Q1: m2("qr", 1024)[:, 512:1024],
                           MQ0: m2("mqr", 1024)[:, 0:512], MQ1: m2("mqr", 1024)[:, 512:1024],
                           MK0: m2("mkr", 1024)[:, 0:512], MK1: m2("mkr", 1024)[:, 512:1024]}
                two = lambda ap: ap.rearrange("p (t n) -> p t n", t=2)
                dve.wait_ge(s_par, 16 * L.deep + 16)
                set_masks()
                dve.memset(m2("hvr", 256), 0.0)
                dve.memset(m2("hu", 128), 0.0)
                dve.memset(m2("hidT", 512), 0.0)
                own.link(dve.memset(m2("kc", 32), 0.0))

                def rotate(m):
                    own.wait()
                    wait_full(dve, L, ("rot", m))
                    own.step(dve.tensor_tensor(two(m2("rc", 512)), two(raw_of(m)), bc(c_("ropeC").unsqueeze(1), [P, 2, SEQ]), ALU.mult))
                    drained(L, ("rot", m), dve.tensor_tensor(two(rotated[m]), two(psum(L, ("rot", m))[:]), bc(c_("ropeS").unsqueeze(1), [P, 2, SEQ]), ALU.mult))
                    own.wait()
                    wait_drained(dve, L, ("rot", m))
                    ins = dve.tensor_tensor(rotated[m], rotated[m], m2("rc", 512), ALU.add)
                    if m == Q1:
                        ins.then_inc(ev("first_roped"), 1)
                        dve.wait_ge(ev("first_roped"), L.one)
                    elif m == MK1:
                        ins.then_inc(ev("roped"), 1)
                    else:
                        own.step(ins)

                gate = m2("gate", 64)
                g4 = gate.rearrange("p (t n) -> p t n", t=NT)
                hid, hx2, hu, he, hv = (m2(n, 128) for n in ("hid", "hx2", "hu", "he", "hv"))
                part = lambda ap: ap.rearrange("p (t n) -> p t n", n=32)[:, :, 0:2 * NCMP]
                cs, cmx, csum, cfac = m2("cs", 256), m2("cmx", 16), m2("csum", 16), m2("cfac", 16)
                y4 = xs[:].rearrange("p t (g n) -> p t g n", n=HD)
                for m in range(IP2 + 1):
                    if m in (Q1, GATES):
                        c = m - Q1
                        dve.wait_ge(ev(f"blk_hi{c}"), L.one)
                        dve.tensor_tensor(hlo[:, c * 480:(c + 1) * 480], m2("blk", 960)[:, c * 480:(c + 1) * 480],
                                          hhi[:, c * 480:(c + 1) * 480].bitcast(F32), ALU.subtract).then_inc(ev(f"blk_ready{c}"), 1)
                        split_shared(L, CMP0 + 2 * c)
                    if m - 1 in ROPED:
                        rotate(m - 1)
                    if m == KSW:
                        wait_drained(dve, L, ("ip", KVC))
                        for c, pos in enumerate(("posk", "posv")):
                            for g in range(2):
                                src = m2("kx", 1024)[:, (2 * c + g) * SEQ:(2 * c + g + 1) * SEQ]
                                src = bass.AP(src.tensor, src.offset, [src.ap[0], (2, NCT), (NCT, NCMP)])
                                dst = m2("blk", 960)[:, c * 480:(c + 1) * 480].rearrange("p (k g n) -> p k g n", k=NCT, g=2)[:, :, g, :]
                                ins = dve.tensor_tensor(dst, src, bc(p2(pos).unsqueeze(2), [P, NCT, NCMP]), ALU.add)
                            ins.then_inc(ev(f"blk{c}"), 1)
                    if m == GATES:
                        split_shared(L, CMP0 + 4)
                        for c in range(2):
                            if c:
                                split_shared(L, CMP0 + 6)
                                split_shared(L, CMP0 + 8)
                            wait_full(dve, L, ("hid", c))
                            drained(L, ("hid", c), dve.tensor_copy(m2("hidT", 512)[0:2 * NCMP, c * 256:(c + 1) * 256], psum(L, ("hid", c))[0:2 * NCMP, 0:256]))
                    if m == VSW:
                        wait_full(dve, L, "hidf")
                        dve.tensor_scalar(gate, psum(L, "hidf")[:, 128:192], 1.0, None, ALU.add)
                        drained(L, "hidf", dve.tensor_copy(part(hid), part(psum(L, "hidf")[:, 0:128])))
                        wait_drained(dve, L, "hidf")
                        own.link(dve.tensor_tensor(part(hx2), part(hid), part(hid), ALU.mult))
                        own.link(dve.tensor_scalar(part(hx2), part(hx2), 0.044715, 1.0, ALU.mult, ALU.add))
                        own.link(dve.tensor_tensor(part(hu), part(hx2), part(hid), ALU.mult))
                        dve.tensor_scalar(part(hu), part(hu), -50.0, None, ALU.max).then_inc(ev("gelu_in"), 1)
                        own.link(dve.reciprocal(gate, gate))
                        dve.wait_ge(ev("gelu_e"), L.one)
                        own.link(dve.tensor_scalar(part(hv), part(he), 1.0, None, ALU.add))
                        own.link(dve.reciprocal(part(hv), part(hv)))
                        dve.tensor_tensor(part(m2("hk", 64)), part(hv)[:, 0:2], part(hid)[:, 0:2], ALU.mult).then_inc(ev("gelu0"), 1)
                        for t in range(2):
                            a, b = (ap[:, (2 + t) * 32:(2 + t) * 32 + 2 * NCMP].rearrange("p (g n) -> p g n", g=2).unsqueeze(1).to_broadcast([P, 4, 2, NCMP])
                                    for ap in (hv, hid))
                            dst = m2("hvr", 256)[:, t * P:(t + 1) * P].rearrange("p (r g n) -> p r g n", r=4, g=2)[:, :, :, 0:NCMP]
                            ins = dve.tensor_tensor(dst, a, b, ALU.mult)
                        ins.then_inc(ev("gelu1"), 1)
                    if m == MQ0:
                        wait_full(dve, L, "kc")
                        drained(L, "kc", dve.tensor_tensor(m2("kc", 32).rearrange("p (g n) -> p g n", g=2)[:, :, 0:NCMP],
                                                           psum(L, "kc")[:, 0:2 * NCMP].rearrange("p (g n) -> p g n", g=2),
                                                           bc(c_("half").unsqueeze(2), [P, 2, NCMP]), ALU.mult))
                        wait_full(dve, L, "vc")
                        drained(L, "vc", dve.tensor_tensor(m2("vcd", 512).rearrange("p (g n) -> p g n", g=8), bc(psum(L, "vc")[:, 0:HD].unsqueeze(1), [P, 8, HD]),
                                                           bc(c_("own").unsqueeze(2), [P, 8, HD]), ALU.mult))
                    if m == MQ1:
                        wait_full(dve, L, "cmp_s")
                        s3 = psum(L, "cmp_s")[:, 0:256].rearrange("p (g n) -> p g n", n=16)
                        own.link(dve.tensor_reduce(cmx, s3, AX, ALU.max))
                        own.link(dve.tensor_scalar(cmx, cmx, NEG / 10, None, ALU.max))
                        drained(L, "cmp_s", dve.tensor_tensor(cs.rearrange("p (g n) -> p g n", n=16), s3, bc(cmx.unsqueeze(2), [P, 16, 16]), ALU.subtract))
                    if m == MK0:
                        dve.wait_ge(ev("cmp_exp"), L.one)
                        own.link(dve.tensor_reduce(csum, cs.rearrange("p (g n) -> p g n", n=16), AX, ALU.add))
                        own.link(dve.tensor_scalar(csum, csum, 1.0, None, ALU.max))
                        own.link(dve.reciprocal(csum, csum))
                        for T in range(NT):
                            heads = lambda ap: ap.rearrange("p (g r) -> p g r", g=2)
                            own.step(dve.tensor_tensor(heads(cfac[:, 8 * T:8 * T + 8]), csum[:, 8 * T:8 * T + 8].rearrange("p (r g) -> p g r", g=2),
                                                       heads(g4[:, T, 0:8]), ALU.mult))
                        own.wait()
                    if m == MK1:
                        for T in range(NT):
                            wait_full(dve, L, f"cmp_o{T}")
                            drained(L, f"cmp_o{T}", dve.tensor_tensor(
                                y4[:, T, 0:8, :], psum(L, f"cmp_o{T}")[:].rearrange("p (g n) -> p g n", g=8),
                                bc(cfac[:, 8 * T:8 * T + 8].unsqueeze(2), [P, 8, HD]), ALU.mult))
                rowsum = m2("rowsum", 2 * UNITS).rearrange("p (t u) -> p t u", t=NT)
                fac = m2("fac", 8).rearrange("p (t u) -> p t u", t=NT)
                otmp = m2("otmp", 512)

                def outputs(q, T):
                    kind, h0 = q // 2, 4 * (q % 2)
                    if T == 0:
                        wait_full(dve, L, ("o", q))
                        own.link(dve.reciprocal(fac, rowsum[:, :, 4 * q:4 * q + 4]))
                        if kind < 2:
                            own.link(dve.tensor_tensor(fac, fac, g4[:, :, 8 + 8 * kind + h0:12 + 8 * kind + h0], ALU.mult))
                    o4 = psum(L, ("o", q))[:].rearrange("p (t h n) -> p t h n", t=NT, h=4)
                    t4 = otmp.rearrange("p (t h n) -> p t h n", t=NT, h=4)
                    dst = t4[:, T] if kind < 2 else y4[:, T, 8 + h0:12 + h0, :]
                    ins = dve.tensor_tensor(dst, o4[:, T], bc(fac[:, T, :].unsqueeze(2), [P, 4, HD]), ALU.mult)
                    if T == NT - 1:
                        drained(L, ("o", q), ins)

                for u in range(UNITS + 2):
                    if u < UNITS:
                        maxima(L, own, u, SCALE, m2("mx", 4), m2("nm", 4))
                    if 1 <= u <= UNITS:
                        keep_turned(L, u - 1, m2("pt", 768))
                    if u >= 6:
                        q, step = (u - 6) // 4, (u - 6) % 4
                        if step < NT:
                            outputs(q, step)
                        elif step == NT and q < UNITS // 6:
                            wait_drained(dve, L, ("o", q))
                            yp = xs[:, :, 4 * (q % 2) * HD:4 * (q % 2 + 1) * HD]
                            own.link(dve.tensor_tensor(yp, yp, otmp.rearrange("p (t n) -> p t n", t=NT), ALU.add))
                y_remainders(L, 0, 1)
                for T in range(NT):
                    outputs(UNITS // 4 - 1, T)
                y_remainders(L, 1, KD // 2)
                finish(L)

            dve.memset(ones[:], 1.0).then_inc(ones_set, 1)
            for b in range(8):
                dve.sem_inc(bank_read[b], 1)
            dve.wait_ge(s_con, 16)
            dve.wait_ge(s_x, 16)
            for blk, mixer in enumerate((first_mixer, second_mixer)):
                with dve.Fori(0, DEPTH) as l:
                    L = Layer(l, blk)
                    own = Own(dve, dve_own, L)
                    norm(L, own, 0)
                    ffn(L, 0)
                    norm(L, own, 1)
                    mixer(L, own)
                    norm(L, own, 2)
                    ffn(L, 1)
                    own.close()
            last = Layer(DEPTH, 1)
            rstd = roots(last, Own(dve, dve_own, last), 0)
            dve.wait_ge(s_par, 16 * 2 * DEPTH + 16)
            for T in range(NT):
                for half in range(2):
                    cols = slice(half * 512, half * 512 + 512)
                    dve.scalar_tensor_tensor(xs[:, T, cols], x[:, T, cols], rstd[:, T:T + 1], par[:, cols], ALU.mult, ALU.mult).then_inc(xs_ready, 1)


def constants():
    con = np.zeros((P, CON_W), np.float32)

    def put(name, value):
        con[:, CON[name][0]:CON[name][1]] = value

    p, c = np.arange(P)[:, None], np.arange(P)[None, :]
    put("ident", p == c)
    put("negq", np.where(c <= p, 0, NEG))
    put("negT", np.where(c >= p, 0, NEG))
    put("glam", (c >= p) & (c // HD == p // HD))
    tok = np.arange(SEQ)[None, :]
    put("rreset", np.where((p % 32 >= 2) & (p % 32 < 4) & (tok == P), 0, 1))
    put("greset", np.arange(2 * SEQ)[None, :] % HD != 0)
    sel = np.zeros((P, 15), np.float32)
    e = [np.arange(P) % 32 == i for i in range(4)]
    sel[:, 0] = np.where(e[0] | e[1], -1, 1)
    for at, picks in ((1, ((0, 0, 1), (1, -1, 0))), (3, ((2, 0, 1), (3, -1, 0))), (5, ((2, 1, 0), (3, 0, 1)))):
        for row, factor, shift in picks:
            sel[e[row], at], sel[e[row], at + 1] = factor, shift
    for h in range(H):
        sel[32 * h, 7 + 2 * h], sel[32 * h + 1, 8 + 2 * h] = 1, 1
    put("sel", sel)
    put("half", p // HD == np.arange(2)[None, :])
    put("own", (p // 16 % 2) * 4 + p // 32 == np.arange(8)[None, :])
    n, T = np.arange(16)[None, None, None, :], np.arange(NT)[None, :, None, None]
    seen = np.broadcast_to((n < NCMP) & (16 * n + 31 <= T * P + p[:, :, None, None]), (P, NT, 8, 16))
    put("cmpmask", np.where(seen, 0, NEG).reshape(P, 256))
    inv_freq = np.power(np.float32(500000.0), -(np.arange(0, 16, 2, dtype=np.float32) / np.float32(16)))
    angle = np.arange(SEQ, dtype=np.float32)[:, None] * inv_freq[None, :]
    cos, sin, turn = np.ones((P, SEQ), np.float32), np.zeros((P, SEQ), np.float32), np.zeros((P, P), np.float32)
    for q in range(P):
        d = q % HD
        if d < 16:
            cos[q], sin[q] = np.cos(angle[:, d % 8]), np.sin(angle[:, d % 8])
            turn[q + 8 if d < 8 else q - 8, q] = -1 if d < 8 else 1
    put("ropeC", cos)
    put("ropeS", sin)
    put("ropeR", turn)
    return con


def rows_tiles(w):
    return w.reshape(-1, P, w.shape[1]).transpose(1, 0, 2)


def fm_slot(w):
    return rows_tiles(w).reshape(P, -1)


def tm_slots(w):
    return [rows_tiles(w[half * 512:(half + 1) * 512]).reshape(P, -1) for half in range(2)]


def ffn_slots(gate, up, down):
    out = []
    for i in range(STEPS + 1):
        if i < STEPS:
            out += [fm_slot(gate[:, i * P:(i + 1) * P]), fm_slot(up[:, i * P:(i + 1) * P])]
        if i:
            out.append(down[(i - 1) * P:i * P])
    return out


def scattered(columns):
    out = np.zeros((D, P), np.float32)
    for at, col in columns:
        out[:, at:at + col.shape[1]] = col
    return out


def first_mixer_slots(w_in, w_out):
    names = ["a_q", "a_k", "a_v", "a_g", "a_lr", "b_q", "b_k", "b_v", "b_f", "c_z", "c_xbc", "c_dt", "d_b", "d_c", "d_v"]
    widths = [GW] * 4 + [16] + [GW] * 3 + [H] + [GW, 3 * GW, H] + [GW] * 3
    part = dict(zip(names, np.split(w_in, np.cumsum(widths)[:-1], axis=1)))
    fm = lambda w: [fm_slot(w[:, 0:P]), fm_slot(w[:, P:2 * P])]
    out = []
    for t in range(3):
        out += fm(part["c_xbc"][:, t * GW:(t + 1) * GW])
    out += tm_slots(part["c_z"]) + tm_slots(part["a_g"])
    rows = []
    for h in range(H):
        f, dt = part["b_f"][:, h:h + 1], part["c_dt"][:, h:h + 1]
        rows += [(32 * h, f), (32 * h + 1, f), (32 * h + 2, dt), (32 * h + 3, dt)]
    out += [fm_slot(scattered([(0, part["a_lr"])])), fm_slot(scattered(rows))]
    out += fm(part["a_q"]) + fm(part["a_k"])
    for name in ("b_q", "b_k", "a_v"):
        out += tm_slots(part[name])
    for name in ("d_c", "d_v", "d_b"):
        out += fm(part[name])
    out += tm_slots(part["b_v"])
    return out + [w_out[k * P:(k + 1) * P] for j in ORDER1 for k in (2 * j, 2 * j + 1)]


def second_mixer_slots(w_in, w_ck1, w_cv1, w_out):
    q, kv, gates, moba = np.split(w_in, [512, 1280, 1304], axis=1)
    q = q.reshape(D, 2, 4, HD)
    k_cmp, v_cmp, k_slc, v_slc, k_win, v_win = (kv[:, i * P:(i + 1) * P] for i in range(6))
    fm = lambda w: fm_slot(np.ascontiguousarray(w))
    out = [fm(k_cmp), fm(v_cmp), fm(k_slc), fm(k_win)]
    out += [fm(q[:, :, r].reshape(D, P)) for r in range(4)]
    by_branch = gates.reshape(D, 8, 3).transpose(0, 2, 1).reshape(D, 24)
    out.append(fm_slot(scattered([(0, by_branch)])))
    for w in (w_ck1, w_cv1):
        out += [rows_tiles(w[s * 512:(s + 1) * 512]).reshape(P, -1) for s in range(CMP_SLOTS)]
    out += tm_slots(np.concatenate([v_slc, v_win], axis=1))
    out += [fm(moba[:, t * P:(t + 1) * P]) for t in range(8)]
    out += tm_slots(moba[:, 1024:1280]) + tm_slots(moba[:, 1280:1536])
    return out + [w_out[k * P:(k + 1) * P] for k in range(KD)]


def stream(a):
    out = []
    for l in range(DEPTH):
        out += ffn_slots(a["ffn1_w_gate"][l], a["ffn1_w_up"][l], a["ffn1_w_down"][l])
        out += first_mixer_slots(a["w_in"][l], a["w_out"][l])
        out += ffn_slots(a["ffn2_w_gate"][l], a["ffn2_w_up"][l], a["ffn2_w_down"][l])
    for l in range(DEPTH):
        out += ffn_slots(a["w_ffn1_gate_2"][l], a["w_ffn1_up_2"][l], a["w_ffn1_down_2"][l])
        out += second_mixer_slots(a["w_in_2"][l], a["w_ck1_2"][l], a["w_cv1_2"][l], a["w_out_2"][l])
        out += ffn_slots(a["w_ffn2_gate_2"][l], a["w_ffn2_up_2"][l], a["w_ffn2_down_2"][l])
    out += [np.zeros((P, SLOT), np.float32)] * TAIL
    assert len(out) == N_SLOTS
    return np.stack(out)


def replicated(row):
    return np.broadcast_to(row, (P,) + row.shape)


def first_parameters(a, l):
    par = np.zeros((P, PAR1_W), np.float32)

    def put(name, value):
        par[:, PAR1[name][0]:PAR1[name][1]] = value

    put("convw", a["ssm_conv_w"][l].reshape(4, 6, P).transpose(2, 1, 0).reshape(P, 24))
    put("convb", a["ssm_conv_b"][l].reshape(6, P).T)
    put("scw", a["sc_conv_w"][l].reshape(3, 2, P).transpose(2, 1, 0).reshape(P, 6))
    put("skip", replicated(a["ssm_D"][l]))
    bias, a_log = np.zeros((P, 1), np.float32), np.zeros((P, 1), np.float32)
    for h in range(H):
        bias[32 * h:32 * h + 2, 0] = a["fox_b_forget"][l, h]
        bias[32 * h + 2:32 * h + 4, 0] = a["ssm_dt_bias"][l, h]
        a_log[32 * h + 2:32 * h + 4, 0] = a["ssm_A_log"][l, h]
    put("rbias", bias)
    put("ralog", a_log)
    put("gbg", a["gla_b_gate"][l].reshape(2, P).T)
    put("fqg", replicated(a["fox_q_norm"][l]))
    put("fkg", replicated(a["fox_k_norm"][l]))
    par[0:16, PAR1["gup"][0]:PAR1["gup"][1]] = a["gla_w_gate_up"][l]
    put("ygain", replicated(np.concatenate([a[n][l] for n in ("gla_norm", "fox_out_norm", "ssm_norm", "sc_out_norm")])))
    return par


def second_parameters(a, l):
    par = np.zeros((P, PAR2_W), np.float32)
    for name, source in (("posk", "pos_ck_2"), ("posv", "pos_cv_2")):
        par[:, PAR2[name][0]:PAR2[name][1]] = a[source][l].reshape(NCT, 2, HD).transpose(1, 2, 0).reshape(P, NCT)
    ck2, cv2 = rows_tiles(a["w_ck2_2"][l]), rows_tiles(a["w_cv2_2"][l])
    par[:, PAR2["ck2"][0]:PAR2["ck2"][1]] = np.concatenate([ck2, ck2], axis=2).reshape(P, 4 * HD)
    par[:, PAR2["cv2"][0]:PAR2["cv2"][1]] = cv2.reshape(P, 2 * HD)
    return par


def kernel(**inputs):
    import concourse.bacc as bacc
    from concourse.bass_utils import run_bass_kernel_spmd

    a = {name: np.asarray(value) for name, value in inputs.items()}
    gains = [a[n][l] for l in range(DEPTH) for n in ("ffn1_norm", "mix_norm", "ffn2_norm")]
    gains += [a[n][l] for l in range(DEPTH) for n in ("norm_ffn1_2", "norm_mix_2", "norm_ffn2_2")]
    arrays = {
        "x": np.ascontiguousarray(a["x"][0].reshape(NT, P, D).transpose(1, 0, 2)),
        "w": stream(a),
        "gain": np.concatenate([np.stack(gains).reshape(2 * DEPTH, 3 * KD, P).transpose(0, 2, 1),
                                np.zeros((1, P, 3 * KD), np.float32)]),
        "last_gain": np.ascontiguousarray(replicated(a["norm_final_2"])),
        "par1": np.stack([first_parameters(a, l) for l in range(DEPTH)]),
        "par2": np.stack([second_parameters(a, l) for l in range(DEPTH)]),
        "con": constants(),
    }
    nc = bacc.Bacc("TRN2", target_bir_lowering=False, num_devices=1)
    args = [nc.dram_tensor(f"in_{name}_dram", array.shape, F32, kind="ExternalInput").ap() for name, array in arrays.items()]
    out_d = nc.dram_tensor("out_0_dram", (P, NT, D), F32, kind="ExternalOutput").ap()
    build(nc, *args, out_d)
    result = run_bass_kernel_spmd(nc, [{f"in_{n}_dram": v for n, v in arrays.items()}], core_ids=[0])
    return np.asarray(result.results[0]["out_0_dram"]).transpose(1, 0, 2).reshape(1, SEQ, D)
```
